# Optimizing a Trainium2 kernel written in Bass

```python
import math
import jax, jax.numpy as jnp
from jax import lax
import numpy as np

D_MODEL = 1024
BATCH = 1
SEQ = 512
DEPTH = 1

F32 = jnp.float32
EPS = 1e-6
NEG_INF = -1e30

N_BRANCH = 4
BRANCH_W = D_MODEL // 2
HEAD_DIM = 64
Q_BLOCK = 128
DA_HEADS = BRANCH_W // (2 * HEAD_DIM)
CONV_W = 3
POOL_WINDOWS = (2, 4, 8, 16)
N_POOL = len(POOL_WINDOWS)
POOL_GROUP = BRANCH_W // N_POOL
SW_WINDOW = 128
SW_Q_HEADS = BRANCH_W // HEAD_DIM
SW_KV_HEADS = 2
SW_REP = SW_Q_HEADS // SW_KV_HEADS
PEER_HEADS = 8
PEER_NKEYS = 128
PEER_EXPERTS = PEER_NKEYS * PEER_NKEYS
PEER_DKEY = 256
PEER_TOPK = 16
PEER_CHUNK = 128

COL_SIZES = (
    DA_HEADS * 2 * HEAD_DIM, DA_HEADS * 2 * HEAD_DIM, DA_HEADS * 2 * HEAD_DIM,
    BRANCH_W, BRANCH_W, BRANCH_W,
    BRANCH_W,
    SW_Q_HEADS * HEAD_DIM, SW_KV_HEADS * HEAD_DIM, SW_KV_HEADS * HEAD_DIM,
    N_BRANCH * D_MODEL,
)
IN_COLS = sum(COL_SIZES)
SPLIT_POINTS = tuple(int(v) for v in np.cumsum(COL_SIZES)[:-1])

kernel_name = 'hybrid_gated_parallel_mixers_peer'

def rmsnorm(x, g):
    xf = x.astype(F32)
    y = xf * lax.rsqrt(jnp.mean(xf * xf, axis=-1, keepdims=True) + EPS)
    return (y * g.astype(F32)).astype(x.dtype)

def diff_attention(q, k, v, lam_q1, lam_k1, lam_q2, lam_k2, g_subln, lam_init):
    Bn, S = q.shape[0], q.shape[1]
    lam = (jnp.exp(jnp.sum(lam_q1.astype(F32) * lam_k1.astype(F32)))
           - jnp.exp(jnp.sum(lam_q2.astype(F32) * lam_k2.astype(F32))) + lam_init)
    scale = HEAD_DIM ** -0.5
    outs = []
    for i in range(S // Q_BLOCK):
        q0 = i * Q_BLOCK
        kend = q0 + Q_BLOCK
        s = jnp.einsum('bqhcd,bkhcd->bhcqk', q[:, q0:kend], k[:, :kend]).astype(F32) * scale
        causal = jnp.arange(kend)[None, :] <= (q0 + jnp.arange(Q_BLOCK))[:, None]
        p = jax.nn.softmax(jnp.where(causal, s, NEG_INF), axis=-1)
        attn = p[:, :, 0] - lam * p[:, :, 1]
        outs.append(jnp.einsum('bhqk,bkhe->bqhe', attn.astype(v.dtype), v[:, :kend]))
    o = jnp.concatenate(outs, axis=1)
    o = rmsnorm(o, g_subln) * (1.0 - lam_init)
    return o.reshape(Bn, S, DA_HEADS * 2 * HEAD_DIM)

def short_conv_mixer(gate_b, gate_c, xt, conv_w):
    S = xt.shape[1]
    z = gate_c * xt
    zp = jnp.pad(z, ((0, 0), (CONV_W - 1, 0), (0, 0)))
    y = sum(conv_w[j] * zp[:, j:j + S] for j in range(CONV_W))
    return gate_b * y

def multiscale_pool(z, w_pool, pool_scale):
    Bn, S, _ = z.shape
    zg = z.astype(F32).reshape(Bn, S, N_POOL, POOL_GROUP)
    cs = jnp.cumsum(zg, axis=1)
    pos1 = jnp.arange(1, S + 1)
    means = []
    for gi, w in enumerate(POOL_WINDOWS):
        cp = jnp.pad(cs[:, :, gi], ((0, 0), (w, 0), (0, 0)))
        win_sum = cp[:, w:] - cp[:, :S]
        count = jnp.minimum(pos1, w).astype(F32)
        means.append(win_sum / count[None, :, None])
    d = jnp.stack(means, axis=2) - zg
    y = jnp.einsum('bsgc,gce->bsge', d, w_pool.astype(F32))
    return (y.reshape(Bn, S, BRANCH_W) * pool_scale.astype(F32)).astype(z.dtype)

def sliding_window_sink_attention(q, k, v, sinks):
    Bn, S = q.shape[0], q.shape[1]
    nb = S // Q_BLOCK
    qb = q.reshape(Bn, nb, Q_BLOCK, SW_KV_HEADS, SW_REP, HEAD_DIM)

    def with_prev(t):
        t = t.reshape(Bn, nb, Q_BLOCK, SW_KV_HEADS, HEAD_DIM)
        prev = jnp.pad(t, ((0, 0), (1, 0), (0, 0), (0, 0), (0, 0)))[:, :nb]
        return jnp.concatenate([prev, t], axis=2)

    kk, vv = with_prev(k), with_prev(v)
    s = jnp.einsum('bnqgrd,bnkgd->bngrqk', qb, kk).astype(F32) * (HEAD_DIM ** -0.5)
    qi = jnp.arange(Q_BLOCK)[:, None]
    kj = jnp.arange(2 * Q_BLOCK)[None, :]
    rel = qi + Q_BLOCK - kj
    band = (rel >= 0) & (rel < SW_WINDOW)
    valid = band[None] & ((jnp.arange(nb)[:, None, None] > 0) | (kj >= Q_BLOCK)[None])
    s = jnp.where(valid[None, :, None, None], s, NEG_INF)
    sink = sinks.astype(F32).reshape(SW_KV_HEADS, SW_REP)[None, None, :, :, None, None]
    sink = jnp.broadcast_to(sink, s.shape[:-1] + (1,))
    p = jax.nn.softmax(jnp.concatenate([s, sink], axis=-1), axis=-1)[..., :-1]
    o = jnp.einsum('bngrqk,bnkgd->bnqgrd', p.astype(v.dtype), vv)
    return o.reshape(Bn, S, SW_Q_HEADS * HEAD_DIM)

def peer_ffn(h, w_q, sub_keys, u_experts, v_experts):
    Bn, S, D = h.shape
    T = Bn * S
    ht = h.reshape(T, D)
    q = (ht @ w_q).reshape(T, PEER_HEADS, 2, PEER_DKEY // 2)
    s = jnp.einsum('thpd,pnd->thpn', q, sub_keys).astype(F32)
    top_s, top_i = lax.top_k(s, PEER_TOPK)
    cand_s = (top_s[:, :, 0, :, None] + top_s[:, :, 1, None, :]).reshape(T, PEER_HEADS, -1)
    cand_i = (top_i[:, :, 0, :, None] * PEER_NKEYS + top_i[:, :, 1, None, :]).reshape(T, PEER_HEADS, -1)
    best_s, best_pos = lax.top_k(cand_s, PEER_TOPK)
    idx = jnp.take_along_axis(cand_i, best_pos, axis=-1)
    g = jax.nn.softmax(best_s, axis=-1)
    nchunk = T // PEER_CHUNK

    def expert_chunk(args):
        xc, ic, gc = args
        act = jax.nn.gelu(jnp.einsum('cd,chkd->chk', xc, u_experts[ic]).astype(F32), approximate=False)
        wgt = (gc * act).astype(xc.dtype)
        return jnp.einsum('chk,chkd->cd', wgt, v_experts[ic])

    out = lax.map(expert_chunk, (ht.reshape(nchunk, PEER_CHUNK, D),
                                 idx.reshape(nchunk, PEER_CHUNK, PEER_HEADS, PEER_TOPK),
                                 g.reshape(nchunk, PEER_CHUNK, PEER_HEADS, PEER_TOPK)))
    return out.reshape(Bn, S, D)

def hybrid_layer(x, mod, g_norm1, w_in, lam_q1, lam_k1, lam_q2, lam_k2, g_subln, conv_w,
                 w_pool, pool_scale, sinks, w_branch, w_o, g_norm2, w_q, sub_keys,
                 u_experts, v_experts, lam_init):
    Bn, S, _ = x.shape
    shift1, scale1, gate1, shift2, scale2, gate2 = [m[:, None, :] for m in jnp.split(mod, 6, axis=-1)]
    h = rmsnorm(x, g_norm1) * (1.0 + scale1) + shift1
    aq, ak, av, bb, bc, bx, cz, dq, dk, dv, gl = jnp.split(h @ w_in, SPLIT_POINTS, axis=-1)
    ya = diff_attention(aq.reshape(Bn, S, DA_HEADS, 2, HEAD_DIM),
                        ak.reshape(Bn, S, DA_HEADS, 2, HEAD_DIM),
                        av.reshape(Bn, S, DA_HEADS, 2 * HEAD_DIM),
                        lam_q1, lam_k1, lam_q2, lam_k2, g_subln, lam_init)
    yb = short_conv_mixer(bb, bc, bx, conv_w)
    yc = multiscale_pool(cz, w_pool, pool_scale)
    yd = sliding_window_sink_attention(dq.reshape(Bn, S, SW_Q_HEADS, HEAD_DIM),
                                       dk.reshape(Bn, S, SW_KV_HEADS, HEAD_DIM),
                                       dv.reshape(Bn, S, SW_KV_HEADS, HEAD_DIM), sinks)
    branches = jnp.einsum('bsgc,gcd->bsgd', jnp.stack([ya, yb, yc, yd], axis=2), w_branch)
    gates = jax.nn.sigmoid(gl.reshape(Bn, S, N_BRANCH, D_MODEL))
    mixed = jnp.sum(gates * branches, axis=2) @ w_o
    x = x + gate1 * mixed
    h2 = rmsnorm(x, g_norm2) * (1.0 + scale2) + shift2
    return x + gate2 * peer_ffn(h2, w_q, sub_keys, u_experts, v_experts)

def setup_inputs(seed: int = 0) -> dict:
    key = jax.random.key(seed)
    ks = jax.random.split(key, 24)
    L, D = DEPTH, D_MODEL

    def nrm(k, shape, scale):
        return jax.random.normal(k, shape, F32) * scale

    return {
        'x': nrm(ks[0], (BATCH, SEQ, D), 1.0),
        'c': nrm(ks[1], (BATCH, D), 1.0),
        'w_ada': nrm(ks[2], (L, D, 6 * D), 0.5 * D ** -0.5),
        'b_ada': nrm(ks[3], (L, 6 * D), 0.01),
        'g_norm1': 1.0 + nrm(ks[4], (L, D), 0.02),
        'w_in': nrm(ks[5], (L, D, IN_COLS), D ** -0.5),
        'lam_q1': nrm(ks[6], (L, HEAD_DIM), 0.1),
        'lam_k1': nrm(ks[7], (L, HEAD_DIM), 0.1),
        'lam_q2': nrm(ks[8], (L, HEAD_DIM), 0.1),
        'lam_k2': nrm(ks[9], (L, HEAD_DIM), 0.1),
        'g_subln': 1.0 + nrm(ks[10], (L, 2 * HEAD_DIM), 0.02),
        'conv_w': nrm(ks[11], (L, CONV_W, BRANCH_W), CONV_W ** -0.5),
        'w_pool': nrm(ks[12], (L, N_POOL, POOL_GROUP, POOL_GROUP), POOL_GROUP ** -0.5),
        'pool_scale': 1.0 + nrm(ks[13], (L, BRANCH_W), 0.1),
        'sinks': nrm(ks[14], (L, SW_Q_HEADS), 1.0),
        'w_branch': nrm(ks[15], (L, N_BRANCH, BRANCH_W, D), BRANCH_W ** -0.5),
        'w_o': nrm(ks[16], (L, D, D), D ** -0.5),
        'g_norm2': 1.0 + nrm(ks[17], (L, D), 0.02),
        'w_q': nrm(ks[18], (L, D, PEER_HEADS * PEER_DKEY), D ** -0.5),
        'sub_keys': nrm(ks[19], (L, 2, PEER_NKEYS, PEER_DKEY // 2), (PEER_DKEY // 2) ** -0.5),
        'u_experts': nrm(ks[20], (L, PEER_EXPERTS, D), D ** -0.5),
        'v_experts': nrm(ks[21], (L, PEER_EXPERTS, D), 1.0),
        'g_final': 1.0 + nrm(ks[22], (D,), 0.02),
    }

def reference(x, c, w_ada, b_ada, g_norm1, w_in, lam_q1, lam_k1, lam_q2, lam_k2, g_subln,
              conv_w, w_pool, pool_scale, sinks, w_branch, w_o, g_norm2, w_q, sub_keys,
              u_experts, v_experts, g_final):
    c_act = jax.nn.silu(c)
    for l in range(DEPTH):
        mod = c_act @ w_ada[l] + b_ada[l]
        lam_init = 0.8 - 0.6 * math.exp(-0.3 * l)
        x = hybrid_layer(x, mod, g_norm1[l], w_in[l], lam_q1[l], lam_k1[l], lam_q2[l], lam_k2[l],
                         g_subln[l], conv_w[l], w_pool[l], pool_scale[l], sinks[l], w_branch[l],
                         w_o[l], g_norm2[l], w_q[l], sub_keys[l], u_experts[l], v_experts[l],
                         lam_init)
    return rmsnorm(x, g_final)


_drawn_inputs = setup_inputs


def setup_inputs(seed=0):
    import zlib

    import numpy as np

    out = dict(_drawn_inputs(seed))
    spreads = {}
    factors = {'g_norm1': 3.394,
     'lam_q1': 64.0,
     'lam_k1': 18.167,
     'lam_q2': 3.318,
     'lam_k2': 200.0,
     'g_subln': 45.376,
     'sinks': 57.88,
     'g_final': 22.689,
     'pool_scale': 7.864,
     'g_norm2': 8.0,
     'w_q': 2.998,
     'sub_keys': 2.97,
     'u_experts': 3.328,
     'v_experts': 2.986}
    for name, (base, spread) in spreads.items():
        noise = np.random.default_rng([zlib.crc32(name.encode()), seed]).standard_normal(out[name].shape)
        drawn = base * np.exp(spread * noise) if base else spread * noise
        out[name] = __import__('jax').numpy.asarray(drawn.astype(out[name].dtype))
    for name, factor in factors.items():
        out[name] = (out[name] * factor).astype(out[name].dtype)
    return out
```

```python
from contextlib import ExitStack

import concourse.bass as bass
from concourse import mybir

P = 128
F32 = mybir.dt.float32
F32R = mybir.dt.float32r
U32 = mybir.dt.uint32
ALU = mybir.AluOpType
ACT = mybir.ActivationFunctionType
AX = mybir.AxisListType

EPS = 1e-6
NEG = -1e30
FLT_MAX = 3.4028234663852886e38
DOWN = 2.0 ** -60
UP = 2.0 ** -30
O_BOUND = 2.0 ** 66
SQ_DOWN = 2.0 ** -16
LAM_INIT = 0.2

D = 1024
S = 512
TT = S // P
KD = D // P
BW = 256
HALF = D // 2
CB = HALF // P
NBR = 4
HD = 64
HA = 4
IN_COLS = 8448
MIX_BLOCKS = 17
GATE_BLOCKS = 16
ADA_BLOCKS = 6 * D // BW
PH = 8
NK = 128
TOPK = 16
NE = NK * NK

V_C, V_ADA, V_G1, V_G2, V_CONV, V_POOL, V_SUB = 0, 8, 56, 64, 72, 84, 88
V_ROWS = 89
M_AQ, M_AK, M_AV, M_BB, M_BC, M_BX, M_CZ, M_DQ, M_DK, M_DV = 0, 4, 8, 12, 16, 20, 24, 28, 32, 33


class Count:

    def __init__(self, sem):
        self.sem = sem
        self.n = 0

    def inc(self, ins, by=1):
        ins.then_inc(self.sem, by)
        self.n += by
        return self.n


KB = 1024
KEEP_AT = 16512
LOW = KEEP_AT + 2 * KB
H_AT, Y_AT, XT_AT, MERGED_AT, X2_AT = LOW, LOW + 32 * KB, LOW + 96 * KB, LOW + 96 * KB, LOW + 112 * KB


class Kit:

    def __init__(self, nc, stack, tag, at):
        self.nc, self.stack, self.tag, self.at = nc, stack, tag, at

    def sb(self, name, shape, dt=F32):
        size = 4
        for n in shape[1:]:
            size *= n
        t = self.nc.alloc_sbuf_tensor_at(f"{self.tag}_{name}", shape, dt, offset=self.at)
        self.at += -(-size // 32) * 32
        return t

    def ps(self, name, shape, dt=F32):
        return self.stack.enter_context(self.nc.psum_tensor(f"{self.tag}_{name}", shape, dt))

    def sem(self, name):
        return self.stack.enter_context(self.nc.semaphore(f"{self.tag}_{name}"))

    def count(self, name):
        return Count(self.sem(name))


def three(nc, out, w, x, first, last):
    nc.tensor.matmul(out, w[0], x[0], start=first, stop=False)
    nc.tensor.matmul(out, w[0], x[1], start=False, stop=False)
    return nc.tensor.matmul(out, w[1], x[0], start=False, stop=last)


def chained(eng, sig, ins):
    eng.wait_ge(sig.sem, sig.inc(ins))


def rstd_dve_in(nc, done, ssq, fin, out, most=FLT_MAX):
    nc.vector.tensor_scalar(fin, ssq, most, None, ALU.is_le).then_inc(done, 1)
    nc.vector.tensor_scalar(out, ssq, most, None, ALU.min).then_inc(done, 1)


def rstd_dve_out(nc, dve, sig, root, fin):
    chained(dve, sig, nc.vector.reciprocal(root, root))
    chained(dve, sig, nc.vector.scalar_tensor_tensor(root, root, UP, fin, ALU.mult, ALU.mult))


def phase_condition(nc, a, keep):
    with ExitStack() as stack:
        k = Kit(nc, stack, "cond", Y_AT)
        ring = [k.sb(f"ada{j}", [P, KD, BW]) for j in range(4)]
        rows = k.sb("rows", [P, P])
        lamv = k.sb("lamv", [P, 4, HD])
        lamp = k.sb("lamp", [P, 2, HD])
        lams = k.sb("lams", [P, 4])
        x = k.sb("x", [P, TT, D])
        xn = k.sb("xn", [P, 2, D])
        sq = k.sb("sq", [P, D])
        ssq, fin, root = (k.sb(n, [P, TT]) for n in ("ssq", "fin", "root"))
        csil = k.sb("csil", [P, KD])
        hf = k.sb("hf", [P, KD, S])
        p_cols = k.ps("cols", [P, 512])
        p_mod = k.ps("mod", [P, 512])
        p_x = [k.ps(f"x{j}", [P, KD, P]) for j in range(2)]

        rows_in, lam_in, x_in = k.sem("rows_in"), k.sem("lam_in"), k.sem("x_in")
        ada_in = [k.sem(f"ada_in{j}") for j in range(4)]
        const, cols_t, cols_ok, sil_ok, mod_mm = (k.sem(n) for n in ("const", "cols_t", "cols_ok", "sil_ok", "mod_mm"))
        lam_e, ssq_ok, root_ok, xn_ok, x_t, h_ok, hi_ok = (
            k.sem(n) for n in ("lam_e", "ssq_ok", "root_ok", "xn_ok", "x_t", "h_ok", "hi_ok"))
        coef_ok, lam_s, v_ok = k.sem("coef_ok"), k.sem("lam_s"), k.sem("v_ok")
        dve_c, pool_c = k.count("dve_chain"), k.count("pool_chain")
        ada = a["w_ada"][0].rearrange("(k p) n -> p k n", p=P)
        block = stack.enter_context(nc.Block())

        @block.sync
        def _(sp):
            r = 0
            sp.wait_ge(const, 5)
            for name, src in (("c", a["c"]), ("b_ada", a["b_ada"]), ("g_norm1", a["g_norm1"]), ("g_norm2", a["g_norm2"]),
                              ("conv_w", a["conv_w"].rearrange("l j n -> l (j n)")), ("pool_scale", a["pool_scale"]),
                              ("g_subln", a["g_subln"])):
                n = src.shape[1] // P
                sp.dma_start(rows[r:r + n, :], src[0].rearrange("(m p) -> m p", p=P)).then_inc(rows_in, 16)
                r += n
            for j in range(4):
                sp.dma_start(ring[j][:, :, :], ada[:, :, j * BW:(j + 1) * BW]).then_inc(ada_in[j], 16)
            sp.dma_start(x[:, :, :], a["x"][0].rearrange("(i p) d -> p i d", p=P)).then_inc(x_in, 16)
            for n, name in enumerate(("lam_q1", "lam_k1", "lam_q2", "lam_k2")):
                sp.dma_start(lamv[:, n, :], a[name].to_broadcast([P, HD])).then_inc(lam_in, 16)
            sp.dma_start(keep["sinks"][:, :], a["sinks"].to_broadcast([P, 8])).then_inc(lam_in, 16)
            with sp.Fori(1, ADA_BLOCKS // 4) as i:
                for j in range(4):
                    sp.wait_ge(mod_mm, 4 * i + j - 3)
                    sp.dma_start(ring[j][:, :, :], ada[:, :, bass.ds((4 * i + j) * BW, BW)]).then_inc(ada_in[j], 16)
            sp.wait_ge(lam_in, 80)

        @block.gpsimd
        def _(pool):
            nc.gpsimd.memset(keep["eps"][:, :], EPS * DOWN).then_inc(const, 1)
            nc.gpsimd.memset(keep["ones"][:, :], 1.0).then_inc(const, 1)
            nc.gpsimd.memset(keep["invn"][:, :], 0.0).then_inc(const, 1)
            nc.gpsimd.memset(rows[:, :], 0.0).then_inc(const, 1)
            chained(pool, pool_c, nc.gpsimd.memset(keep["ident"][:, :], 0.0))
            nc.gpsimd.affine_select(out=keep["ident"][:, :], in_=keep["ident"][:, :], compare_op=ALU.not_equal, fill=1.0,
                                    base=0, pattern=[[-1, P]], channel_multiplier=1).then_inc(const, 1)
            for i in range(TT):
                pool.wait_ge(h_ok, i + 1)
                ts = slice(i * P, (i + 1) * P)
                nc.gpsimd.tensor_copy(keep["h_hi"][:, :, ts], hf[:, :, ts]).then_inc(hi_ok, 1)

        @block.scalar
        def _(act):
            act.wait_ge(cols_ok, 1)
            nc.scalar.activation(csil[:, :], keep["cols"][:, V_C:V_C + KD], ACT.Silu).then_inc(sil_ok, 1)
            act.wait_ge(lam_s, 2)
            nc.scalar.activation(lams[:, 2:4], lams[:, 0:2], ACT.Exp).then_inc(lam_e, 1)
            act.wait_ge(ssq_ok, 2)
            act.wait_ge(const, 5)
            nc.scalar.activation(root[:, :], root[:, :], ACT.Sqrt, bias=keep["eps"][:, :], scale=DOWN / D).then_inc(root_ok, 1)
            act.wait_ge(coef_ok, 1)
            for i in range(TT):
                act.wait_ge(x_t, i + 1)
                for c in range(KD):
                    ins = nc.scalar.activation(hf[:, c, i * P:(i + 1) * P], p_x[i % 2][:, c, :], ACT.Identity,
                                               bias=keep["mod"][:, c:c + 1], scale=keep["scale1"][:, c:c + 1])
                ins.then_inc(h_ok, 1)

        @block.vector
        def _(dve):
            dve.wait_ge(cols_t, 1)
            nc.vector.tensor_copy(keep["cols"][:, :], p_cols[:, 0:V_ROWS]).then_inc(cols_ok, 1)
            dve.wait_ge(x_in, 16)
            for i in range(TT):
                chained(dve, dve_c, nc.vector.tensor_tensor_reduce(
                    out=sq[:, :], in0=x[:, i, :], in1=x[:, i, :], scale=1.0, scalar=0.0,
                    op0=ALU.mult, op1=ALU.add, accum_out=ssq[:, i:i + 1]))
            rstd_dve_in(nc, ssq_ok, ssq[:, :], fin[:, :], root[:, :])
            dve.wait_ge(lam_in, 80)
            for n in range(2):
                nc.vector.tensor_tensor_reduce(
                    out=lamp[:, n, :], in0=lamv[:, 2 * n, :], in1=lamv[:, 2 * n + 1, :], scale=1.0, scalar=0.0,
                    op0=ALU.mult, op1=ALU.add, accum_out=lams[:, n:n + 1]).then_inc(lam_s, 1)
            dve.wait_ge(root_ok, 1)
            rstd_dve_out(nc, dve, dve_c, root[:, :], fin[:, :])
            for i in range(TT):
                if i >= 2:
                    dve.wait_ge(x_t, i - 1)
                nc.vector.tensor_scalar(xn[:, i % 2, :], x[:, i, :], root[:, i:i + 1], None, ALU.mult).then_inc(xn_ok, 1)
                if i == 1:
                    dve.wait_ge(lam_e, 1)
                    chained(dve, dve_c, nc.vector.tensor_tensor(keep["neglam"][:, :], lams[:, 3:4], lams[:, 2:3], ALU.subtract))
                    chained(dve, dve_c, nc.vector.tensor_scalar(keep["neglam"][:, :], keep["neglam"][:, :], -LAM_INIT, None, ALU.add))
                    dve.wait_ge(mod_mm, ADA_BLOCKS)
                    chained(dve, dve_c, nc.vector.tensor_tensor(keep["mod"][:, :], p_mod[:, 0:48], keep["cols"][:, V_ADA:V_ADA + 48], ALU.add))
                    for out, m, g in ((keep["scale1"], 8, V_G1), (keep["scale2"], 32, V_G2)):
                        ins = nc.vector.scalar_tensor_tensor(out[:, :], keep["mod"][:, m:m + 8], 1.0, keep["cols"][:, g:g + 8], ALU.add, ALU.mult)
                    ins.then_inc(coef_ok, 1)
            for i in range(TT):
                dve.wait_ge(hi_ok, i + 1)
                ts = slice(i * P, (i + 1) * P)
                nc.vector.tensor_tensor(keep["h_lo"][:, :, ts], hf[:, :, ts], keep["h_hi"][:, :, ts].bitcast(F32),
                                        ALU.subtract).then_inc(v_ok, 1)

        @block.tensor
        def _(pe):
            pe.wait_ge(rows_in, 7 * 16)
            pe.wait_ge(const, 5)
            nc.tensor.transpose(p_cols[:, 0:P], rows[:, :], keep["ident"][:, :]).then_inc(cols_t, 1)
            pe.wait_ge(sil_ok, 1)

            def modulate(i, j):
                pe.wait_ge(ada_in[j], 16 * i + 16)
                for m in range(2):
                    col = p_mod[:, bass.ds((4 * i + j) * 2 + m, 1)]
                    for c in range(KD):
                        ins = nc.tensor.matmul(col, ring[j][:, c, m * P:(m + 1) * P], csil[:, c:c + 1],
                                               start=c == 0, stop=c == KD - 1)
                ins.then_inc(mod_mm, 1)

            with pe.Fori(0, ADA_BLOCKS // 4) as i:
                for j in range(4):
                    modulate(i, j)
            for i in range(TT):
                pe.wait_ge(xn_ok, i + 1)
                if i >= 2:
                    pe.wait_ge(h_ok, i - 1)
                for c in range(KD):
                    ins = nc.tensor.transpose(p_x[i % 2][:, c, :], xn[:, i % 2, c * P:(c + 1) * P], keep["ident"][:, :])
                ins.then_inc(x_t, 1)


def phase_project(nc, a, keep, xt, space):
    with ExitStack() as stack:
        k = Kit(nc, stack, "proj", XT_AT + 68 * KB)
        raw = [k.sb(f"raw{j}", [P, KD, BW]) for j in range(4)]
        parts = space[:, :, :].rearrange("p (x a) b -> p x (a b)", x=4).rearrange("p x (k n) -> p x k n", k=KD)
        hi, lo = [parts[:, j] for j in (0, 1)], [parts[:, j] for j in (2, 3)]
        acc = [k.ps(f"acc{j}", [P, S]) for j in range(4)]
        w_in = [k.sem(f"w_in{j}") for j in range(4)]
        hi_ok, lo_ok, mm, out_ok = (k.sem(n) for n in ("hi_ok", "lo_ok", "mm", "out_ok"))
        w = a["w_in"][0].rearrange("(k p) n -> p k n", p=P)
        NB = MIX_BLOCKS
        LOOPS = (NB - 5) // 4
        block = stack.enter_context(nc.Block())

        def cols(b):
            return w[:, :, bass.ds(b * BW, BW)]

        @block.sync
        def _(sp):
            for b in range(4):
                sp.dma_start(raw[b][:, :, :], cols(b)).then_inc(w_in[b], 16)

            def load(b, j):
                sp.wait_ge(lo_ok, b - 3)
                sp.dma_start(raw[j][:, :, :], cols(b)).then_inc(w_in[j], 16)

            with sp.Fori(1, NB // 4) as i:
                for j in range(4):
                    load(4 * i + j, j)
            load(NB - 1, 0)

        def split_hi(act, b, j, turn, first=False):
            act.wait_ge(w_in[j], 16 * turn + 16)
            if not first:
                act.wait_ge(mm, 2 * b - 2)
            nc.scalar.activation(hi[j % 2][:, :, :], raw[j][:, :, :], ACT.Copy).then_inc(hi_ok, 1)

        @block.scalar
        def _(act):
            def store(b, j):
                for m in range(2):
                    act.wait_ge(mm, 2 * b + m + 1)
                    nc.scalar.activation(xt[:, bass.ds(2 * b + m, 1), :], acc[2 * (j % 2) + m][:, :], ACT.Copy).then_inc(out_ok, 1)

            split_hi(act, 0, 0, 0, True)
            split_hi(act, 1, 1, 0, True)
            store(0, 0)
            for b in range(1, 4):
                split_hi(act, b + 1, (b + 1) % 4, (b + 1) // 4)
                store(b, b)
            with act.Fori(1, NB // 4) as i:
                for j in range(4):
                    split_hi(act, 4 * i + j + 1, (j + 1) % 4, i + (j + 1) // 4)
                    store(4 * i + j, j)
            store(NB - 1, 0)

        @block.vector
        def _(dve):
            def split_lo(b, j, first=False):
                dve.wait_ge(hi_ok, b + 1)
                nc.vector.tensor_tensor(lo[j % 2][:, :, :], raw[j][:, :, :], hi[j % 2][:, :, :].bitcast(F32),
                                        ALU.subtract).then_inc(lo_ok, 1)

            with dve.Fori(0, NB // 4) as i:
                for j in range(4):
                    split_lo(4 * i + j, j)
            split_lo(NB - 1, 0)

        @block.tensor
        def _(pe):
            def product(b, j, first=False):
                pe.wait_ge(lo_ok, b + 1)
                for m in range(2):
                    if not first:
                        pe.wait_ge(out_ok, 2 * b + m - 3)
                    ms = slice(m * P, (m + 1) * P)
                    for c in range(KD):
                        ins = three(nc, acc[2 * (j % 2) + m][:, :], (hi[j % 2][:, c, ms], lo[j % 2][:, c, ms]),
                                    (keep["h_hi"][:, c, :], keep["h_lo"][:, c, :]), c == 0, c == KD - 1)
                    ins.then_inc(mm, 1)

            for b in range(4):
                product(b, b, b < 2)
            with pe.Fori(1, NB // 4) as i:
                for j in range(4):
                    product(4 * i + j, j)
            product(NB - 1, 0)
            pe.wait_ge(out_ok, 2 * NB)


def phase_mix(nc, a, keep, xt, y_hi, y_lo):
    units = [u for i in range(TT) for u in [("A", i, h) for h in range(HA)] + [("B", i, g) for g in range(2)]]
    NU = len(units)
    with ExitStack() as stack:
        k = Kit(nc, stack, "mix", XT_AT + 68 * KB)
        vn = k.sb("vn", [P, TT, HA, P])
        dvn = k.sb("dvn", [P, TT, P])
        kd = k.sb("kd", [P, 2, S])
        sm = k.sb("sm", [P, 2, 1024])
        pt = k.sb("pt", [P, 2, 8, P])
        causal = k.sb("causal", [P, S])
        band = k.sb("band", [P, 2 * P])
        pad = [k.sb(f"pad{j}", [P, 16 + S]) for j in range(2)]
        rcount = k.sb("rcount", [P, 16])
        wpool = k.sb("wpool", [P, 4, P])
        small = {n: k.sb(n, [P, 2, 4]) for n in ("mx", "nm", "z", "r", "sd", "es")}
        ssq, fin, root = (k.sb(n, [P, 16]) for n in ("ssq", "fin", "root"))
        subg = k.sb("subg", [P, 1])
        p_s = [k.ps(f"s{j}", [P, 1024]) for j in range(2)]
        p_t = k.ps("t", [P, 8, P])
        p_o = k.ps("o", [P, S])
        p_w = k.ps("w", [P, S])
        names = ("masks wpool_in kd_in vt vn_ok sc masked stats exped normed tr pt_ok pv o_ok pool_d pw y2_ok conv_ok "
                 "ssq_ok root_ok on_ok yt y0_ok y2_hi y3_hi y0_hi pads subg_ok").split()
        sem = {n: k.sem(n) for n in names}
        dve_c, pool_c = k.count("dve_chain"), k.count("pool_chain")
        block = stack.enter_context(nc.Block())
        scale = HD ** -0.5

        def width(u):
            kind, i, _ = u
            return (i + 1) * P if kind == "A" else (P if i == 0 else 2 * P)

        def group(n):
            kind = units[n][0]
            return 2 if kind == "A" else 4

        def view(t, n):
            m = group(n)
            return t.rearrange("p (m w) -> p m w", m=m)[:, :, 0:width(units[n])]

        def blocks(n):
            w = width(units[n]) // P
            return [(m, j) for m in range(1 if units[n][0] == "A" else 4) for j in range(w)]

        @block.sync
        def _(sp):
            for g in range(2):
                for half in range(2):
                    sp.dma_start(kd[half * HD:(half + 1) * HD, g, :], xt[g * HD:(g + 1) * HD, M_DK, :]).then_inc(sem["kd_in"], 16)
            sp.dma_start(wpool[:, :, :], a["w_pool"][0].rearrange("g c e -> c g e")).then_inc(sem["wpool_in"], 16)
            sp.wait_ge(sem["kd_in"], 64)
            sp.wait_ge(sem["wpool_in"], 16)

        @block.gpsimd
        def _(pool):
            nc.gpsimd.memset(causal[:, :], 0.0).then_inc(sem["pads"], 1)
            nc.gpsimd.memset(band[:, :], 0.0).then_inc(sem["pads"], 1)
            nc.gpsimd.memset(pad[0][:, 0:16], 0.0).then_inc(sem["pads"], 1)
            nc.gpsimd.memset(pad[1][:, 0:16], 0.0).then_inc(sem["pads"], 1)
            pool.wait_ge(sem["pads"], 4)
            nc.gpsimd.affine_select(out=causal[:, :], in_=causal[:, :], compare_op=ALU.is_ge, fill=NEG, base=S - P,
                                    pattern=[[-1, S]], channel_multiplier=1).then_inc(sem["masks"], 1)
            chained(pool, pool_c, nc.gpsimd.affine_select(out=band[:, :], in_=band[:, :], compare_op=ALU.is_gt, fill=NEG, base=0,
                                                         pattern=[[1, 2 * P]], channel_multiplier=-1))
            nc.gpsimd.affine_select(out=band[:, :], in_=band[:, :], compare_op=ALU.is_ge, fill=NEG, base=P,
                                    pattern=[[-1, 2 * P]], channel_multiplier=1).then_inc(sem["masks"], 1)
            chained(pool, pool_c, nc.gpsimd.iota(rcount[:, :], pattern=[[1, 16]], base=1, channel_multiplier=0,
                                                 allow_small_or_imprecise_dtypes=True))
            nc.gpsimd.tensor_copy(keep["invn"][:, :], rcount[:, :]).then_inc(sem["pads"], 1)

            pool.wait_ge(sem["y2_ok"], 1)
            for g in range(4):
                w = 2 << g
                src, at = xt[:, M_CZ + g, :], 0
                chained(pool, pool_c, nc.gpsimd.tensor_copy(pad[0][:, 16:], src))
                for level in range(g + 1):
                    sh = 1 << level
                    chained(pool, pool_c, nc.gpsimd.tensor_tensor(pad[1 - at][:, 16:], pad[at][:, 16:], pad[at][:, 16 - sh:16 + S - sh], ALU.add))
                    at = 1 - at
                t = pad[at]
                nc.gpsimd.tensor_scalar(t[:, 16 + w:], t[:, 16 + w:], 1.0 / w, None, ALU.mult).then_inc(pool_c.sem, 1)
                nc.gpsimd.tensor_tensor(t[:, 16:16 + w], t[:, 16:16 + w], keep["invn"][:, 0:w], ALU.mult).then_inc(pool_c.sem, 1)
                pool_c.n += 2
                pool.wait_ge(pool_c.sem, pool_c.n)
                nc.gpsimd.tensor_tensor(src, t[:, 16:], src, ALU.subtract).then_inc(sem["pool_d"], 1)
                pool.wait_ge(sem["pool_d"], g + 1)

            z = xt[:, M_BX:M_BX + 4, :]
            chained(pool, pool_c, nc.gpsimd.tensor_tensor(z, z, xt[:, M_BC:M_BC + 4, :], ALU.mult))
            for c in range(CB):
                y, zc = xt[:, M_BC + c, :], xt[:, M_BX + c, :]
                taps = [keep["cols"][:, V_CONV + 4 * j + c:V_CONV + 4 * j + c + 1] for j in range(3)]
                chained(pool, pool_c, nc.gpsimd.tensor_scalar(y, zc, taps[2], None, ALU.mult))
                for back, tap in ((1, taps[1]), (2, taps[0])):
                    n = S - back
                    tmp = pad[back - 1][:, 16:16 + n]
                    chained(pool, pool_c, nc.gpsimd.tensor_scalar(tmp, zc[:, 0:n], tap, None, ALU.mult))
                    chained(pool, pool_c, nc.gpsimd.tensor_tensor(y[:, back:], y[:, back:], tmp, ALU.add))
                chained(pool, pool_c, nc.gpsimd.tensor_tensor(y, y, xt[:, M_BB + c, :], ALU.mult))
                chained(pool, pool_c, nc.gpsimd.tensor_copy(y_hi[:, 1, c, :], y))
                nc.gpsimd.tensor_tensor(y_lo[:, 1, c, :], y, y_hi[:, 1, c, :].bitcast(F32), ALU.subtract).then_inc(sem["conv_ok"], 1)
            for n, (ready, times, m, hi) in enumerate((("y2_ok", 5, M_CZ, "y2_hi"), ("o_ok", NU, M_DQ, "y3_hi"), ("y0_ok", 4, M_AQ, "y0_hi"))):
                pool.wait_ge(sem[ready], times)
                nc.gpsimd.tensor_copy(y_hi[:, (2, 3, 0)[n], :, :], xt[:, m:m + 4, :]).then_inc(sem[hi], 1)
            pool.wait_ge(sem["conv_ok"], 4)

        @block.scalar
        def _(act):
            act.wait_ge(sem["vt"], 1)
            nc.scalar.activation(vn[:, 0:2, :, :].rearrange("p i h e -> p (i h e)"), p_s[0][:, :], ACT.Copy).then_inc(sem["vn_ok"], 1)
            act.wait_ge(sem["vt"], 2)
            nc.scalar.activation(vn[:, 2:4, :, :].rearrange("p i h e -> p (i h e)"), p_s[1][:, :], ACT.Copy).then_inc(sem["vn_ok"], 1)
            act.wait_ge(sem["vt"], 3)
            nc.scalar.activation(dvn[:, :, :], p_t[:, 0:4, :], ACT.Copy).then_inc(sem["vn_ok"], 1)

            def exps(n):
                u, b = units[n], n % 2
                act.wait_ge(sem["stats"], n + 1)
                for m in range(group(n)):
                    t = view(sm[:, b, :], n)[:, m, :]
                    ins = nc.scalar.activation(t, t, ACT.Exp, bias=small["nm"][:, b, m:m + 1], accum_out=small["z"][:, b, m:m + 1])
                if u[0] == "B":
                    ins = nc.scalar.activation(small["es"][:, b, :], small["sd"][:, b, :], ACT.Exp)
                ins.then_inc(sem["exped"], 1)

            exps(0)
            for n, (kind, i, h) in enumerate(units):
                if n + 1 < NU:
                    exps(n + 1)
                act.wait_ge(sem["tr"], n + 1)
                if n >= 2:
                    act.wait_ge(sem["pv"], n - 1)
                nb = len(blocks(n))
                nc.scalar.activation(pt[:, n % 2, 0:nb, :], p_t[:, 0:nb, :], ACT.Copy).then_inc(sem["pt_ok"], 1)
                act.wait_ge(sem["pv"], n + 1)
                if kind == "A":
                    nc.scalar.activation(xt[:, M_AV + i, h * P:(h + 1) * P], p_o[:, 0:P], ACT.Copy).then_inc(sem["o_ok"], 1)
                else:
                    nc.scalar.activation(xt[:, M_DQ + 2 * h:M_DQ + 2 * h + 2, i * P:(i + 1) * P],
                                         p_o[:, 0:2 * P].rearrange("p (m q) -> p m q", m=2), ACT.Copy).then_inc(sem["o_ok"], 1)
            for g in range(4):
                act.wait_ge(sem["pw"], g + 1)
                nc.scalar.activation(xt[:, M_CZ + g, :], p_w[:, :], ACT.Copy, scale=keep["cols"][:, V_POOL + g:V_POOL + g + 1]).then_inc(sem["y2_ok"], 1)
            act.wait_ge(sem["ssq_ok"], 2)
            nc.scalar.activation(root[:, :], root[:, :], ACT.Sqrt, bias=keep["eps"][:, :], scale=DOWN / SQ_DOWN / P).then_inc(sem["root_ok"], 1)
            act.wait_ge(sem["subg_ok"], 1)
            for h in range(HA):
                act.wait_ge(sem["yt"], h + 1)
                nc.scalar.activation(xt[:, M_AQ + h, :], p_s[h % 2][:, 0:S], ACT.Copy, scale=subg[:, :]).then_inc(sem["y0_ok"], 1)

        @block.vector
        def _(dve):
            nc.vector.tensor_scalar(subg[:, :], keep["cols"][:, V_SUB:V_SUB + 1], 1.0 - LAM_INIT, None, ALU.mult).then_inc(sem["subg_ok"], 1)
            dve.wait_ge(sem["pads"], 5)
            nc.vector.reciprocal(keep["invn"][:, :], keep["invn"][:, :]).then_inc(sem["y2_ok"], 1)
            dve.wait_ge(sem["masks"], 2)

            def scores_in(n):
                (kind, i, h), b = units[n], n % 2
                m, w = group(n), width(units[n])
                t = view(sm[:, b, :], n)
                mask = causal[:, S - w:] if kind == "A" else band[:, 2 * P - w:]
                dve.wait_ge(sem["sc"], n + 1)
                if n >= 2:
                    dve.wait_ge(sem["tr"], n - 1)
                dve_c.inc(nc.vector.scalar_tensor_tensor(t, view(p_s[b][:, :], n), scale, mask.rearrange("p (o w) -> p o w", o=1).broadcast_to([P, m, w]),
                                                         ALU.mult, ALU.add))
                dve.wait_ge(dve_c.sem, dve_c.n)
                mx, nm = small["mx"][:, b, 0:m], small["nm"][:, b, 0:m]
                chained(dve, dve_c, nc.vector.reduce_max(mx, t, AX.X))
                if kind == "B":
                    sink = keep["sinks"][:, 4 * h:4 * h + 4].rearrange("p (pair odd) -> p odd pair", odd=2)
                    mx2, sd2 = (small[x][:, b, :].rearrange("p (odd pair) -> p odd pair", odd=2) for x in ("mx", "sd"))
                    chained(dve, dve_c, nc.vector.tensor_tensor(mx2, mx2, sink, ALU.max))
                    chained(dve, dve_c, nc.vector.tensor_tensor(sd2, sink, mx2, ALU.subtract))
                nc.vector.tensor_scalar(nm, mx, -1.0, None, ALU.mult).then_inc(sem["stats"], 1)

            def normalise(n):
                (kind, i, h), b = units[n], n % 2
                t = view(sm[:, b, :], n)
                z, r = small["z"][:, b, :], small["r"][:, b, :]
                dve.wait_ge(sem["exped"], n + 1)
                if kind == "A":
                    chained(dve, dve_c, nc.vector.reciprocal(r[:, 0:2], z[:, 0:2]))
                    chained(dve, dve_c, nc.vector.tensor_tensor(r[:, 1:2], r[:, 1:2], keep["neglam"][:, :], ALU.mult))
                    chained(dve, dve_c, nc.vector.tensor_scalar(t[:, 0, :], t[:, 0, :], r[:, 0:1], None, ALU.mult))
                    nc.vector.scalar_tensor_tensor(t[:, 0, :], t[:, 1, :], r[:, 1:2], t[:, 0, :], ALU.mult, ALU.add).then_inc(sem["normed"], 1)
                else:
                    chained(dve, dve_c, nc.vector.tensor_tensor(z, z, small["es"][:, b, :], ALU.add))
                    chained(dve, dve_c, nc.vector.reciprocal(r, z))
                    nc.vector.tensor_tensor(t, t, r.rearrange("p (m o) -> p m o", o=1).broadcast_to([P, 4, width(units[n])]),
                                            ALU.mult).then_inc(sem["normed"], 1)

            scores_in(0)
            for n in range(NU):
                if n + 1 < NU:
                    scores_in(n + 1)
                normalise(n)
            dve.wait_ge(sem["o_ok"], NU)
            dve.wait_ge(sem["tr"], NU)
            o = xt[:, M_AV:M_AV + 4, :].rearrange("p i (h e) -> p (i h) e", e=P)
            sq = sm[:, :, :].rearrange("p b (x e) -> p (b x) e", e=P)
            chained(dve, dve_c, nc.vector.tensor_scalar(sq, o, O_BOUND, -O_BOUND, ALU.min, ALU.max))
            chained(dve, dve_c, nc.vector.scalar_tensor_tensor(sq, sq, SQ_DOWN, sq, ALU.mult, ALU.mult))
            chained(dve, dve_c, nc.vector.reduce_sum(ssq[:, :], sq, AX.X))
            rstd_dve_in(nc, sem["ssq_ok"], ssq[:, :], fin[:, :], root[:, :], FLT_MAX * SQ_DOWN)
            dve.wait_ge(sem["root_ok"], 1)
            rstd_dve_out(nc, dve, dve_c, root[:, :], fin[:, :])
            nc.vector.tensor_tensor(o, o, root[:, :].rearrange("p (x o) -> p x o", o=1).broadcast_to([P, 16, P]),
                                    ALU.mult).then_inc(sem["on_ok"], 1)
            for n, (m, hi) in enumerate(((M_CZ, "y2_hi"), (M_DQ, "y3_hi"), (M_AQ, "y0_hi"))):
                dve.wait_ge(sem[hi], 1)
                y = (2, 3, 0)[n]
                nc.vector.tensor_tensor(y_lo[:, y, :, :], xt[:, m:m + 4, :], y_hi[:, y, :, :].bitcast(F32), ALU.subtract).then_inc(dve_c.sem, 1)
                dve_c.n += 1
            dve.wait_ge(dve_c.sem, dve_c.n)

        @block.tensor
        def _(pe):
            ident = keep["ident"][:, :]
            for half in range(2):
                for j in range(8):
                    i, h = 2 * half + j // 4, j % 4
                    ins = nc.tensor.transpose(p_s[half][:, j * P:(j + 1) * P], xt[:, M_AV + h, i * P:(i + 1) * P], ident)
                ins.then_inc(sem["vt"], 1)
            for i in range(TT):
                ins = nc.tensor.transpose(p_t[:, i, :], xt[:, M_DV, i * P:(i + 1) * P], ident)
            ins.then_inc(sem["vt"], 1)
            pe.wait_ge(sem["kd_in"], 64)

            def scores(n):
                kind, i, h = units[n]
                if n < 2:
                    pe.wait_ge(sem["vn_ok"], n + 1)
                else:
                    pe.wait_ge(sem["stats"], n - 1)
                out = view(p_s[n % 2][:, :], n)
                qs = slice(i * P, (i + 1) * P)
                for m in range(group(n)):
                    if kind == "A":
                        rows = slice(m * HD, (m + 1) * HD)
                        q, kk = xt[rows, M_AQ + h, qs], xt[rows, M_AK + h, 0:(i + 1) * P]
                    else:
                        rows = slice(m // 2 * HD, (m // 2 + 1) * HD)
                        q, kk = xt[rows, M_DQ + 2 * h + m % 2, qs], kd[rows, h, max(0, (i - 1) * P):(i + 1) * P]
                    ins = nc.tensor.matmul(out[:, m, :], q, kk, start=True, stop=True)
                ins.then_inc(sem["sc"], 1)

            scores(0)
            scores(1)
            for n, (kind, i, h) in enumerate(units):
                pe.wait_ge(sem["normed"], n + 1)
                if n == 0:
                    pe.wait_ge(sem["vn_ok"], 3)
                else:
                    pe.wait_ge(sem["pt_ok"], n)
                for x, (m, j) in enumerate(blocks(n)):
                    ins = nc.tensor.transpose(p_t[:, x, :], view(sm[:, n % 2, :], n)[:, m, j * P:(j + 1) * P], ident)
                ins.then_inc(sem["tr"], 1)
                if n + 2 < NU:
                    scores(n + 2)
                pe.wait_ge(sem["pt_ok"], n + 1)
                if n >= 1:
                    pe.wait_ge(sem["o_ok"], n)
                w = width(units[n]) // P
                for x, (m, j) in enumerate(blocks(n)):
                    if kind == "A":
                        ins = nc.tensor.matmul(p_o[:, 0:P], pt[:, n % 2, x, :], vn[:, j, h, :], start=j == 0, stop=j == w - 1)
                    else:
                        lo = m // 2 * HD
                        ins = nc.tensor.matmul(p_o[lo:lo + HD, m % 2 * P:(m % 2 + 1) * P], dvn[:, i + 1 - w + j, h * HD:(h + 1) * HD],
                                               pt[:, n % 2, x, :], start=j == 0, stop=j == w - 1)
                ins.then_inc(sem["pv"], 1)
            pe.wait_ge(sem["wpool_in"], 16)
            for g in range(4):
                pe.wait_ge(sem["pool_d"], g + 1)
                if g:
                    pe.wait_ge(sem["y2_ok"], g + 1)
                nc.tensor.matmul(p_w[:, :], wpool[:, g, :], xt[:, M_CZ + g, :], start=True, stop=True).then_inc(sem["pw"], 1)
            pe.wait_ge(sem["on_ok"], 1)
            for h in range(HA):
                if h >= 2:
                    pe.wait_ge(sem["y0_ok"], h - 1)
                for i in range(TT):
                    ins = nc.tensor.transpose(p_s[h % 2][:, i * P:(i + 1) * P], xt[:, M_AV + i, h * P:(h + 1) * P], ident)
                ins.then_inc(sem["yt"], 1)


def phase_gate(nc, a, keep, y_hi, y_lo, merged):
    with ExitStack() as stack:
        k = Kit(nc, stack, "gate", MERGED_AT + 16 * KB)
        raw_g = [k.sb(f"raw_g{j}", [P, KD, BW]) for j in range(2)]
        raw_b = [k.sb(f"raw_b{j}", [P, CB, BW]) for j in range(2)]
        gate_w = [[k.sb(f"g{x}{j}", [P, KD, BW], F32R) for x in ("hi", "lo")] for j in range(2)]
        br_w = [[k.sb(f"b{x}{j}", [P, CB, BW], F32R) for x in ("hi", "lo")] for j in range(2)]
        sig = [k.sb(f"sig{j}", [P, S]) for j in range(2)]
        part = [k.sb(f"part{j}", [P, S]) for j in range(2)]
        p_g = [k.ps(f"g{j}", [P, S]) for j in range(4)]
        p_b = [k.ps(f"b{j}", [P, S]) for j in range(4)]
        g_in, b_in = [k.sem(f"g_in{j}") for j in range(2)], [k.sem(f"b_in{j}") for j in range(2)]
        zeroed, hi_ok, lo_ok, mm, sig_ok, part_ok, add_ok = (k.sem(n) for n in ("zeroed", "hi_ok", "lo_ok", "mm", "sig_ok", "part_ok", "add_ok"))
        wg = a["w_in"][0].rearrange("(k p) n -> p k n", p=P)
        wb = a["w_branch"][0].rearrange("g (k p) n -> p (g k) n", p=P)
        STEPS = NBR * 4
        block = stack.enter_context(nc.Block())

        @block.sync
        def _(sp):
            def load(g, d, wait=True):
                s = 4 * g + d
                if wait:
                    sp.wait_ge(lo_ok, 2 * s - 2)
                sp.dma_start(raw_g[d % 2][:, :, :], wg[:, :, bass.ds((MIX_BLOCKS + s) * BW, BW)]).then_inc(g_in[d % 2], 16)
                sp.dma_start(raw_b[d % 2][:, :, :], wb[:, bass.ds(4 * g, CB), d * BW:(d + 1) * BW]).then_inc(b_in[d % 2], 16)

            load(0, 0, False)
            load(0, 1, False)
            load(0, 2)
            load(0, 3)
            with sp.Fori(1, NBR) as g:
                for d in range(4):
                    load(g, d)

        @block.scalar
        def _(act):
            def split(g, d, wait=True):
                s, j = 4 * g + d, d % 2
                act.wait_ge(g_in[j], (2 * g + d // 2) * 16 + 16)
                act.wait_ge(b_in[j], (2 * g + d // 2) * 16 + 16)
                if wait:
                    act.wait_ge(mm, 2 * s - 2)
                nc.scalar.activation(gate_w[j][0][:, :, :], raw_g[j][:, :, :], ACT.Copy).then_inc(hi_ok, 1)
                nc.scalar.activation(br_w[j][0][:, :, :], raw_b[j][:, :, :], ACT.Copy).then_inc(hi_ok, 1)

            def sigmoid(g, d, first=False):
                s = 4 * g + d
                for m in range(2):
                    act.wait_ge(mm, 2 * s + m + 1)
                    if not (first and d == 0):
                        act.wait_ge(part_ok, 2 * s + m - 1)
                    nc.scalar.activation(sig[m][:, :], p_g[2 * (d % 2) + m][:, :], ACT.Sigmoid).then_inc(sig_ok, 1)

            split(0, 0, False)
            split(0, 1, False)
            sigmoid(0, 0, True)
            for d in range(1, 4):
                split(0, d + 1) if d < 3 else split(1, 0)
                sigmoid(0, d)
            with act.Fori(1, NBR - 1) as g:
                for d in range(4):
                    split(g, d + 1) if d < 3 else split(g + 1, 0)
                    sigmoid(g, d)
            for d in range(4):
                if d < 3:
                    split(NBR - 1, d + 1)
                sigmoid(NBR - 1, d)

        @block.vector
        def _(dve):
            def split(g, d):
                s, j = 4 * g + d, d % 2
                dve.wait_ge(hi_ok, 2 * s + 1)
                nc.vector.tensor_tensor(gate_w[j][1][:, :, :], raw_g[j][:, :, :], gate_w[j][0][:, :, :].bitcast(F32), ALU.subtract).then_inc(lo_ok, 1)
                dve.wait_ge(hi_ok, 2 * s + 2)
                nc.vector.tensor_tensor(br_w[j][1][:, :, :], raw_b[j][:, :, :], br_w[j][0][:, :, :].bitcast(F32), ALU.subtract).then_inc(lo_ok, 1)

            def weigh(g, d, first=False):
                s = 4 * g + d
                for m in range(2):
                    dve.wait_ge(sig_ok, 2 * s + m + 1)
                    if not (first and d == 0):
                        dve.wait_ge(add_ok, 2 * s + m - 1)
                    nc.vector.tensor_tensor(part[m][:, :], sig[m][:, :], p_b[2 * (d % 2) + m][:, :], ALU.mult).then_inc(part_ok, 1)

            split(0, 0)
            for d in range(4):
                split(0, d + 1) if d < 3 else split(1, 0)
                weigh(0, d, True)
            with dve.Fori(1, NBR - 1) as g:
                for d in range(4):
                    split(g, d + 1) if d < 3 else split(g + 1, 0)
                    weigh(g, d)
            for d in range(4):
                if d < 3:
                    split(NBR - 1, d + 1)
                weigh(NBR - 1, d)

        @block.gpsimd
        def _(pool):
            nc.gpsimd.memset(merged[:, :, :], 0.0).then_inc(zeroed, 1)
            pool.wait_ge(zeroed, 1)
            with pool.Fori(0, NBR) as g:
                for d in range(4):
                    for m in range(2):
                        s = 4 * g + d
                        pool.wait_ge(part_ok, 2 * s + m + 1)
                        c = 2 * d + m
                        nc.gpsimd.tensor_tensor(merged[:, c, :], merged[:, c, :], part[m][:, :], ALU.add).then_inc(add_ok, 1)

        @block.tensor
        def _(pe):
            def product(g, d, first=False):
                s, j = 4 * g + d, d % 2
                pe.wait_ge(lo_ok, 2 * s + 2)
                for m in range(2):
                    if not (first and d < 2):
                        pe.wait_ge(part_ok, 2 * s + m - 3)
                    ms = slice(m * P, (m + 1) * P)
                    for c in range(KD):
                        three(nc, p_g[2 * j + m][:, :], (gate_w[j][0][:, c, ms], gate_w[j][1][:, c, ms]),
                              (keep["h_hi"][:, c, :], keep["h_lo"][:, c, :]), c == 0, c == KD - 1)
                    for c in range(CB):
                        ins = three(nc, p_b[2 * j + m][:, :], (br_w[j][0][:, c, ms], br_w[j][1][:, c, ms]),
                                    (y_hi[:, bass.ds(4 * g + c, 1), :], y_lo[:, bass.ds(4 * g + c, 1), :]), c == 0, c == CB - 1)
                    ins.then_inc(mm, 1)

            for d in range(4):
                product(0, d, True)
            with pe.Fori(1, NBR) as g:
                for d in range(4):
                    product(g, d)



def phase_out(nc, a, keep, merged, m_hi, m_lo, space, x2):
    with ExitStack() as stack:
        k = Kit(nc, stack, "out", X2_AT + 16 * KB)
        parts = space[:, :, :].rearrange("p (x a) b -> p x (a b)", x=4).rearrange("p x (k n) -> p x k n", k=KD)
        hi, lo = [parts[:, j] for j in (0, 1)], [parts[:, j] for j in (2, 3)]
        raw = [k.sb(f"raw{j}", [P, KD, BW]) for j in range(2)]
        gate1 = k.sb("gate1", [P, D])
        diag = k.sb("diag", [P, KD, P])
        mixed = [k.sb(f"mixed{j}", [P, BW]) for j in range(2)]
        xn = k.sb("xn", [P, 2, D])
        sq = k.sb("sq", [P, D])
        hf = k.sb("hf", [P, KD, S])
        ssq, fin, root = (k.sb(n, [P, TT]) for n in ("ssq", "fin", "root"))
        acc = [k.ps(f"acc{j}", [P, S]) for j in range(4)]
        p_x = [k.ps(f"x{j}", [P, KD, P]) for j in range(2)]
        names = "w0 w1 x_in diag_ok bc bc_ok m_hi_ok m_lo_ok hi_ok lo_ok mm x2_ok ssq_ok root_ok xn_ok x_t h_ok h_hi_ok h_lo_ok".split()
        sem = {n: k.sem(n) for n in names}
        dve_c = k.count("dve_chain")
        w = a["w_o"][0].rearrange("(k p) n -> p k n", p=P)
        NB = D // BW
        block = stack.enter_context(nc.Block())

        @block.sync
        def _(sp):
            sp.dma_start(x2[:, :, :], a["x"][0].rearrange("(i p) d -> p i d", p=P)).then_inc(sem["x_in"], 16)
            for b in range(NB):
                if b >= 2:
                    sp.wait_ge(sem["lo_ok"], b - 1)
                sp.dma_start(raw[b % 2][:, :, :], w[:, :, b * BW:(b + 1) * BW]).then_inc(sem[f"w{b % 2}"], 16)

        @block.gpsimd
        def _(pool):
            for c in range(KD):
                nc.gpsimd.tensor_scalar(diag[:, c, :], keep["ident"][:, :], keep["mod"][:, 16 + c:17 + c], None, ALU.mult).then_inc(sem["diag_ok"], 1)
            for i in range(TT):
                pool.wait_ge(sem["h_ok"], i + 1)
                ts = slice(i * P, (i + 1) * P)
                nc.gpsimd.tensor_copy(keep["h_hi"][:, :, ts], hf[:, :, ts]).then_inc(sem["h_hi_ok"], 1)

        @block.scalar
        def _(act):
            nc.scalar.activation(m_hi[:, :, :], merged[:, :, :], ACT.Copy).then_inc(sem["m_hi_ok"], 1)
            for b in range(NB):
                act.wait_ge(sem[f"w{b % 2}"], 16 * (b // 2) + 16)
                if b >= 2:
                    act.wait_ge(sem["mm"], TT * (b - 1))
                nc.scalar.activation(hi[b % 2], raw[b % 2][:, :, :], ACT.Copy).then_inc(sem["hi_ok"], 1)
                if b == 0:
                    act.wait_ge(sem["bc"], 1)
                    nc.scalar.activation(gate1[:, :], p_x[0][:, :, :].rearrange("p k n -> p (k n)"), ACT.Copy).then_inc(sem["bc_ok"], 1)
            act.wait_ge(sem["ssq_ok"], 2)
            nc.scalar.activation(root[:, :], root[:, :], ACT.Sqrt, bias=keep["eps"][:, :], scale=DOWN / D).then_inc(sem["root_ok"], 1)
            for i in range(TT):
                act.wait_ge(sem["x_t"], i + 1)
                for c in range(KD):
                    ins = nc.scalar.activation(hf[:, c, i * P:(i + 1) * P], p_x[i % 2][:, c, :], ACT.Identity,
                                               bias=keep["mod"][:, 24 + c:25 + c], scale=keep["scale2"][:, c:c + 1])
                ins.then_inc(sem["h_ok"], 1)

        @block.vector
        def _(dve):
            dve.wait_ge(sem["m_hi_ok"], 1)
            nc.vector.tensor_tensor(m_lo[:, :, :], merged[:, :, :], m_hi[:, :, :].bitcast(F32), ALU.subtract).then_inc(sem["m_lo_ok"], 1)

            def split_lo(b):
                dve.wait_ge(sem["hi_ok"], b + 1)
                nc.vector.tensor_tensor(lo[b % 2], raw[b % 2][:, :, :], hi[b % 2].bitcast(F32), ALU.subtract).then_inc(sem["lo_ok"], 1)

            split_lo(0)
            dve.wait_ge(sem["x_in"], 16)
            dve.wait_ge(sem["bc_ok"], 1)
            for b in range(NB):
                if b + 1 < NB:
                    split_lo(b + 1)
                cs = slice(b * BW, (b + 1) * BW)
                for i in range(TT):
                    dve.wait_ge(sem["mm"], TT * b + i + 1)
                    chained(dve, dve_c, nc.vector.tensor_tensor(mixed[i % 2][:, :], acc[i][:, 0:BW], gate1[:, cs], ALU.mult))
                    nc.vector.tensor_tensor(x2[:, i, cs], x2[:, i, cs], mixed[i % 2][:, :], ALU.add).then_inc(sem["x2_ok"], 1)
            dve.wait_ge(sem["x2_ok"], NB * TT)
            for i in range(TT):
                chained(dve, dve_c, nc.vector.tensor_tensor_reduce(
                    out=sq[:, :], in0=x2[:, i, :], in1=x2[:, i, :], scale=1.0, scalar=0.0,
                    op0=ALU.mult, op1=ALU.add, accum_out=ssq[:, i:i + 1]))
            rstd_dve_in(nc, sem["ssq_ok"], ssq[:, :], fin[:, :], root[:, :])
            dve.wait_ge(sem["root_ok"], 1)
            rstd_dve_out(nc, dve, dve_c, root[:, :], fin[:, :])
            for i in range(TT):
                if i >= 2:
                    dve.wait_ge(sem["x_t"], i - 1)
                nc.vector.tensor_scalar(xn[:, i % 2, :], x2[:, i, :], root[:, i:i + 1], None, ALU.mult).then_inc(sem["xn_ok"], 1)
            for i in range(TT):
                dve.wait_ge(sem["h_hi_ok"], i + 1)
                ts = slice(i * P, (i + 1) * P)
                nc.vector.tensor_tensor(keep["h_lo"][:, :, ts], hf[:, :, ts], keep["h_hi"][:, :, ts].bitcast(F32),
                                        ALU.subtract).then_inc(sem["h_lo_ok"], 1)

        @block.tensor
        def _(pe):
            pe.wait_ge(sem["diag_ok"], KD)
            for c in range(KD):
                ins = nc.tensor.matmul(p_x[0][:, c, :], keep["ones"][:, :], diag[:, c, :], start=True, stop=True)
            ins.then_inc(sem["bc"], 1)
            pe.wait_ge(sem["m_lo_ok"], 1)
            for b in range(NB):
                pe.wait_ge(sem["lo_ok"], b + 1)
                for i in range(TT):
                    if b:
                        pe.wait_ge(sem["x2_ok"], TT * (b - 1) + i + 1)
                    ts = slice(i * P, (i + 1) * P)
                    for c in range(KD):
                        ins = three(nc, acc[i][:, 0:BW], (m_hi[:, c, ts], m_lo[:, c, ts]), (hi[b % 2][:, c, :], lo[b % 2][:, c, :]), c == 0, c == KD - 1)
                    ins.then_inc(sem["mm"], 1)
            for i in range(TT):
                pe.wait_ge(sem["xn_ok"], i + 1)
                if i == 0:
                    pe.wait_ge(sem["bc_ok"], 1)
                if i >= 2:
                    pe.wait_ge(sem["h_ok"], i - 1)
                for c in range(KD):
                    ins = nc.tensor.transpose(p_x[i % 2][:, c, :], xn[:, i % 2, c * P:(c + 1) * P], keep["ident"][:, :])
                ins.then_inc(sem["x_t"], 1)


def phase_query(nc, a, keep, scores):
    with ExitStack() as stack:
        k = Kit(nc, stack, "query", X2_AT + 16 * KB)
        raw = [k.sb(f"raw{j}", [P, KD, BW]) for j in range(2)]
        hi = [k.sb(f"hi{j}", [P, KD, BW], F32R) for j in range(2)]
        lo = [k.sb(f"lo{j}", [P, KD, BW], F32R) for j in range(2)]
        q = [k.sb(f"q{j}", [P, S]) for j in range(2)]
        keys = k.sb("keys", [P, 2, P])
        keys_t = k.sb("keys_t", [P, 2, P])
        acc = [k.ps(f"acc{j}", [P, S]) for j in range(4)]
        p_s = [k.ps(f"s{j}", [P, TT, P]) for j in range(2)]
        p_k = k.ps("k", [P, 2, P])
        names = "w0 w1 keys_in kt kt_ok hi_ok lo_ok mm q_ok sc s_ok".split()
        sem = {n: k.sem(n) for n in names}
        w = a["w_q"][0].rearrange("(k p) n -> p k n", p=P)
        block = stack.enter_context(nc.Block())

        @block.sync
        def _(sp):
            sp.dma_start(keys[:, :, :], a["sub_keys"][0].rearrange("s n d -> n s d")).then_inc(sem["keys_in"], 16)
            for b in range(2):
                sp.dma_start(raw[b][:, :, :], w[:, :, b * BW:(b + 1) * BW]).then_inc(sem[f"w{b}"], 16)
            with sp.Fori(1, PH // 2) as i:
                for j in range(2):
                    sp.wait_ge(sem["lo_ok"], 2 * i + j - 1)
                    sp.dma_start(raw[j][:, :, :], w[:, :, bass.ds((2 * i + j) * BW, BW)]).then_inc(sem[f"w{j}"], 16)

        @block.scalar
        def _(act):
            act.wait_ge(sem["kt"], 1)
            nc.scalar.activation(keys_t[:, :, :], p_k[:, :, :], ACT.Copy).then_inc(sem["kt_ok"], 1)

            def split(b, j, turn, first=False):
                act.wait_ge(sem[f"w{j}"], 16 * turn + 16)
                if not first:
                    act.wait_ge(sem["mm"], 2 * b - 2)
                nc.scalar.activation(hi[j][:, :, :], raw[j][:, :, :], ACT.Copy).then_inc(sem["hi_ok"], 1)

            def queries(b, j, first=False):
                for m in range(2):
                    act.wait_ge(sem["mm"], 2 * b + m + 1)
                    if not first:
                        act.wait_ge(sem["sc"], 2 * b + m - 1)
                    nc.scalar.activation(q[m][:, :], acc[2 * j + m][:, :], ACT.Copy).then_inc(sem["q_ok"], 1)

            split(0, 0, 0, True)
            split(1, 1, 0, True)
            queries(0, 0, True)
            split(2, 0, 1)
            queries(1, 1)
            with act.Fori(1, PH // 2 - 1) as i:
                for j in range(2):
                    split(2 * i + j + 1, 1 - j, i + j)
                    queries(2 * i + j, j)
            split(PH - 1, 1, PH // 2 - 1)
            queries(PH - 2, 0)
            queries(PH - 1, 1)

        @block.vector
        def _(dve):
            def split(b, j):
                dve.wait_ge(sem["hi_ok"], b + 1)
                nc.vector.tensor_tensor(lo[j][:, :, :], raw[j][:, :, :], hi[j][:, :, :].bitcast(F32), ALU.subtract).then_inc(sem["lo_ok"], 1)

            def out(b):
                for m in range(2):
                    dve.wait_ge(sem["sc"], 2 * b + m + 1)
                    nc.vector.tensor_copy(scores[:, :, bass.ds(2 * b + m, 1), :], p_s[m][:, :, :]).then_inc(sem["s_ok"], 1)

            split(0, 0)
            split(1, 1)
            out(0)
            with dve.Fori(1, PH // 2) as i:
                split(2 * i, 0)
                out(2 * i - 1)
                split(2 * i + 1, 1)
                out(2 * i)
            out(PH - 1)

        @block.tensor
        def _(pe):
            pe.wait_ge(sem["keys_in"], 16)
            for x in range(2):
                ins = nc.tensor.transpose(p_k[:, x, :], keys[:, x, :], keep["ident"][:, :])
            ins.then_inc(sem["kt"], 1)
            pe.wait_ge(sem["kt_ok"], 1)

            def product(b, j, first=False):
                pe.wait_ge(sem["lo_ok"], b + 1)
                for m in range(2):
                    if not first:
                        pe.wait_ge(sem["q_ok"], 2 * b + m - 3)
                    ms = slice(m * P, (m + 1) * P)
                    for c in range(KD):
                        ins = three(nc, acc[2 * j + m][:, :], (hi[j][:, c, ms], lo[j][:, c, ms]),
                                    (keep["h_hi"][:, c, :], keep["h_lo"][:, c, :]), c == 0, c == KD - 1)
                    ins.then_inc(sem["mm"], 1)

            def score(b, first=False):
                for m in range(2):
                    pe.wait_ge(sem["q_ok"], 2 * b + m + 1)
                    if not first:
                        pe.wait_ge(sem["s_ok"], 2 * b + m - 1)
                    for i in range(TT):
                        ins = nc.tensor.matmul(p_s[m][:, i, :], q[m][:, i * P:(i + 1) * P], keys_t[:, m, :], start=True, stop=True)
                    ins.then_inc(sem["sc"], 1)

            product(0, 0, True)
            product(1, 1, True)
            score(0, True)
            with pe.Fori(1, PH // 2) as i:
                product(2 * i, 0)
                score(2 * i - 1)
                product(2 * i + 1, 1)
                score(2 * i)
            score(PH - 1)


PLAIN = 64
SOFT_AT = 48
CH = 32
CHUNKS = S // CH
UNROLL = 8


def phase_experts(nc, a, keep, scores, acts, gates):
    with ExitStack() as stack:
        k = Kit(nc, stack, "u", Y_AT + 32 * KB)
        raw = [k.sb(f"raw{j}", [P, 2, D]) for j in range(2)]
        ut = [k.sb(f"ut{j}", [P, KD, P]) for j in range(2)]
        hi = [k.sb(f"hi{j}", [P, KD, P], F32R) for j in range(2)]
        lo = [k.sb(f"lo{j}", [P, KD, P], F32R) for j in range(2)]
        ao = [k.sb(f"ao{j}", [P, 2, S]) for j in range(2)]
        assert k.at <= X2_AT
        k.at = X2_AT + 16 * KB
        gs_at = k.at
        gs = [k.sb(f"gs{j}", [P, P, CH]) for j in range(2)]
        after = k.at
        k.at = gs_at
        sc, sc2, eq, cand = (k.sb(n, [P, 16 * P]) for n in ("sc", "sc2", "eq", "cand"))
        assert k.at <= after
        k.at = after
        top = k.sb("top", [P, 16, TOPK])
        topi = k.sb("topi", [P, 16, TOPK], U32)
        topf = k.sb("topf", [P, 16, TOPK])
        best = k.sb("best", [P, PH, TOPK])
        pos = k.sb("pos", [P, PH * TOPK], U32)
        ab = k.sb("ab", [P, 2, PH * TOPK], U32)
        abf = k.sb("abf", [P, 2, PH * TOPK])
        carrier = k.sb("carrier", [P, 1])
        sel = k.sb("sel", [P, 3, TT, P])
        z = k.sb("z", [P, TT * PH])
        sel_t = k.sb("sel_t", [P, 4, S])
        stage = k.sb("stage", [P, 4, 2 * CH])
        iota_i = k.sb("iota_i", [P, P], U32)
        iota = k.sb("iota", [P, P])
        hot = [k.sb(f"hot{j}", [P, 4, 3, P], F32R) for j in range(2)]
        p_u = [k.ps(f"u{j}", [P, KD, P]) for j in range(2)]
        p_s = [k.ps(f"s{j}", [P, S]) for j in range(2)]
        p_g = [k.ps(f"g{j}", [P, 4, P]) for j in range(2)]
        names = ("iota_ok u_in0 u_in1 tr ut_ok hi_ok lo_ok mm act_ok a_out0 a_out1 step exp_ok sel_ok sel_tr sel_sp hot_ok g_mm g_ok "
                 "g_out0 g_out1").split()
        sem = {n: k.sem(n) for n in names}
        dve_c = k.count("dve_chain")
        block = stack.enter_context(nc.Block())
        u = a["u_experts"][0].rearrange("(b x p) d -> b p x d", x=2, p=P)
        au = acts.rearrange("(b x) p t -> b p x t", x=2)
        TILES = NE // P
        TURNS = (TILES - PLAIN) // UNROLL
        STEPS = 1 + 5 * 2 * PH + 2 + 5 * PH + 2 + 2 + 2 * 3 + 17

        @block.sync
        def _(sp):
            def load(q, j, wait=True):
                if wait:
                    sp.wait_ge(sem["tr"], 2 * q - 2)
                sp.dma_start(raw[j][:, :, :], u[q]).then_inc(sem[f"u_in{j}"], 16)

            def store(q, j):
                sp.wait_ge(sem["act_ok"], 2 * q + 2)
                sp.dma_start(au[q], ao[j][:, :, :]).then_inc(sem[f"a_out{j}"], 16)

            def gates_out(c, j):
                sp.wait_ge(sem["g_ok"], (c + 1) * (CH // 4))
                sp.dma_start(gates[c], gs[j][:, :, :]).then_inc(sem[f"g_out{j}"], 16)

            load(0, 0, False)
            load(1, 1, False)
            with sp.Fori(0, PLAIN // 4) as i:
                for j in range(2):
                    load(2 * i + j + 2, j)
                    store(2 * i + j, j)

            def turn(i, last=False):
                for x in range(UNROLL // 2):
                    q = PLAIN // 2 + i * (UNROLL // 2) + x
                    if not (last and x >= UNROLL // 2 - 2):
                        load(q + 2, x % 2)
                    store(q, x % 2)
                    if x % 2:
                        gates_out(2 * i + x // 2, x // 2)

            with sp.Fori(0, TURNS - 1) as i:
                turn(i)
            turn(TURNS - 1, True)
            for j in range(2):
                sp.wait_ge(sem[f"a_out{j}"], 16 * TILES // 4)
                sp.wait_ge(sem[f"g_out{j}"], 16 * TURNS)

        @block.gpsimd
        def _(pool):
            nc.gpsimd.iota(iota_i[:, :], pattern=[[1, P]], base=0, channel_multiplier=0).then_inc(sem["iota_ok"], 1)
            pool.wait_ge(sem["iota_ok"], 1)
            nc.gpsimd.tensor_copy(iota[:, :], iota_i[:, :]).then_inc(sem["iota_ok"], 1)

            def split_lo(t, j, wait=True):
                pool.wait_ge(sem["hi_ok"], t + 1)
                if wait:
                    pool.wait_ge(sem["mm"], t - 1)
                nc.gpsimd.tensor_tensor(lo[j][:, :, :], ut[j][:, :, :], hi[j][:, :, :].bitcast(F32), ALU.subtract).then_inc(sem["lo_ok"], 1)

            split_lo(0, 0, False)
            split_lo(1, 1, False)
            with pool.Fori(1, TILES // 2) as i:
                for j in range(2):
                    split_lo(2 * i + j, j)

        @block.scalar
        def _(act):
            def take(t, j, wait=True):
                act.wait_ge(sem["tr"], t + 1)
                if wait:
                    act.wait_ge(sem["lo_ok"], t - 1)
                nc.scalar.activation(ut[j][:, :, :], p_u[j][:, :, :], ACT.Copy).then_inc(sem["ut_ok"], 1)
                if wait:
                    act.wait_ge(sem["mm"], t - 1)
                nc.scalar.activation(hi[j][:, :, :], p_u[j][:, :, :], ACT.Copy).then_inc(sem["hi_ok"], 1)

            def gelu(t, j, first=False):
                act.wait_ge(sem["mm"], t + 1)
                if not first and j % 2 == 0:
                    act.wait_ge(sem[f"a_out{j // 2}"], 16 * (t // 4) if isinstance(t, int) else (t - j) * 4)
                nc.scalar.activation(ao[j // 2][:, j % 2, :], p_s[j % 2][:, :], ACT.Gelu).then_inc(sem["act_ok"], 1)

            def plain(i, first=False):
                for j in range(4):
                    t = 4 * i + j
                    take(t + 1, (j + 1) % 2, not (first and j == 0))
                    gelu(t, j, first)

            take(0, 0, False)
            plain(0, True)
            with act.Fori(1, SOFT_AT // 4) as i:
                plain(i)
            act.wait_ge(sem["step"], TT * STEPS)
            nc.scalar.activation(sel[:, 2, :, :], sel[:, 2, :, :], ACT.Exp).then_inc(sem["exp_ok"], 1)
            with act.Fori(SOFT_AT // 4, PLAIN // 4) as i:
                plain(i)

            def turn(i, first=False, last=False):
                for x in range(UNROLL):
                    t = PLAIN + i * UNROLL + x
                    j = x % 4
                    if not (last and x == UNROLL - 1):
                        take(t + 1, (x + 1) % 2)
                    act.wait_ge(sem["mm"], t + 1)
                    if x % 2 == 0:
                        act.wait_ge(sem[f"a_out{j // 2}"], (PLAIN + i * UNROLL + x - j) * 4)
                    nc.scalar.activation(ao[j // 2][:, j % 2, :], p_s[x % 2][:, :], ACT.Gelu).then_inc(sem["act_ok"], 1)
                    chunk = x // 4
                    if x % 4 == 0 and not first:
                        act.wait_ge(sem[f"g_out{chunk}"], 16 * i)
                    for y in range(2):
                        n = 2 * x + y
                        act.wait_ge(sem["g_mm"], 2 * UNROLL * i + n + 1)
                        at = (n % 8) * 4
                        nc.scalar.activation(gs[chunk][:, :, at:at + 4].rearrange("p i t -> p t i"), p_g[y][:, :, :], ACT.Copy).then_inc(sem["g_ok"], 1)

            turn(0, True)
            with act.Fori(1, TURNS - 1) as i:
                turn(i)
            turn(TURNS - 1, False, True)

        @block.vector
        def _(dve):
            slots = [P, PH, TOPK, TOPK]
            steps = Count(sem["step"])

            def fence(i):
                dve.wait_ge(steps.sem, i * STEPS + steps.n)
                steps.inc(nc.vector.memset(carrier[:, :], 0.0))

            def largest(i, n, w, src, tmp, vals, index):
                for x in range(n):
                    steps.inc(nc.vector.max(vals[:, x, 0:8], src[:, x * w:(x + 1) * w]))
                fence(i)
                for x in range(n):
                    steps.inc(nc.vector.max_index(index[:, x, 0:8], vals[:, x, 0:8], src[:, x * w:(x + 1) * w]))
                    steps.inc(nc.vector.match_replace(tmp[:, x * w:(x + 1) * w], vals[:, x, 0:8], src[:, x * w:(x + 1) * w], -FLT_MAX))
                fence(i)
                for x in range(n):
                    steps.inc(nc.vector.max(vals[:, x, 8:16], tmp[:, x * w:(x + 1) * w]))
                fence(i)
                for x in range(n):
                    steps.inc(nc.vector.max_index(index[:, x, 8:16], vals[:, x, 8:16], tmp[:, x * w:(x + 1) * w]))
                fence(i)

            dve.wait_ge(sem["iota_ok"], 2)
            with dve.Fori(0, TT) as i:
                steps.inc(nc.vector.tensor_copy(sc[:, :].rearrange("p (o h n) -> p o h n", o=1, h=16), scores[:, bass.ds(i, 1), :, :]))
                fence(i)
                largest(i, 2 * PH, P, sc, sc2, top, topi)
                steps.inc(nc.vector.tensor_copy(topf[:, :, :], topi[:, :, :]))
                half = top[:, :, :].rearrange("p (h s) k -> p s h k", s=2)
                first = half[:, 0].rearrange("p h (k o) -> p h k o", o=1).broadcast_to(slots)
                second = half[:, 1].rearrange("p h (o k) -> p h o k", o=1).broadcast_to(slots)
                steps.inc(nc.vector.tensor_tensor(cand[:, :].rearrange("p (h a b) -> p h a b", h=PH, a=TOPK), first, second, ALU.add))
                fence(i)
                largest(i, PH, TOPK * TOPK, cand, sc2, best, pos[:, :].rearrange("p (h k) -> p h k", h=PH))
                steps.inc(nc.vector.tensor_scalar(ab[:, 0, :], pos[:, :], 4, None, ALU.logical_shift_right))
                steps.inc(nc.vector.tensor_scalar(ab[:, 1, :], pos[:, :], 15, None, ALU.bitwise_and))
                fence(i)
                steps.inc(nc.vector.tensor_copy(abf[:, :, :], ab[:, :, :]))
                steps.inc(nc.vector.tensor_tensor(sel[:, 2, bass.ds(i, 1), :].rearrange("p o (h k) -> p (o h) k", h=PH), best[:, :, :],
                                                  best[:, :, 0:1].broadcast_to([P, PH, TOPK]), ALU.subtract))
                fence(i)
                for s, e_flat in enumerate((eq, sc)):
                    e = e_flat[:, :].rearrange("p (h k a) -> p h k a", h=PH, k=TOPK)
                    rank = abf[:, s, :].rearrange("p (h k o) -> p h k o", h=PH, o=1).broadcast_to(slots)
                    upto = iota[:, 0:TOPK].rearrange("p (x y a) -> p x y a", x=1, y=1).broadcast_to(slots)
                    key = topf[:, :, :].rearrange("p (h s) k -> p s h k", s=2)[:, s].rearrange("p h (o a) -> p h o a", o=1).broadcast_to(slots)
                    steps.inc(nc.vector.tensor_tensor(e, rank, upto, ALU.is_equal))
                    fence(i)
                    steps.inc(nc.vector.tensor_tensor(e, e, key, ALU.mult))
                    fence(i)
                    steps.inc(nc.vector.reduce_sum(sel[:, s, bass.ds(i, 1), :].rearrange("p o (n q) -> p (o n) q", q=1), e_flat[:, :].rearrange("p (n a) -> p n a", a=TOPK), AX.X))
                fence(i)
            assert steps.n == STEPS
            dve.wait_ge(sem["exp_ok"], 1)
            ev = sel[:, 2, :, :].rearrange("p i (h k) -> p (i h) k", k=TOPK)
            chained(dve, dve_c, nc.vector.reduce_sum(z[:, :], ev, AX.X))
            chained(dve, dve_c, nc.vector.reciprocal(z[:, :], z[:, :]))
            nc.vector.tensor_tensor(ev, ev, z[:, :].rearrange("p (x o) -> p x o", o=1).broadcast_to([P, TT * PH, TOPK]),
                                    ALU.mult).then_inc(sem["sel_ok"], 1)
            for s in range(3):
                dve.wait_ge(sem["sel_tr"], s + 1)
                out = sel_t[:, s, :] if s < 2 else hot[0][:, :, :, :].rearrange("p a b c -> p (a b c)")[:, 0:S]
                nc.vector.tensor_copy(out, p_g[s % 2][:, :, :].rearrange("p i n -> p (i n)")).then_inc(sem["sel_sp"], 1)
            dve.wait_ge(sem["sel_sp"], 3)
            chained(dve, dve_c, nc.vector.tensor_copy(sel_t[:, 2, :], hot[0][:, :, :, :].rearrange("p a b c -> p (a b c)")[:, 0:S].bitcast(F32)))
            nc.vector.tensor_tensor(sel_t[:, 3, :], p_g[0][:, :, :].rearrange("p i n -> p (i n)"), sel_t[:, 2, :], ALU.subtract).then_inc(sem["sel_sp"], 1)
            dve.wait_ge(sem["sel_sp"], 4)

            def turn(i, first=False):
                if not first:
                    dve.wait_ge(sem["hot_ok"], 2 * UNROLL * i)
                nc.vector.tensor_copy(stage[:, :, :], sel_t[:, :, bass.ds(i * 2 * CH, 2 * CH)]).then_inc(sem["sel_sp"], 1)
                dve.wait_ge(sem["sel_sp"], i + 5)
                for n in range(2 * UNROLL):
                    if not (first and n < 2):
                        dve.wait_ge(sem["g_mm"], 2 * UNROLL * i + n - 1)
                    for y in range(4):
                        t = n * 4 + y
                        h = hot[n % 2]
                        nc.vector.tensor_scalar(h[:, y, 0, :], iota[:, :], stage[:, 1, t:t + 1], None, ALU.is_equal)
                        for part in range(2):
                            ins = nc.vector.tensor_scalar(h[:, y, 1 + part, :], iota[:, :], stage[:, 0, t:t + 1], stage[:, 2 + part, t:t + 1],
                                                          ALU.is_equal, ALU.mult)
                    ins.then_inc(sem["hot_ok"], 1)

            turn(0, True)
            with dve.Fori(1, TURNS) as i:
                turn(i)

        @block.tensor
        def _(pe):
            ident = keep["ident"][:, :]

            def transposes(t, j, wait=True):
                if j % 2 == 0:
                    pe.wait_ge(sem[f"u_in{j // 2}"], (t - j) * 4 + 16)
                if wait:
                    pe.wait_ge(sem["hi_ok"], t - 1)
                for c in range(KD):
                    ins = nc.tensor.transpose(p_u[j % 2][:, c, :], raw[j // 2][:, j % 2, c * P:(c + 1) * P], ident)
                ins.then_inc(sem["tr"], 1)

            def product(t, j, wait=True):
                pe.wait_ge(sem["lo_ok"], t + 1)
                if wait:
                    pe.wait_ge(sem["act_ok"], t - 1)
                for c in range(KD):
                    ins = three(nc, p_s[j % 2][:, :], (hi[j % 2][:, c, :], lo[j % 2][:, c, :]),
                                (keep["h_hi"][:, c, :], keep["h_lo"][:, c, :]), c == 0, c == KD - 1)
                ins.then_inc(sem["mm"], 1)

            def plain(i, first=False):
                for j in range(4):
                    t = 4 * i + j
                    transposes(t + 1, (j + 1) % 4, not (first and j == 0))
                    product(t, j, not (first and j < 2))

            transposes(0, 0, False)
            plain(0, True)
            with pe.Fori(1, PLAIN // 4) as i:
                plain(i)
            pe.wait_ge(sem["sel_ok"], 1)
            for s in range(3):
                if s == 2:
                    pe.wait_ge(sem["sel_sp"], 1)
                for i in range(TT):
                    ins = nc.tensor.transpose(p_g[s % 2][:, i, :], sel[:, s, i, :], ident)
                ins.then_inc(sem["sel_tr"], 1)

            def turn(i, first=False, last=False):
                for x in range(UNROLL):
                    t = PLAIN + i * UNROLL + x
                    if not (last and x == UNROLL - 1):
                        transposes(t + 1, (x + 1) % 4)
                    product(t, x)
                    for y in range(2):
                        n = 2 * UNROLL * i + 2 * x + y
                        pe.wait_ge(sem["hot_ok"], n + 1)
                        if not (first and x == 0):
                            pe.wait_ge(sem["g_ok"], n - 1)
                        for b in range(4):
                            h = hot[y]
                            nc.tensor.matmul(p_g[y][:, b, :], h[:, b, 0, :], h[:, b, 1, :], start=True, stop=False)
                            ins = nc.tensor.matmul(p_g[y][:, b, :], h[:, b, 0, :], h[:, b, 2, :], start=False, stop=True)
                        ins.then_inc(sem["g_mm"], 1)

            pe.wait_ge(sem["sel_sp"], 4)
            turn(0, True)
            with pe.Fori(1, TURNS - 1) as i:
                turn(i)
            turn(TURNS - 1, False, True)


GT = 4


def phase_combine(nc, a, keep, acts, gates, x2, out):
    with ExitStack() as stack:
        k = Kit(nc, stack, "v", LOW)
        v = k.sb("v", [P, GT, D])
        v_hi = [k.sb(f"v_hi{j}", [P, GT, D], F32R) for j in range(2)]
        v_lo = [k.sb(f"v_lo{j}", [P, GT, D], F32R) for j in range(2)]
        at = [k.sb(f"at{j}", [P, GT, S]) for j in range(2)]
        assert k.at <= X2_AT
        k.at = X2_AT + 16 * KB
        gt = [k.sb(f"gt{j}", [P, CHUNKS, GT * CH]) for j in range(2)]
        w_hi = [k.sb(f"w_hi{j}", [P, GT, S], F32R) for j in range(2)]
        w_lo = [k.sb(f"w_lo{j}", [P, GT, S], F32R) for j in range(2)]
        acc = k.sb("acc", [P, TT, D])
        gate2 = k.sb("gate2", [P, D])
        g_fin = k.sb("g_fin", [P, D])
        ssq, fin, root = (k.sb(n, [P, TT]) for n in ("ssq", "fin", "root"))
        diag = at[0][:, 0:2, :].rearrange("p a (b n) -> p (a b) n", n=P)
        p_o = [k.ps(f"o{j}", [P, S]) for j in range(8)]
        names = ("v_in a_in0 a_in1 g_in0 g_in1 gf_in diag_ok bc bc_ok zeroed vhi_ok vlo_ok w_ok whi_ok wlo_ok mm add_ok "
                 "ssq_ok root_ok y_ok out_ok").split()
        sem = {n: k.sem(n) for n in names}
        dve_c = k.count("dve_chain")
        block = stack.enter_context(nc.Block())
        vv = a["v_experts"][0].rearrange("(g x p) d -> g p x d", x=GT, p=P)
        av = acts.rearrange("(g x) p t -> g p x t", x=GT)
        gv = gates.rearrange("c j (g x) t -> g j c (x t)", x=GT)
        NG = NE // P // GT

        @block.sync
        def _(sp):
            def load(g, j, first=False):
                if not first:
                    sp.wait_ge(sem["vlo_ok"], g)
                sp.dma_start(v[:, :, :], vv[g]).then_inc(sem["v_in"], 16)
                if not first:
                    sp.wait_ge(sem["wlo_ok"], g - 1)
                sp.dma_start(at[j][:, :, :], av[g]).then_inc(sem[f"a_in{j}"], 16)
                sp.dma_start(gt[j][:, :, :], gv[g]).then_inc(sem[f"g_in{j}"], 16)

            sp.wait_ge(sem["bc"], 1)
            load(0, 0, True)
            sp.dma_start(g_fin[:, :], a["g_final"].rearrange("(o d) -> o d", o=1).to_broadcast([P, D])).then_inc(sem["gf_in"], 16)
            sp.wait_ge(sem["vlo_ok"], 1)
            sp.dma_start(v[:, :, :], vv[1]).then_inc(sem["v_in"], 16)
            sp.dma_start(at[1][:, :, :], av[1]).then_inc(sem["a_in1"], 16)
            sp.dma_start(gt[1][:, :, :], gv[1]).then_inc(sem["g_in1"], 16)
            with sp.Fori(1, NG // 2) as i:
                for j in range(2):
                    load(2 * i + j, j)
            ov = out[0].rearrange("(i p) d -> p i d", p=P)
            for i in range(TT):
                sp.wait_ge(sem["y_ok"], i + 1)
                sp.dma_start(ov[:, i, :], acc[:, i, :]).then_inc(sem["out_ok"], 16)
            sp.wait_ge(sem["out_ok"], 16 * TT)

        @block.gpsimd
        def _(pool):
            for c in range(KD):
                nc.gpsimd.tensor_scalar(diag[:, c, :], keep["ident"][:, :], keep["mod"][:, 40 + c:41 + c], None, ALU.mult).then_inc(sem["diag_ok"], 1)
            nc.gpsimd.memset(acc[:, :, :], 0.0).then_inc(sem["zeroed"], 1)

            def weigh(i, j):
                pool.wait_ge(sem[f"a_in{j}"], 16 * i + 16)
                pool.wait_ge(sem[f"g_in{j}"], 16 * i + 16)
                x = at[j][:, :, :].rearrange("p x (c t) -> p x c t", t=CH)
                nc.gpsimd.tensor_tensor(x, x, gt[j][:, :, :].rearrange("p c (x t) -> p x c t", t=CH), ALU.mult).then_inc(sem["w_ok"], 1)

            with pool.Fori(0, NG // 2) as i:
                for j in range(2):
                    weigh(i, j)

        @block.scalar
        def _(act):
            act.wait_ge(sem["bc"], 1)
            for j in range(2):
                nc.scalar.activation(gate2[:, j * S:(j + 1) * S], p_o[j][:, :], ACT.Copy).then_inc(sem["bc_ok"], 1)

            def split(g, j, first=False):
                act.wait_ge(sem["v_in"], 16 * g + 16)
                if not first:
                    act.wait_ge(sem["mm"], 8 * g - 8)
                nc.scalar.activation(v_hi[j][:, :, :], v[:, :, :], ACT.Copy).then_inc(sem["vhi_ok"], 1)
                act.wait_ge(sem["w_ok"], g + 1)
                nc.scalar.activation(w_hi[j][:, :, :], at[j][:, :, :], ACT.Copy).then_inc(sem["whi_ok"], 1)

            split(0, 0, True)
            split(1, 1, True)
            with act.Fori(1, NG // 2) as i:
                for j in range(2):
                    split(2 * i + j, j)
            act.wait_ge(sem["ssq_ok"], 2)
            nc.scalar.activation(root[:, :], root[:, :], ACT.Sqrt, bias=keep["eps"][:, :], scale=DOWN / D).then_inc(sem["root_ok"], 1)

        @block.vector
        def _(dve):
            def split(g, j):
                dve.wait_ge(sem["vhi_ok"], g + 1)
                nc.vector.tensor_tensor(v_lo[j][:, :, :], v[:, :, :], v_hi[j][:, :, :].bitcast(F32), ALU.subtract).then_inc(sem["vlo_ok"], 1)
                dve.wait_ge(sem["whi_ok"], g + 1)
                nc.vector.tensor_tensor(w_lo[j][:, :, :], at[j][:, :, :], w_hi[j][:, :, :].bitcast(F32), ALU.subtract).then_inc(sem["wlo_ok"], 1)

            def add(g, banks, first=False):
                for n in banks:
                    dve.wait_ge(sem["mm"], 8 * g + n + 1)
                    if not first:
                        dve.wait_ge(sem["add_ok"], 8 * g + n - 7)
                    o = acc[:, n // 2, n % 2 * S:(n % 2 + 1) * S]
                    nc.vector.tensor_tensor(o, o, p_o[n][:, :], ALU.add).then_inc(sem["add_ok"], 1)

            split(0, 0)
            dve.wait_ge(sem["zeroed"], 1)
            split(1, 1)
            add(0, range(8), True)
            split(2, 0)
            add(1, range(8))
            with dve.Fori(1, NG // 2 - 1) as i:
                split(2 * i + 1, 1)
                add(2 * i, range(8))
                split(2 * i + 2, 0)
                add(2 * i + 1, range(8))
            split(NG - 1, 1)
            add(NG - 2, range(8))
            add(NG - 1, range(8))
            dve.wait_ge(sem["add_ok"], 8 * NG)
            dve.wait_ge(sem["bc_ok"], 2)
            sq = at[0][:, 0:2, :].rearrange("p a b -> p (a b)")
            for i in range(TT):
                chained(dve, dve_c, nc.vector.tensor_tensor(acc[:, i, :], acc[:, i, :], gate2[:, :], ALU.mult))
                chained(dve, dve_c, nc.vector.tensor_tensor(acc[:, i, :], acc[:, i, :], x2[:, i, :], ALU.add))
                chained(dve, dve_c, nc.vector.tensor_tensor_reduce(
                    out=sq, in0=acc[:, i, :], in1=acc[:, i, :], scale=1.0, scalar=0.0,
                    op0=ALU.mult, op1=ALU.add, accum_out=ssq[:, i:i + 1]))
            rstd_dve_in(nc, sem["ssq_ok"], ssq[:, :], fin[:, :], root[:, :])
            dve.wait_ge(sem["root_ok"], 1)
            rstd_dve_out(nc, dve, dve_c, root[:, :], fin[:, :])
            dve.wait_ge(sem["gf_in"], 16)
            for i in range(TT):
                nc.vector.scalar_tensor_tensor(acc[:, i, :], acc[:, i, :], root[:, i:i + 1], g_fin[:, :], ALU.mult, ALU.mult).then_inc(sem["y_ok"], 1)

        @block.tensor
        def _(pe):
            pe.wait_ge(sem["diag_ok"], KD)
            for c in range(KD):
                ins = nc.tensor.matmul(p_o[c // 4][:, c % 4 * P:(c % 4 + 1) * P], keep["ones"][:, :], diag[:, c, :], start=True, stop=True)
            ins.then_inc(sem["bc"], 1)
            pe.wait_ge(sem["bc_ok"], 2)

            def group(g, j, first=False):
                pe.wait_ge(sem["vlo_ok"], g + 1)
                pe.wait_ge(sem["wlo_ok"], g + 1)
                for n in range(8):
                    if not first:
                        pe.wait_ge(sem["add_ok"], 8 * g + n - 7)
                    ts, cs = slice(n // 2 * P, (n // 2 + 1) * P), slice(n % 2 * S, (n % 2 + 1) * S)
                    for x in range(GT):
                        ins = three(nc, p_o[n][:, :], (w_hi[j][:, x, ts], w_lo[j][:, x, ts]), (v_hi[j][:, x, cs], v_lo[j][:, x, cs]), x == 0, x == GT - 1)
                    ins.then_inc(sem["mm"], 1)

            group(0, 0, True)
            group(1, 1)
            with pe.Fori(1, NG // 2) as i:
                for j in range(2):
                    group(2 * i + j, j)


def program(nc, a, out, stop=99):
    with ExitStack() as top:
        k = Kit(nc, top, "keep", KEEP_AT)
        keep = {n: k.sb(n, shape) for n, shape in (
            ("ident", [P, P]), ("ones", [P, P]), ("invn", [P, 16]), ("eps", [P, 1]), ("cols", [P, V_ROWS]), ("mod", [P, 48]),
            ("scale1", [P, KD]), ("scale2", [P, KD]), ("neglam", [P, 1]), ("sinks", [P, 8]))}
        assert k.at <= LOW
        kh = Kit(nc, top, "h", H_AT)
        keep["h_hi"], keep["h_lo"] = (kh.sb(n, [P, KD, S], F32R) for n in ("hi", "lo"))
        phase_condition(nc, a, keep)
        if stop <= 1:
            return
        ky = Kit(nc, top, "y", Y_AT)
        y_hi, y_lo = (ky.sb(n, [P, NBR * CB, S], F32R) for n in ("hi", "lo"))
        xt = Kit(nc, top, "mixin", XT_AT).sb("xt", [P, 2 * MIX_BLOCKS, S])
        phase_project(nc, a, keep, xt, y_hi)
        if stop <= 2:
            return
        phase_mix(nc, a, keep, xt, *(y[:, :, :].rearrange("p (g c) t -> p g c t", c=CB) for y in (y_hi, y_lo)))
        if stop <= 3:
            return
        merged = Kit(nc, top, "y", MERGED_AT).sb("merged", [P, KD, S])
        phase_gate(nc, a, keep, y_hi, y_lo, merged)
        if stop <= 4:
            return
        x2 = Kit(nc, top, "x2", X2_AT).sb("x2", [P, TT, D])
        phase_out(nc, a, keep, merged, y_hi[:, 0:KD, :], y_hi[:, KD:, :], y_lo, x2)
        if stop <= 5:
            return
        scores = Kit(nc, top, "peer", Y_AT).sb("scores", [P, TT, 2 * PH, NK])
        phase_query(nc, a, keep, scores)
        if stop <= 6:
            return
        acts = nc.dram_tensor("expert_acts", [NE // P, P, S], F32, kind="Internal").ap()
        gates = nc.dram_tensor("expert_gates", [CHUNKS, P, P, CH], F32, kind="Internal").ap()
        phase_experts(nc, a, keep, scores, acts, gates)
        if stop <= 7:
            return
        phase_combine(nc, a, keep, acts, gates, x2, out)


_INS = ["x", "c", "w_ada", "b_ada", "g_norm1", "w_in", "lam_q1", "lam_k1", "lam_q2", "lam_k2", "g_subln", "conv_w", "w_pool",
        "pool_scale", "sinks", "w_branch", "w_o", "g_norm2", "w_q", "sub_keys", "u_experts", "v_experts", "g_final"]


def kernel(**inputs):
    import numpy as _np
    import concourse.bacc as _bacc
    from concourse import mybir as _mybir
    from concourse.bass_utils import run_bass_kernel_spmd as _run

    nc = _bacc.Bacc("TRN2", target_bir_lowering=False, num_devices=1)
    arrays, args = {}, {}
    for name in _INS:
        arr = _np.ascontiguousarray(inputs[name])
        arrays[f"in_{name}_dram"] = arr
        args[name] = nc.dram_tensor(f"in_{name}_dram", arr.shape, _mybir.dt.from_np(arr.dtype), kind="ExternalInput").ap()
    out = nc.dram_tensor("out_0_dram", (1, S, D), F32, kind="ExternalOutput").ap()
    program(nc, args, out)
    r = _run(nc, [arrays], core_ids=[0])
    return r.results[0]["out_0_dram"]
```

```python
from contextlib import ExitStack

import concourse.bass as bass
from concourse import mybir

P = 128
F32 = mybir.dt.float32
F32R = mybir.dt.float32r
BF16 = mybir.dt.bfloat16
U32 = mybir.dt.uint32
ALU = mybir.AluOpType
ACT = mybir.ActivationFunctionType
AX = mybir.AxisListType

EPS = 1e-6
NEG = -1e30
FLT_MAX = 3.4028234663852886e38
DOWN = 2.0 ** -60
UP = 2.0 ** -30
O_BOUND = 2.0 ** 66
SQ_DOWN = 2.0 ** -16
LAM_INIT = 0.2

D = 1024
S = 512
TT = S // P
KD = D // P
BW = 256
HALF = D // 2
CB = HALF // P
NBR = 4
HD = 64
HA = 4
IN_COLS = 8448
MIX_BLOCKS = 17
GATE_BLOCKS = 16
ADA_BLOCKS = 6 * D // BW
PH = 8
NK = 128
TOPK = 16
NE = NK * NK

V_C, V_ADA, V_G1, V_G2, V_CONV, V_POOL, V_SUB = 0, 8, 56, 64, 72, 84, 88
V_ROWS = 89
M_AQ, M_AK, M_AV, M_BB, M_BC, M_BX, M_CZ, M_DQ, M_DK, M_DV = 0, 4, 8, 12, 16, 20, 24, 28, 32, 33


class Count:

    def __init__(self, sem):
        self.sem = sem
        self.n = 0

    def inc(self, ins, by=1):
        ins.then_inc(self.sem, by)
        self.n += by
        return self.n


KB = 1024
KEEP_AT = 16512
LOW = KEEP_AT + 2 * KB
H_AT, Y_AT, XT_AT, MERGED_AT, X2_AT = LOW, LOW + 32 * KB, LOW + 96 * KB, LOW + 96 * KB, LOW + 112 * KB


class Kit:

    def __init__(self, nc, stack, tag, at):
        self.nc, self.stack, self.tag, self.at = nc, stack, tag, at

    def sb(self, name, shape, dt=F32):
        size = 2 if dt == BF16 else 4
        for n in shape[1:]:
            size *= n
        t = self.nc.alloc_sbuf_tensor_at(f"{self.tag}_{name}", shape, dt, offset=self.at)
        self.at += -(-size // 32) * 32
        return t

    def ps(self, name, shape, dt=F32):
        return self.stack.enter_context(self.nc.psum_tensor(f"{self.tag}_{name}", shape, dt))

    def sem(self, name):
        return self.stack.enter_context(self.nc.semaphore(f"{self.tag}_{name}"))

    def count(self, name):
        return Count(self.sem(name))


def three(nc, out, w, x, first, last):
    nc.tensor.matmul(out, w[0], x[0], start=first, stop=False)
    nc.tensor.matmul(out, w[0], x[1], start=False, stop=False)
    return nc.tensor.matmul(out, w[1], x[0], start=False, stop=last)


def chained(eng, sig, ins):
    eng.wait_ge(sig.sem, sig.inc(ins))


def rstd_dve_in(nc, done, ssq, fin, out, most=FLT_MAX):
    nc.vector.tensor_scalar(fin, ssq, most, None, ALU.is_le).then_inc(done, 1)
    nc.vector.tensor_scalar(out, ssq, most, None, ALU.min).then_inc(done, 1)


def rstd_dve_out(nc, dve, sig, root, fin):
    chained(dve, sig, nc.vector.reciprocal(root, root))
    chained(dve, sig, nc.vector.scalar_tensor_tensor(root, root, UP, fin, ALU.mult, ALU.mult))


def model_order(x, q=4):
    return x.rearrange("p (q m r) -> p q m r", q=q, m=KD)


def h2_order(x):
    return x.rearrange("p (m q r) -> p q m r", q=4, m=KD)


def modulate(nc, out, coef, x, bank, ready, engine):
    scale, shift = coef
    for c in range(4 * bank, 4 * bank + 4):
        if engine == "act":
            ins = nc.scalar.activation(out[:, c, :], x[:, c, :], ACT.Identity, bias=shift[:, c:c + 1], scale=scale[:, c:c + 1])
        else:
            ins = nc.vector.tensor_scalar(out[:, c, :], x[:, c, :], scale[:, c:c + 1], shift[:, c:c + 1], ALU.mult, ALU.add)
        ins.then_inc(ready, 1)


def phase_condition(nc, a, keep):
    with ExitStack() as stack:
        k = Kit(nc, stack, "cond", Y_AT)
        ring = [k.sb(f"ada{j}", [P, KD, S]) for j in range(4)]
        rows = k.sb("rows", [P, P])
        lamv = k.sb("lamv", [P, 4, HD])
        lamp = k.sb("lamp", [P, 2, HD])
        lams = k.sb("lams", [P, 4])
        x = k.sb("x", [P, TT, D])
        xn = k.sb("xn", [P, TT, D])
        sq = k.sb("sq", [P, D])
        ssq, fin, root = (k.sb(n, [P, TT]) for n in ("ssq", "fin", "root"))
        acc = k.sb("acc", [P, 2, D])
        hf = k.sb("hf", [P, KD, S])
        p_cols = k.ps("cols", [P, 512])
        p_mod = k.ps("mod", [P, 512])
        p_x = [k.ps(f"x{j}", [P, KD, P]) for j in range(2)]

        rows_in, lam_in, x_in = k.sem("rows_in"), k.sem("lam_in"), k.sem("x_in")
        ada_in = [k.sem(f"ada_in{j}") for j in range(4)]
        const, cols_t, cols_ok, sil_ok, mod_mm = (k.sem(n) for n in ("const", "cols_t", "cols_ok", "sil_ok", "mod_mm"))
        lam_e, ssq_ok, root_ok, xn_ok, x_t, h_ok, hi_ok = (
            k.sem(n) for n in ("lam_e", "ssq_ok", "root_ok", "xn_ok", "x_t", "h_ok", "hi_ok"))
        coef_ok, lam_s, v_ok, acc_ok, hv_ok = (k.sem(n) for n in ("coef_ok", "lam_s", "v_ok", "acc_ok", "hv_ok"))
        dve_c, pool_c, acc_c = k.count("dve_chain"), k.count("pool_chain"), k.count("acc_chain")
        ada = a["w_ada"][0].rearrange("(k p) n -> p k n", p=P)
        coef = (keep["scale1"], keep["mod"])
        block = stack.enter_context(nc.Block())
        vectors = []
        r = 0
        for name, src in (("c", a["c"]), ("b_ada", a["b_ada"]), ("g_norm1", a["g_norm1"]), ("g_norm2", a["g_norm2"]),
                          ("conv_w", a["conv_w"].rearrange("l j n -> l (j n)")), ("pool_scale", a["pool_scale"]),
                          ("g_subln", a["g_subln"])):
            n = src.shape[1] // P
            plain = 2 * KD if name == "b_ada" else 0 if name == "g_norm2" else n
            if plain:
                vectors.append((rows[r:r + plain, :], src[0, 0:plain * P].rearrange("(m p) -> m p", p=P)))
            for m in range(plain, n, KD):
                vectors.append((rows[r + m:r + m + KD, :].rearrange("m (q r) -> m q r", q=4),
                                src[0, m * P:(m + KD) * P].rearrange("(q m r) -> m q r", q=4, m=KD)))
            r += n

        @block.sync
        def _(sp):
            sp.wait_ge(const, 5)
            for dst, src in vectors:
                sp.dma_start(dst, src).then_inc(rows_in, 16)
            sp.dma_start(x[:, :, :], a["x"][0].rearrange("(i p) d -> p i d", p=P)).then_inc(x_in, 16)
            for j in range(4):
                sp.dma_start(ring[j][:, :, :], ada[:, :, j * S:(j + 1) * S]).then_inc(ada_in[j], 16)
            for n, name in enumerate(("lam_q1", "lam_k1", "lam_q2", "lam_k2")):
                sp.dma_start(lamv[:, n, :], a[name].to_broadcast([P, HD])).then_inc(lam_in, 16)
            sp.dma_start(keep["sinks"][:, :], a["sinks"].to_broadcast([P, 8])).then_inc(lam_in, 16)
            sp.wait_ge(lam_in, 80)

        @block.gpsimd
        def _(pool):
            nc.gpsimd.memset(rows[:, :], 0.0).then_inc(const, 1)
            nc.gpsimd.memset(keep["eps"][:, :], EPS * DOWN).then_inc(const, 1)
            nc.gpsimd.memset(keep["ones"][:, :], 1.0).then_inc(const, 1)
            nc.gpsimd.memset(keep["invn"][:, :], 0.0).then_inc(const, 1)
            chained(pool, pool_c, nc.gpsimd.memset(keep["ident"][:, :], 0.0))
            nc.gpsimd.affine_select(out=keep["ident"][:, :], in_=keep["ident"][:, :], compare_op=ALU.not_equal, fill=1.0,
                                    base=0, pattern=[[-1, P]], channel_multiplier=1).then_inc(const, 1)

        @block.scalar
        def _(act):
            act.wait_ge(cols_ok, 1)
            nc.scalar.activation(keep["csil"][:, :], keep["cols"][:, V_C:V_C + KD], ACT.Silu).then_inc(sil_ok, 1)
            act.wait_ge(ssq_ok, 2)
            nc.scalar.activation(root[:, :], root[:, :], ACT.Sqrt, bias=keep["eps"][:, :], scale=DOWN / D).then_inc(root_ok, 1)
            act.wait_ge(lam_s, 2)
            nc.scalar.activation(lams[:, 2:4], lams[:, 0:2], ACT.Exp).then_inc(lam_e, 1)
            act.wait_ge(coef_ok, 2)
            for i in range(TT):
                act.wait_ge(x_t, i + 1)
                ts = slice(i * P, (i + 1) * P)
                modulate(nc, hf[:, :, ts], coef, p_x[i % 2], 0, h_ok, "act")
                act.wait_ge(h_ok, 4 * i + 4)
                act.wait_ge(hv_ok, 4 * i + 4)
                nc.scalar.activation(keep["h_hi"][:, :, ts], hf[:, :, ts], ACT.Copy).then_inc(hi_ok, 1)

        @block.vector
        def _(dve):
            dve.wait_ge(cols_t, 1)
            nc.vector.tensor_copy(keep["cols"][:, :], p_cols[:, 0:V_ROWS]).then_inc(cols_ok, 1)
            dve.wait_ge(x_in, 16)
            for i in range(TT):
                chained(dve, dve_c, nc.vector.tensor_tensor_reduce(
                    out=sq[:, :], in0=x[:, i, :], in1=x[:, i, :], scale=1.0, scalar=0.0,
                    op0=ALU.mult, op1=ALU.add, accum_out=ssq[:, i:i + 1]))
            rstd_dve_in(nc, ssq_ok, ssq[:, :], fin[:, :], root[:, :])
            dve.wait_ge(root_ok, 1)
            rstd_dve_out(nc, dve, dve_c, root[:, :], fin[:, :])
            dve.wait_ge(sil_ok, 1)
            for b in range(4):
                dve.wait_ge(ada_in[b], 16)
                nc.vector.tensor_scalar(xn[:, b, :], x[:, b, :], root[:, b:b + 1], None, ALU.mult).then_inc(xn_ok, 1)
                o = acc[:, b // 2, b % 2 * S:(b % 2 + 1) * S]
                chained(dve, acc_c, nc.vector.tensor_scalar(o, ring[b][:, 0, :], keep["csil"][:, 0:1], None, ALU.mult))
                for c in range(1, KD):
                    chained(dve, acc_c, nc.vector.scalar_tensor_tensor(o, ring[b][:, c, :], keep["csil"][:, c:c + 1], o, ALU.mult, ALU.add))
            dve.wait_ge(lam_in, 80)
            for n in range(2):
                nc.vector.tensor_tensor_reduce(
                    out=lamp[:, n, :], in0=lamv[:, 2 * n, :], in1=lamv[:, 2 * n + 1, :], scale=1.0, scalar=0.0,
                    op0=ALU.mult, op1=ALU.add, accum_out=lams[:, n:n + 1]).then_inc(lam_s, 1)
            dve.wait_ge(mod_mm, 1)
            nc.vector.tensor_tensor(keep["mod"][:, 0:2 * KD], p_mod[:, 0:2 * KD], keep["cols"][:, V_ADA:V_ADA + 2 * KD], ALU.add).then_inc(coef_ok, 1)
            dve.wait_ge(coef_ok, 1)
            nc.vector.scalar_tensor_tensor(keep["scale1"][:, :], keep["mod"][:, KD:2 * KD], 1.0, keep["cols"][:, V_G1:V_G1 + KD], ALU.add, ALU.mult).then_inc(coef_ok, 1)
            dve.wait_ge(coef_ok, 2)

            def low(i):
                dve.wait_ge(hi_ok, i + 1)
                ts = slice(i * P, (i + 1) * P)
                nc.vector.tensor_tensor(keep["h_lo"][:, :, ts], hf[:, :, ts], keep["h_hi"][:, :, ts].bitcast(F32),
                                        ALU.subtract).then_inc(v_ok, 1)

            for i in range(TT):
                dve.wait_ge(x_t, i + 1)
                modulate(nc, hf[:, :, i * P:(i + 1) * P], coef, p_x[i % 2], 1, hv_ok, "dve")
                if i:
                    low(i - 1)
            low(TT - 1)
            dve.wait_ge(lam_e, 1)
            chained(dve, dve_c, nc.vector.tensor_tensor(keep["neglam"][:, :], lams[:, 3:4], lams[:, 2:3], ALU.subtract))
            nc.vector.tensor_scalar(keep["neglam"][:, :], keep["neglam"][:, :], -LAM_INIT, None, ALU.add).then_inc(v_ok, 1)

        @block.tensor
        def _(pe):
            pe.wait_ge(rows_in, len(vectors) * 16)
            pe.wait_ge(const, 5)
            nc.tensor.transpose(p_cols[:, 0:P], rows[:, :], keep["ident"][:, :]).then_inc(cols_t, 1)

            def transposes(i):
                pe.wait_ge(xn_ok, i + 1)
                for c in range(KD):
                    ins = nc.tensor.transpose(p_x[i % 2][:, c, :], xn[:, i, c * P:(c + 1) * P], keep["ident"][:, :])
                ins.then_inc(x_t, 1)

            transposes(0)
            transposes(1)
            for s in range(2):
                pe.wait_ge(acc_c.sem, 2 * KD * (s + 1))
                for c in range(KD):
                    ins = nc.tensor.matmul(p_mod[:, s * KD + c:s * KD + c + 1], acc[:, s, c * P:(c + 1) * P], keep["ones"][:, 0:1], start=True, stop=True)
            ins.then_inc(mod_mm, 1)
            for i in range(2, TT):
                pe.wait_ge(h_ok, 4 * i - 4)
                pe.wait_ge(hv_ok, 4 * i - 4)
                transposes(i)


def phase_project(nc, a, keep, xt, space):
    with ExitStack() as stack:
        k = Kit(nc, stack, "proj", XT_AT + 68 * KB)
        raw = [k.sb(f"raw{j}", [P, KD, BW]) for j in range(4)]
        parts = space[:, :, :].rearrange("p (x a) b -> p x (a b)", x=4).rearrange("p x (k n) -> p x k n", k=KD)
        hi, lo = [parts[:, j] for j in (0, 1)], [parts[:, j] for j in (2, 3)]
        acc = [k.ps(f"acc{j}", [P, S]) for j in range(4)]
        share, ordered = k.sb("share", [P, D]), k.sb("ordered", [P, D])
        ka = Kit(nc, stack, "proj", Y_AT + 32 * KB)
        ring = [ka.sb(f"ada{j}", [P, KD, S]) for j in range(2)]
        p_mod = k.ps("mod", [P, 4 * KD])
        ada_in = [k.sem(f"ada_in{j}") for j in range(2)]
        share_ok, order_ok, mod_mm, mod_ok = (k.sem(n) for n in ("share_ok", "order_ok", "mod_mm", "mod_ok"))
        ada = a["w_ada"][0].rearrange("(k p) n -> p k n", p=P)
        w_in = [k.sem(f"w_in{j}") for j in range(4)]
        hi_ok, lo_ok, mm, out_ok = (k.sem(n) for n in ("hi_ok", "lo_ok", "mm", "out_ok"))
        w = a["w_in"][0].rearrange("(k p) n -> p k n", p=P)
        NB = MIX_BLOCKS
        block = stack.enter_context(nc.Block())

        def cols(b):
            return w[:, :, bass.ds(b * BW, BW)]

        @block.sync
        def _(sp):
            for b in range(4):
                sp.dma_start(raw[b][:, :, :], cols(b)).then_inc(w_in[b], 16)
            for j in range(2):
                sp.dma_start(ring[j][:, :, :], ada[:, :, 2 * D + j * S:2 * D + (j + 1) * S]).then_inc(ada_in[j], 16)

            def load(b, j):
                sp.wait_ge(lo_ok, b - 3)
                sp.dma_start(raw[j][:, :, :], cols(b)).then_inc(w_in[j], 16)

            with sp.Fori(1, NB // 4) as i:
                for j in range(4):
                    load(4 * i + j, j)
                    if j >= 2:
                        sp.wait_ge(share_ok, 16 * i + 8 * (j - 1) - 16)
                        sp.dma_start(ring[j - 2][:, :, :], ada[:, :, bass.ds((4 + 2 * i + j - 2) * S, S)]).then_inc(ada_in[j - 2], 16)
            load(NB - 1, 0)

        def split_hi(act, b, j, turn, first=False):
            act.wait_ge(w_in[j], 16 * turn + 16)
            if not first:
                act.wait_ge(mm, 2 * b - 2)
            nc.scalar.activation(hi[j % 2][:, :, :], raw[j][:, :, :], ACT.Copy).then_inc(hi_ok, 1)

        @block.scalar
        def _(act):
            def store(b, j):
                for m in range(2):
                    act.wait_ge(mm, 2 * b + m + 1)
                    nc.scalar.activation(xt[:, bass.ds(2 * b + m, 1), :], acc[2 * (j % 2) + m][:, :], ACT.Copy).then_inc(out_ok, 1)

            split_hi(act, 0, 0, 0, True)
            split_hi(act, 1, 1, 0, True)
            store(0, 0)
            for b in range(1, 4):
                split_hi(act, b + 1, (b + 1) % 4, (b + 1) // 4)
                store(b, b)
            with act.Fori(1, NB // 4) as i:
                for j in range(4):
                    split_hi(act, 4 * i + j + 1, (j + 1) % 4, i + (j + 1) // 4)
                    store(4 * i + j, j)
            store(NB - 1, 0)

        @block.vector
        def _(dve):
            def split_lo(b, j, first=False):
                dve.wait_ge(hi_ok, b + 1)
                nc.vector.tensor_tensor(lo[j % 2][:, :, :], raw[j][:, :, :], hi[j % 2][:, :, :].bitcast(F32),
                                        ALU.subtract).then_inc(lo_ok, 1)

            def shares(i, steps):
                for n in steps:
                    x, c = n // KD, n % KD
                    o = share[:, x * S:(x + 1) * S]
                    if c == 0:
                        dve.wait_ge(ada_in[x], 16 * i + 16)
                        nc.vector.tensor_scalar(o, ring[x][:, 0, :], keep["csil"][:, 0:1], None, ALU.mult).then_inc(share_ok, 1)
                    else:
                        dve.wait_ge(share_ok, 16 * i + n)
                        nc.vector.scalar_tensor_tensor(o, ring[x][:, c, :], keep["csil"][:, c:c + 1], o, ALU.mult, ALU.add).then_inc(share_ok, 1)

            def turn(i, first=False):
                split_lo(4 * i, 0)
                split_lo(4 * i + 1, 1)
                if not first:
                    dve.wait_ge(order_ok, i)
                shares(i, range(0, 5))
                split_lo(4 * i + 2, 2)
                shares(i, range(5, 11))
                split_lo(4 * i + 3, 3)
                shares(i, range(11, 16))
                dve.wait_ge(share_ok, 16 * i + 16)
                if not first:
                    dve.wait_ge(mod_mm, i)
                nc.vector.tensor_copy(h2_order(ordered[:, :]), model_order(share[:, :])).then_inc(order_ok, 1)

            turn(0, True)
            with dve.Fori(1, NB // 4) as i:
                turn(i)
            split_lo(NB - 1, 0)
            dve.wait_ge(mod_mm, 4)
            nc.vector.tensor_tensor(keep["mod"][:, 2 * KD:], p_mod[:, :], keep["cols"][:, V_ADA + 2 * KD:V_ADA + 6 * KD], ALU.add).then_inc(mod_ok, 1)
            dve.wait_ge(mod_ok, 1)
            nc.vector.scalar_tensor_tensor(keep["scale2"][:, :], keep["mod"][:, 4 * KD:5 * KD], 1.0, keep["cols"][:, V_G2:V_G2 + KD],
                                           ALU.add, ALU.mult).then_inc(mod_ok, 1)

        @block.tensor
        def _(pe):
            def product(b, j, first=False):
                pe.wait_ge(lo_ok, b + 1)
                for m in range(2):
                    if not first:
                        pe.wait_ge(out_ok, 2 * b + m - 3)
                    ms = slice(m * P, (m + 1) * P)
                    for c in range(KD):
                        ins = three(nc, acc[2 * (j % 2) + m][:, :], (hi[j % 2][:, c, ms], lo[j % 2][:, c, ms]),
                                    (keep["h_hi"][:, c, :], keep["h_lo"][:, c, :]), c == 0, c == KD - 1)
                    ins.then_inc(mm, 1)

            def section(i):
                pe.wait_ge(order_ok, i + 1)
                for m in range(KD):
                    ins = nc.tensor.matmul(p_mod[:, bass.ds(KD * i + m, 1)], ordered[:, m * P:(m + 1) * P], keep["ones"][:, 0:1], start=True, stop=True)
                ins.then_inc(mod_mm, 1)

            for b in range(4):
                product(b, b, b < 2)
            section(0)
            with pe.Fori(1, NB // 4) as i:
                for j in range(4):
                    product(4 * i + j, j)
                section(i)
            product(NB - 1, 0)
            pe.wait_ge(out_ok, 2 * NB)


def phase_mix(nc, a, keep, xt, y_hi, y_lo):
    units = [u for i in range(TT) for u in [("A", i, h) for h in range(HA)] + [("B", i, g) for g in range(2)]]
    NU = len(units)
    with ExitStack() as stack:
        k = Kit(nc, stack, "mix", XT_AT + 68 * KB)
        vn = k.sb("vn", [P, TT, HA, P])
        dvn = k.sb("dvn", [P, TT, P])
        kd = k.sb("kd", [P, 2, S])
        sm = k.sb("sm", [P, 2, 1024])
        pt = k.sb("pt", [P, 2, 8, P])
        causal = k.sb("causal", [P, S])
        band = k.sb("band", [P, 2 * P])
        pad = [k.sb(f"pad{j}", [P, 16 + S]) for j in range(2)]
        rcount = k.sb("rcount", [P, 16])
        wpool = k.sb("wpool", [P, 4, P])
        small = {n: k.sb(n, [P, 2, 4]) for n in ("mx", "nm", "z", "r", "sd", "es")}
        ssq, fin, root = (k.sb(n, [P, 16]) for n in ("ssq", "fin", "root"))
        subg = k.sb("subg", [P, 1])
        p_s = [k.ps(f"s{j}", [P, 1024]) for j in range(2)]
        p_t = k.ps("t", [P, 8, P])
        p_o = k.ps("o", [P, S])
        p_w = k.ps("w", [P, S])
        names = ("masks wpool_in kd_in vt vn_ok sc masked stats exped normed tr pt_ok pv o_ok pool_d pw y2_ok conv_ok "
                 "ssq_ok root_ok on_ok yt y0_ok y2_hi y3_hi y0_hi pads subg_ok").split()
        sem = {n: k.sem(n) for n in names}
        dve_c, pool_c = k.count("dve_chain"), k.count("pool_chain")
        block = stack.enter_context(nc.Block())
        scale = HD ** -0.5

        def width(u):
            kind, i, _ = u
            return (i + 1) * P if kind == "A" else (P if i == 0 else 2 * P)

        def group(n):
            kind = units[n][0]
            return 2 if kind == "A" else 4

        def view(t, n):
            m = group(n)
            return t.rearrange("p (m w) -> p m w", m=m)[:, :, 0:width(units[n])]

        def blocks(n):
            w = width(units[n]) // P
            return [(m, j) for m in range(1 if units[n][0] == "A" else 4) for j in range(w)]

        @block.sync
        def _(sp):
            for g in range(2):
                for half in range(2):
                    sp.dma_start(kd[half * HD:(half + 1) * HD, g, :], xt[g * HD:(g + 1) * HD, M_DK, :]).then_inc(sem["kd_in"], 16)
            sp.dma_start(wpool[:, :, :], a["w_pool"][0].rearrange("g c e -> c g e")).then_inc(sem["wpool_in"], 16)
            sp.wait_ge(sem["kd_in"], 64)
            sp.wait_ge(sem["wpool_in"], 16)

        @block.gpsimd
        def _(pool):
            nc.gpsimd.memset(causal[:, :], 0.0).then_inc(sem["pads"], 1)
            nc.gpsimd.memset(band[:, :], 0.0).then_inc(sem["pads"], 1)
            nc.gpsimd.memset(pad[0][:, 0:16], 0.0).then_inc(sem["pads"], 1)
            nc.gpsimd.memset(pad[1][:, 0:16], 0.0).then_inc(sem["pads"], 1)
            pool.wait_ge(sem["pads"], 4)
            nc.gpsimd.affine_select(out=causal[:, :], in_=causal[:, :], compare_op=ALU.is_ge, fill=NEG, base=S - P,
                                    pattern=[[-1, S]], channel_multiplier=1).then_inc(sem["masks"], 1)
            chained(pool, pool_c, nc.gpsimd.affine_select(out=band[:, :], in_=band[:, :], compare_op=ALU.is_gt, fill=NEG, base=0,
                                                         pattern=[[1, 2 * P]], channel_multiplier=-1))
            nc.gpsimd.affine_select(out=band[:, :], in_=band[:, :], compare_op=ALU.is_ge, fill=NEG, base=P,
                                    pattern=[[-1, 2 * P]], channel_multiplier=1).then_inc(sem["masks"], 1)
            chained(pool, pool_c, nc.gpsimd.iota(rcount[:, :], pattern=[[1, 16]], base=1, channel_multiplier=0,
                                                 allow_small_or_imprecise_dtypes=True))
            nc.gpsimd.tensor_copy(keep["invn"][:, :], rcount[:, :]).then_inc(sem["pads"], 1)

            pool.wait_ge(sem["y2_ok"], 1)
            for g in range(4):
                w = 2 << g
                src, at = xt[:, M_CZ + g, :], 0
                chained(pool, pool_c, nc.gpsimd.tensor_copy(pad[0][:, 16:], src))
                for level in range(g + 1):
                    sh = 1 << level
                    chained(pool, pool_c, nc.gpsimd.tensor_tensor(pad[1 - at][:, 16:], pad[at][:, 16:], pad[at][:, 16 - sh:16 + S - sh], ALU.add))
                    at = 1 - at
                t = pad[at]
                nc.gpsimd.tensor_scalar(t[:, 16 + w:], t[:, 16 + w:], 1.0 / w, None, ALU.mult).then_inc(pool_c.sem, 1)
                nc.gpsimd.tensor_tensor(t[:, 16:16 + w], t[:, 16:16 + w], keep["invn"][:, 0:w], ALU.mult).then_inc(pool_c.sem, 1)
                pool_c.n += 2
                pool.wait_ge(pool_c.sem, pool_c.n)
                nc.gpsimd.tensor_tensor(src, t[:, 16:], src, ALU.subtract).then_inc(sem["pool_d"], 1)
                pool.wait_ge(sem["pool_d"], g + 1)

            z = xt[:, M_BX:M_BX + 4, :]
            chained(pool, pool_c, nc.gpsimd.tensor_tensor(z, z, xt[:, M_BC:M_BC + 4, :], ALU.mult))
            for c in range(CB):
                y, zc = xt[:, M_BC + c, :], xt[:, M_BX + c, :]
                taps = [keep["cols"][:, V_CONV + 4 * j + c:V_CONV + 4 * j + c + 1] for j in range(3)]
                chained(pool, pool_c, nc.gpsimd.tensor_scalar(y, zc, taps[2], None, ALU.mult))
                for back, tap in ((1, taps[1]), (2, taps[0])):
                    n = S - back
                    tmp = pad[back - 1][:, 16:16 + n]
                    chained(pool, pool_c, nc.gpsimd.tensor_scalar(tmp, zc[:, 0:n], tap, None, ALU.mult))
                    chained(pool, pool_c, nc.gpsimd.tensor_tensor(y[:, back:], y[:, back:], tmp, ALU.add))
                chained(pool, pool_c, nc.gpsimd.tensor_tensor(y, y, xt[:, M_BB + c, :], ALU.mult))
                chained(pool, pool_c, nc.gpsimd.tensor_copy(y_hi[:, 1, c, :], y))
                nc.gpsimd.tensor_tensor(y_lo[:, 1, c, :], y, y_hi[:, 1, c, :].bitcast(F32), ALU.subtract).then_inc(sem["conv_ok"], 1)
            for n, (ready, times, m, hi) in enumerate((("y2_ok", 5, M_CZ, "y2_hi"), ("o_ok", NU, M_DQ, "y3_hi"), ("y0_ok", 4, M_AQ, "y0_hi"))):
                pool.wait_ge(sem[ready], times)
                nc.gpsimd.tensor_copy(y_hi[:, (2, 3, 0)[n], :, :], xt[:, m:m + 4, :]).then_inc(sem[hi], 1)
            pool.wait_ge(sem["conv_ok"], 4)

        @block.scalar
        def _(act):
            act.wait_ge(sem["vt"], 1)
            nc.scalar.activation(vn[:, 0:2, :, :].rearrange("p i h e -> p (i h e)"), p_s[0][:, :], ACT.Copy).then_inc(sem["vn_ok"], 1)
            act.wait_ge(sem["vt"], 2)
            nc.scalar.activation(vn[:, 2:4, :, :].rearrange("p i h e -> p (i h e)"), p_s[1][:, :], ACT.Copy).then_inc(sem["vn_ok"], 1)
            act.wait_ge(sem["vt"], 3)
            nc.scalar.activation(dvn[:, :, :], p_t[:, 0:4, :], ACT.Copy).then_inc(sem["vn_ok"], 1)

            def exps(n):
                u, b = units[n], n % 2
                act.wait_ge(sem["stats"], n + 1)
                for m in range(group(n)):
                    t = view(sm[:, b, :], n)[:, m, :]
                    ins = nc.scalar.activation(t, t, ACT.Exp, bias=small["nm"][:, b, m:m + 1], accum_out=small["z"][:, b, m:m + 1])
                if u[0] == "B":
                    ins = nc.scalar.activation(small["es"][:, b, :], small["sd"][:, b, :], ACT.Exp)
                ins.then_inc(sem["exped"], 1)

            exps(0)
            for n, (kind, i, h) in enumerate(units):
                if n + 1 < NU:
                    exps(n + 1)
                act.wait_ge(sem["tr"], n + 1)
                if n >= 2:
                    act.wait_ge(sem["pv"], n - 1)
                nb = len(blocks(n))
                nc.scalar.activation(pt[:, n % 2, 0:nb, :], p_t[:, 0:nb, :], ACT.Copy).then_inc(sem["pt_ok"], 1)
                act.wait_ge(sem["pv"], n + 1)
                if kind == "A":
                    nc.scalar.activation(xt[:, M_AV + i, h * P:(h + 1) * P], p_o[:, 0:P], ACT.Copy).then_inc(sem["o_ok"], 1)
                else:
                    nc.scalar.activation(xt[:, M_DQ + 2 * h:M_DQ + 2 * h + 2, i * P:(i + 1) * P],
                                         p_o[:, 0:2 * P].rearrange("p (m q) -> p m q", m=2), ACT.Copy).then_inc(sem["o_ok"], 1)
            for g in range(4):
                act.wait_ge(sem["pw"], g + 1)
                nc.scalar.activation(xt[:, M_CZ + g, :], p_w[:, :], ACT.Copy, scale=keep["cols"][:, V_POOL + g:V_POOL + g + 1]).then_inc(sem["y2_ok"], 1)
            act.wait_ge(sem["ssq_ok"], 2)
            nc.scalar.activation(root[:, :], root[:, :], ACT.Sqrt, bias=keep["eps"][:, :], scale=DOWN / SQ_DOWN / P).then_inc(sem["root_ok"], 1)
            act.wait_ge(sem["subg_ok"], 1)
            for h in range(HA):
                act.wait_ge(sem["yt"], h + 1)
                nc.scalar.activation(xt[:, M_AQ + h, :], p_s[h % 2][:, 0:S], ACT.Copy, scale=subg[:, :]).then_inc(sem["y0_ok"], 1)

        @block.vector
        def _(dve):
            nc.vector.tensor_scalar(subg[:, :], keep["cols"][:, V_SUB:V_SUB + 1], 1.0 - LAM_INIT, None, ALU.mult).then_inc(sem["subg_ok"], 1)
            dve.wait_ge(sem["pads"], 5)
            nc.vector.reciprocal(keep["invn"][:, :], keep["invn"][:, :]).then_inc(sem["y2_ok"], 1)
            dve.wait_ge(sem["masks"], 2)

            def scores_in(n):
                (kind, i, h), b = units[n], n % 2
                m, w = group(n), width(units[n])
                t = view(sm[:, b, :], n)
                mask = causal[:, S - w:] if kind == "A" else band[:, 2 * P - w:]
                dve.wait_ge(sem["sc"], n + 1)
                if n >= 2:
                    dve.wait_ge(sem["tr"], n - 1)
                dve_c.inc(nc.vector.scalar_tensor_tensor(t, view(p_s[b][:, :], n), scale, mask.rearrange("p (o w) -> p o w", o=1).broadcast_to([P, m, w]),
                                                         ALU.mult, ALU.add))
                dve.wait_ge(dve_c.sem, dve_c.n)
                mx, nm = small["mx"][:, b, 0:m], small["nm"][:, b, 0:m]
                chained(dve, dve_c, nc.vector.reduce_max(mx, t, AX.X))
                if kind == "B":
                    sink = keep["sinks"][:, 4 * h:4 * h + 4].rearrange("p (pair odd) -> p odd pair", odd=2)
                    mx2, sd2 = (small[x][:, b, :].rearrange("p (odd pair) -> p odd pair", odd=2) for x in ("mx", "sd"))
                    chained(dve, dve_c, nc.vector.tensor_tensor(mx2, mx2, sink, ALU.max))
                    chained(dve, dve_c, nc.vector.tensor_tensor(sd2, sink, mx2, ALU.subtract))
                nc.vector.tensor_scalar(nm, mx, -1.0, None, ALU.mult).then_inc(sem["stats"], 1)

            def normalise(n):
                (kind, i, h), b = units[n], n % 2
                t = view(sm[:, b, :], n)
                z, r = small["z"][:, b, :], small["r"][:, b, :]
                dve.wait_ge(sem["exped"], n + 1)
                if kind == "A":
                    chained(dve, dve_c, nc.vector.reciprocal(r[:, 0:2], z[:, 0:2]))
                    chained(dve, dve_c, nc.vector.tensor_tensor(r[:, 1:2], r[:, 1:2], keep["neglam"][:, :], ALU.mult))
                    chained(dve, dve_c, nc.vector.tensor_scalar(t[:, 0, :], t[:, 0, :], r[:, 0:1], None, ALU.mult))
                    nc.vector.scalar_tensor_tensor(t[:, 0, :], t[:, 1, :], r[:, 1:2], t[:, 0, :], ALU.mult, ALU.add).then_inc(sem["normed"], 1)
                else:
                    chained(dve, dve_c, nc.vector.tensor_tensor(z, z, small["es"][:, b, :], ALU.add))
                    chained(dve, dve_c, nc.vector.reciprocal(r, z))
                    nc.vector.tensor_tensor(t, t, r.rearrange("p (m o) -> p m o", o=1).broadcast_to([P, 4, width(units[n])]),
                                            ALU.mult).then_inc(sem["normed"], 1)

            scores_in(0)
            for n in range(NU):
                if n + 1 < NU:
                    scores_in(n + 1)
                normalise(n)
            dve.wait_ge(sem["o_ok"], NU)
            dve.wait_ge(sem["tr"], NU)
            o = xt[:, M_AV:M_AV + 4, :].rearrange("p i (h e) -> p (i h) e", e=P)
            sq = sm[:, :, :].rearrange("p b (x e) -> p (b x) e", e=P)
            chained(dve, dve_c, nc.vector.tensor_scalar(sq, o, O_BOUND, -O_BOUND, ALU.min, ALU.max))
            chained(dve, dve_c, nc.vector.scalar_tensor_tensor(sq, sq, SQ_DOWN, sq, ALU.mult, ALU.mult))
            chained(dve, dve_c, nc.vector.reduce_sum(ssq[:, :], sq, AX.X))
            rstd_dve_in(nc, sem["ssq_ok"], ssq[:, :], fin[:, :], root[:, :], FLT_MAX * SQ_DOWN)
            dve.wait_ge(sem["root_ok"], 1)
            rstd_dve_out(nc, dve, dve_c, root[:, :], fin[:, :])
            nc.vector.tensor_tensor(o, o, root[:, :].rearrange("p (x o) -> p x o", o=1).broadcast_to([P, 16, P]),
                                    ALU.mult).then_inc(sem["on_ok"], 1)
            for n, (m, hi) in enumerate(((M_CZ, "y2_hi"), (M_DQ, "y3_hi"), (M_AQ, "y0_hi"))):
                dve.wait_ge(sem[hi], 1)
                y = (2, 3, 0)[n]
                nc.vector.tensor_tensor(y_lo[:, y, :, :], xt[:, m:m + 4, :], y_hi[:, y, :, :].bitcast(F32), ALU.subtract).then_inc(dve_c.sem, 1)
                dve_c.n += 1
            dve.wait_ge(dve_c.sem, dve_c.n)

        @block.tensor
        def _(pe):
            ident = keep["ident"][:, :]
            for half in range(2):
                for j in range(8):
                    i, h = 2 * half + j // 4, j % 4
                    ins = nc.tensor.transpose(p_s[half][:, j * P:(j + 1) * P], xt[:, M_AV + h, i * P:(i + 1) * P], ident)
                ins.then_inc(sem["vt"], 1)
            for i in range(TT):
                ins = nc.tensor.transpose(p_t[:, i, :], xt[:, M_DV, i * P:(i + 1) * P], ident)
            ins.then_inc(sem["vt"], 1)
            pe.wait_ge(sem["kd_in"], 64)

            def scores(n):
                kind, i, h = units[n]
                if n < 2:
                    pe.wait_ge(sem["vn_ok"], n + 1)
                else:
                    pe.wait_ge(sem["stats"], n - 1)
                out = view(p_s[n % 2][:, :], n)
                qs = slice(i * P, (i + 1) * P)
                for m in range(group(n)):
                    if kind == "A":
                        rows = slice(m * HD, (m + 1) * HD)
                        q, kk = xt[rows, M_AQ + h, qs], xt[rows, M_AK + h, 0:(i + 1) * P]
                    else:
                        rows = slice(m // 2 * HD, (m // 2 + 1) * HD)
                        q, kk = xt[rows, M_DQ + 2 * h + m % 2, qs], kd[rows, h, max(0, (i - 1) * P):(i + 1) * P]
                    ins = nc.tensor.matmul(out[:, m, :], q, kk, start=True, stop=True)
                ins.then_inc(sem["sc"], 1)

            scores(0)
            scores(1)
            for n, (kind, i, h) in enumerate(units):
                pe.wait_ge(sem["normed"], n + 1)
                if n == 0:
                    pe.wait_ge(sem["vn_ok"], 3)
                else:
                    pe.wait_ge(sem["pt_ok"], n)
                for x, (m, j) in enumerate(blocks(n)):
                    ins = nc.tensor.transpose(p_t[:, x, :], view(sm[:, n % 2, :], n)[:, m, j * P:(j + 1) * P], ident)
                ins.then_inc(sem["tr"], 1)
                if n + 2 < NU:
                    scores(n + 2)
                pe.wait_ge(sem["pt_ok"], n + 1)
                if n >= 1:
                    pe.wait_ge(sem["o_ok"], n)
                w = width(units[n]) // P
                for x, (m, j) in enumerate(blocks(n)):
                    if kind == "A":
                        ins = nc.tensor.matmul(p_o[:, 0:P], pt[:, n % 2, x, :], vn[:, j, h, :], start=j == 0, stop=j == w - 1)
                    else:
                        lo = m // 2 * HD
                        ins = nc.tensor.matmul(p_o[lo:lo + HD, m % 2 * P:(m % 2 + 1) * P], dvn[:, i + 1 - w + j, h * HD:(h + 1) * HD],
                                               pt[:, n % 2, x, :], start=j == 0, stop=j == w - 1)
                ins.then_inc(sem["pv"], 1)
            pe.wait_ge(sem["wpool_in"], 16)
            for g in range(4):
                pe.wait_ge(sem["pool_d"], g + 1)
                if g:
                    pe.wait_ge(sem["y2_ok"], g + 1)
                nc.tensor.matmul(p_w[:, :], wpool[:, g, :], xt[:, M_CZ + g, :], start=True, stop=True).then_inc(sem["pw"], 1)
            pe.wait_ge(sem["on_ok"], 1)
            for h in range(HA):
                if h >= 2:
                    pe.wait_ge(sem["y0_ok"], h - 1)
                for i in range(TT):
                    ins = nc.tensor.transpose(p_s[h % 2][:, i * P:(i + 1) * P], xt[:, M_AV + i, h * P:(h + 1) * P], ident)
                ins.then_inc(sem["yt"], 1)


def phase_gate(nc, a, keep, y_hi, y_lo, merged):
    with ExitStack() as stack:
        k = Kit(nc, stack, "gate", MERGED_AT + 16 * KB)
        raw_g = [k.sb(f"raw_g{j}", [P, KD, BW]) for j in range(2)]
        raw_b = [k.sb(f"raw_b{j}", [P, CB, BW]) for j in range(2)]
        gate_w = [[k.sb(f"g{x}{j}", [P, KD, BW], F32R) for x in ("hi", "lo")] for j in range(2)]
        br_w = [[k.sb(f"b{x}{j}", [P, CB, BW], F32R) for x in ("hi", "lo")] for j in range(2)]
        sig = [k.sb(f"sig{j}", [P, S]) for j in range(2)]
        part = [k.sb(f"part{j}", [P, S]) for j in range(2)]
        p_g = [k.ps(f"g{j}", [P, S]) for j in range(4)]
        p_b = [k.ps(f"b{j}", [P, S]) for j in range(4)]
        g_in, b_in = [k.sem(f"g_in{j}") for j in range(2)], [k.sem(f"b_in{j}") for j in range(2)]
        zeroed, hi_ok, lo_ok, mm, sig_ok, part_ok, add_ok = (k.sem(n) for n in ("zeroed", "hi_ok", "lo_ok", "mm", "sig_ok", "part_ok", "add_ok"))
        wg = a["w_in"][0].rearrange("(k p) n -> p k n", p=P)
        wb = a["w_branch"][0].rearrange("g (k p) n -> p (g k) n", p=P)
        STEPS = NBR * 4
        block = stack.enter_context(nc.Block())

        @block.sync
        def _(sp):
            def load(g, d, wait=True):
                s = 4 * g + d
                if wait:
                    sp.wait_ge(lo_ok, 2 * s - 2)
                sp.dma_start(raw_g[d % 2][:, :, :], wg[:, :, bass.ds((MIX_BLOCKS + s) * BW, BW)]).then_inc(g_in[d % 2], 16)
                sp.dma_start(raw_b[d % 2][:, :, :], wb[:, bass.ds(4 * g, CB), d * BW:(d + 1) * BW]).then_inc(b_in[d % 2], 16)

            load(0, 0, False)
            load(0, 1, False)
            load(0, 2)
            load(0, 3)
            with sp.Fori(1, NBR) as g:
                for d in range(4):
                    load(g, d)

        @block.scalar
        def _(act):
            def split(g, d, wait=True):
                s, j = 4 * g + d, d % 2
                act.wait_ge(g_in[j], (2 * g + d // 2) * 16 + 16)
                act.wait_ge(b_in[j], (2 * g + d // 2) * 16 + 16)
                if wait:
                    act.wait_ge(mm, 2 * s - 2)
                nc.scalar.activation(gate_w[j][0][:, :, :], raw_g[j][:, :, :], ACT.Copy).then_inc(hi_ok, 1)
                nc.scalar.activation(br_w[j][0][:, :, :], raw_b[j][:, :, :], ACT.Copy).then_inc(hi_ok, 1)

            def sigmoid(g, d, first=False):
                s = 4 * g + d
                for m in range(2):
                    act.wait_ge(mm, 2 * s + m + 1)
                    if not (first and d == 0):
                        act.wait_ge(part_ok, 2 * s + m - 1)
                    nc.scalar.activation(sig[m][:, :], p_g[2 * (d % 2) + m][:, :], ACT.Sigmoid).then_inc(sig_ok, 1)

            split(0, 0, False)
            split(0, 1, False)
            sigmoid(0, 0, True)
            for d in range(1, 4):
                split(0, d + 1) if d < 3 else split(1, 0)
                sigmoid(0, d)
            with act.Fori(1, NBR - 1) as g:
                for d in range(4):
                    split(g, d + 1) if d < 3 else split(g + 1, 0)
                    sigmoid(g, d)
            for d in range(4):
                if d < 3:
                    split(NBR - 1, d + 1)
                sigmoid(NBR - 1, d)

        @block.vector
        def _(dve):
            def split(g, d):
                s, j = 4 * g + d, d % 2
                dve.wait_ge(hi_ok, 2 * s + 1)
                nc.vector.tensor_tensor(gate_w[j][1][:, :, :], raw_g[j][:, :, :], gate_w[j][0][:, :, :].bitcast(F32), ALU.subtract).then_inc(lo_ok, 1)
                dve.wait_ge(hi_ok, 2 * s + 2)
                nc.vector.tensor_tensor(br_w[j][1][:, :, :], raw_b[j][:, :, :], br_w[j][0][:, :, :].bitcast(F32), ALU.subtract).then_inc(lo_ok, 1)

            def weigh(g, d, first=False):
                s = 4 * g + d
                for m in range(2):
                    dve.wait_ge(sig_ok, 2 * s + m + 1)
                    if not (first and d == 0):
                        dve.wait_ge(add_ok, 2 * s + m - 1)
                    nc.vector.tensor_tensor(part[m][:, :], sig[m][:, :], p_b[2 * (d % 2) + m][:, :], ALU.mult).then_inc(part_ok, 1)

            split(0, 0)
            for d in range(4):
                split(0, d + 1) if d < 3 else split(1, 0)
                weigh(0, d, True)
            with dve.Fori(1, NBR - 1) as g:
                for d in range(4):
                    split(g, d + 1) if d < 3 else split(g + 1, 0)
                    weigh(g, d)
            for d in range(4):
                if d < 3:
                    split(NBR - 1, d + 1)
                weigh(NBR - 1, d)

        @block.gpsimd
        def _(pool):
            nc.gpsimd.memset(merged[:, :, :], 0.0).then_inc(zeroed, 1)
            pool.wait_ge(zeroed, 1)
            with pool.Fori(0, NBR) as g:
                for d in range(4):
                    for m in range(2):
                        s = 4 * g + d
                        pool.wait_ge(part_ok, 2 * s + m + 1)
                        c = 2 * d + m
                        nc.gpsimd.tensor_tensor(merged[:, c, :], merged[:, c, :], part[m][:, :], ALU.add).then_inc(add_ok, 1)

        @block.tensor
        def _(pe):
            def product(g, d, first=False):
                s, j = 4 * g + d, d % 2
                pe.wait_ge(lo_ok, 2 * s + 2)
                for m in range(2):
                    if not (first and d < 2):
                        pe.wait_ge(part_ok, 2 * s + m - 3)
                    ms = slice(m * P, (m + 1) * P)
                    for c in range(KD):
                        three(nc, p_g[2 * j + m][:, :], (gate_w[j][0][:, c, ms], gate_w[j][1][:, c, ms]),
                              (keep["h_hi"][:, c, :], keep["h_lo"][:, c, :]), c == 0, c == KD - 1)
                    for c in range(CB):
                        ins = three(nc, p_b[2 * j + m][:, :], (br_w[j][0][:, c, ms], br_w[j][1][:, c, ms]),
                                    (y_hi[:, bass.ds(4 * g + c, 1), :], y_lo[:, bass.ds(4 * g + c, 1), :]), c == 0, c == CB - 1)
                    ins.then_inc(mm, 1)

            for d in range(4):
                product(0, d, True)
            with pe.Fori(1, NBR) as g:
                for d in range(4):
                    product(g, d)



def phase_out(nc, a, keep, merged, m_hi, m_lo, space, x2):
    with ExitStack() as stack:
        k = Kit(nc, stack, "out", X2_AT + 16 * KB)
        parts = space[:, :, :].rearrange("p (x a) b -> p x (a b)", x=4).rearrange("p x (k n) -> p x k n", k=KD)
        hi, lo = [parts[:, j] for j in (0, 1)], [parts[:, j] for j in (2, 3)]
        raw = [k.sb(f"raw{j}", [P, KD, BW]) for j in range(2)]
        gate1 = k.sb("gate1", [P, D])
        diag = k.sb("diag", [P, KD, P])
        mixed = [k.sb(f"mixed{j}", [P, BW]) for j in range(2)]
        xn = k.sb("xn", [P, 2, D])
        sq = k.sb("sq", [P, D])
        hf = k.sb("hf", [P, KD, S])
        ssq, fin, root = (k.sb(n, [P, TT]) for n in ("ssq", "fin", "root"))
        acc = [k.ps(f"acc{j}", [P, S]) for j in range(4)]
        p_x = [k.ps(f"x{j}", [P, KD, P]) for j in range(2)]
        coef = (keep["scale2"], keep["mod"][:, 3 * KD:4 * KD])
        names = "hv_ok w0 w1 x_in diag_ok bc bc_ok m_hi_ok m_lo_ok hi_ok lo_ok mm x2_ok ssq_ok root_ok xn_ok x_t h_ok h_hi_ok h_lo_ok".split()
        sem = {n: k.sem(n) for n in names}
        dve_c = k.count("dve_chain")
        w = a["w_o"][0].rearrange("(k p) n -> p k n", p=P)
        NB = D // BW
        block = stack.enter_context(nc.Block())

        @block.sync
        def _(sp):
            sp.dma_start(x2[:, :, :], a["x"][0].rearrange("(i p) d -> p i d", p=P)).then_inc(sem["x_in"], 16)
            for b in range(NB):
                if b >= 2:
                    sp.wait_ge(sem["lo_ok"], b - 1)
                sp.dma_start(raw[b % 2][:, :, :], w[:, :, b * BW:(b + 1) * BW]).then_inc(sem[f"w{b % 2}"], 16)

        @block.gpsimd
        def _(pool):
            for c in range(KD):
                nc.gpsimd.tensor_scalar(diag[:, c, :], keep["ident"][:, :], keep["mod"][:, 16 + c:17 + c], None, ALU.mult).then_inc(sem["diag_ok"], 1)

        @block.scalar
        def _(act):
            nc.scalar.activation(m_hi[:, :, :], merged[:, :, :], ACT.Copy).then_inc(sem["m_hi_ok"], 1)
            for b in range(NB):
                act.wait_ge(sem[f"w{b % 2}"], 16 * (b // 2) + 16)
                if b >= 2:
                    act.wait_ge(sem["mm"], TT * (b - 1))
                nc.scalar.activation(hi[b % 2], raw[b % 2][:, :, :], ACT.Copy).then_inc(sem["hi_ok"], 1)
                if b == 0:
                    act.wait_ge(sem["bc"], 1)
                    nc.scalar.activation(gate1[:, :], p_x[0][:, :, :].rearrange("p k n -> p (k n)"), ACT.Copy).then_inc(sem["bc_ok"], 1)
            act.wait_ge(sem["ssq_ok"], 2)
            nc.scalar.activation(root[:, :], root[:, :], ACT.Sqrt, bias=keep["eps"][:, :], scale=DOWN / D).then_inc(sem["root_ok"], 1)
            for i in range(TT):
                act.wait_ge(sem["x_t"], i + 1)
                ts = slice(i * P, (i + 1) * P)
                modulate(nc, hf[:, :, ts], coef, p_x[i % 2], 0, sem["h_ok"], "act")
                act.wait_ge(sem["h_ok"], 4 * i + 4)
                act.wait_ge(sem["hv_ok"], 4 * i + 4)
                nc.scalar.activation(keep["h_hi"][:, :, ts], hf[:, :, ts], ACT.Copy).then_inc(sem["h_hi_ok"], 1)

        @block.vector
        def _(dve):
            dve.wait_ge(sem["m_hi_ok"], 1)
            nc.vector.tensor_tensor(m_lo[:, :, :], merged[:, :, :], m_hi[:, :, :].bitcast(F32), ALU.subtract).then_inc(sem["m_lo_ok"], 1)

            def split_lo(b):
                dve.wait_ge(sem["hi_ok"], b + 1)
                nc.vector.tensor_tensor(lo[b % 2], raw[b % 2][:, :, :], hi[b % 2].bitcast(F32), ALU.subtract).then_inc(sem["lo_ok"], 1)

            split_lo(0)
            dve.wait_ge(sem["x_in"], 16)
            dve.wait_ge(sem["bc_ok"], 1)
            for b in range(NB):
                if b + 1 < NB:
                    split_lo(b + 1)
                cs = slice(b * BW, (b + 1) * BW)
                for i in range(TT):
                    dve.wait_ge(sem["mm"], TT * b + i + 1)
                    chained(dve, dve_c, nc.vector.tensor_tensor(mixed[i % 2][:, :], acc[i][:, 0:BW], gate1[:, cs], ALU.mult))
                    nc.vector.tensor_tensor(x2[:, i, cs], x2[:, i, cs], mixed[i % 2][:, :], ALU.add).then_inc(sem["x2_ok"], 1)
            dve.wait_ge(sem["x2_ok"], NB * TT)
            for i in range(TT):
                chained(dve, dve_c, nc.vector.tensor_tensor_reduce(
                    out=sq[:, :], in0=x2[:, i, :], in1=x2[:, i, :], scale=1.0, scalar=0.0,
                    op0=ALU.mult, op1=ALU.add, accum_out=ssq[:, i:i + 1]))
            rstd_dve_in(nc, sem["ssq_ok"], ssq[:, :], fin[:, :], root[:, :])
            dve.wait_ge(sem["root_ok"], 1)
            rstd_dve_out(nc, dve, dve_c, root[:, :], fin[:, :])

            def norm(i):
                nc.vector.tensor_scalar(h2_order(xn[:, i % 2, :]), model_order(x2[:, i, :]), root[:, i:i + 1], None, ALU.mult).then_inc(sem["xn_ok"], 1)

            def low(i):
                dve.wait_ge(sem["h_hi_ok"], i + 1)
                ts = slice(i * P, (i + 1) * P)
                nc.vector.tensor_tensor(keep["h_lo"][:, :, ts], hf[:, :, ts], keep["h_hi"][:, :, ts].bitcast(F32),
                                        ALU.subtract).then_inc(sem["h_lo_ok"], 1)

            norm(0)
            norm(1)
            for i in range(TT):
                dve.wait_ge(sem["x_t"], i + 1)
                modulate(nc, hf[:, :, i * P:(i + 1) * P], coef, p_x[i % 2], 1, sem["hv_ok"], "dve")
                if i + 2 < TT:
                    norm(i + 2)
                if i:
                    low(i - 1)
            low(TT - 1)

        @block.tensor
        def _(pe):
            pe.wait_ge(sem["diag_ok"], KD)
            for c in range(KD):
                for x in range(2):
                    half = model_order(p_x[0][:, 4 * x:4 * x + 4, :].rearrange("p k n -> p (k n)"), 2)
                    ins = nc.tensor.matmul(half[:, :, c], keep["ones"][:, :], diag[:, c, 2 * x * 32:(2 * x + 2) * 32], start=True, stop=True)
            ins.then_inc(sem["bc"], 1)
            pe.wait_ge(sem["m_lo_ok"], 1)
            for b in range(NB):
                pe.wait_ge(sem["lo_ok"], b + 1)
                for i in range(TT):
                    if b:
                        pe.wait_ge(sem["x2_ok"], TT * (b - 1) + i + 1)
                    ts = slice(i * P, (i + 1) * P)
                    for c in range(KD):
                        ins = three(nc, acc[i][:, 0:BW], (m_hi[:, c, ts], m_lo[:, c, ts]), (hi[b % 2][:, c, :], lo[b % 2][:, c, :]), c == 0, c == KD - 1)
                    ins.then_inc(sem["mm"], 1)
            for i in range(TT):
                pe.wait_ge(sem["xn_ok"], i + 1)
                if i == 0:
                    pe.wait_ge(sem["bc_ok"], 1)
                if i >= 2:
                    pe.wait_ge(sem["h_ok"], 4 * i - 4)
                    pe.wait_ge(sem["hv_ok"], 4 * i - 4)
                for c in range(KD):
                    ins = nc.tensor.transpose(p_x[i % 2][:, c, :], xn[:, i % 2, c * P:(c + 1) * P], keep["ident"][:, :])
                ins.then_inc(sem["x_t"], 1)


def phase_query(nc, a, keep, scores):
    with ExitStack() as stack:
        k = Kit(nc, stack, "query", X2_AT + 16 * KB)
        raw = [k.sb(f"raw{j}", [P, KD, BW]) for j in range(2)]
        hi = [k.sb(f"hi{j}", [P, KD, BW], F32R) for j in range(2)]
        lo = [k.sb(f"lo{j}", [P, KD, BW], F32R) for j in range(2)]
        q = [k.sb(f"q{j}", [P, S]) for j in range(2)]
        keys = k.sb("keys", [P, 2, P])
        keys_t = k.sb("keys_t", [P, 2, P])
        acc = [k.ps(f"acc{j}", [P, S]) for j in range(4)]
        p_s = [k.ps(f"s{j}", [P, TT, P]) for j in range(2)]
        p_k = k.ps("k", [P, 2, P])
        names = "w0 w1 keys_in kt kt_ok hi_ok lo_ok mm q_ok sc s_ok".split()
        sem = {n: k.sem(n) for n in names}
        w = a["w_q"][0].rearrange("(q m r) n -> q r m n", q=4, m=KD)
        block = stack.enter_context(nc.Block())

        @block.sync
        def _(sp):
            sp.dma_start(keys[:, :, :], a["sub_keys"][0].rearrange("s n d -> n s d")).then_inc(sem["keys_in"], 16)

            def load(b, j):
                for x in range(4):
                    sp.dma_start(raw[j][32 * x:32 * x + 32, :, :], w[x, :, :, bass.ds(b * BW, BW)]).then_inc(sem[f"w{j}"], 16)

            load(0, 0)
            load(1, 1)
            with sp.Fori(1, PH // 2) as i:
                for j in range(2):
                    sp.wait_ge(sem["lo_ok"], 2 * i + j - 1)
                    load(2 * i + j, j)

        @block.scalar
        def _(act):
            act.wait_ge(sem["kt"], 1)
            nc.scalar.activation(keys_t[:, :, :], p_k[:, :, :], ACT.Copy).then_inc(sem["kt_ok"], 1)

            def split(b, j, turn, first=False):
                act.wait_ge(sem[f"w{j}"], 64 * turn + 64)
                if not first:
                    act.wait_ge(sem["mm"], 2 * b - 2)
                nc.scalar.activation(hi[j][:, :, :], raw[j][:, :, :], ACT.Copy).then_inc(sem["hi_ok"], 1)

            def queries(b, j, first=False):
                for m in range(2):
                    act.wait_ge(sem["mm"], 2 * b + m + 1)
                    if not first:
                        act.wait_ge(sem["sc"], 2 * b + m - 1)
                    nc.scalar.activation(q[m][:, :], acc[2 * j + m][:, :], ACT.Copy).then_inc(sem["q_ok"], 1)

            split(0, 0, 0, True)
            split(1, 1, 0, True)
            queries(0, 0, True)
            split(2, 0, 1)
            queries(1, 1)
            with act.Fori(1, PH // 2 - 1) as i:
                for j in range(2):
                    split(2 * i + j + 1, 1 - j, i + j)
                    queries(2 * i + j, j)
            split(PH - 1, 1, PH // 2 - 1)
            queries(PH - 2, 0)
            queries(PH - 1, 1)

        @block.vector
        def _(dve):
            def split(b, j):
                dve.wait_ge(sem["hi_ok"], b + 1)
                nc.vector.tensor_tensor(lo[j][:, :, :], raw[j][:, :, :], hi[j][:, :, :].bitcast(F32), ALU.subtract).then_inc(sem["lo_ok"], 1)

            def out(b):
                for m in range(2):
                    dve.wait_ge(sem["sc"], 2 * b + m + 1)
                    nc.vector.tensor_copy(scores[:, :, bass.ds(2 * b + m, 1), :], p_s[m][:, :, :]).then_inc(sem["s_ok"], 1)

            split(0, 0)
            split(1, 1)
            out(0)
            with dve.Fori(1, PH // 2) as i:
                split(2 * i, 0)
                out(2 * i - 1)
                split(2 * i + 1, 1)
                out(2 * i)
            out(PH - 1)

        @block.tensor
        def _(pe):
            pe.wait_ge(sem["keys_in"], 16)
            for x in range(2):
                ins = nc.tensor.transpose(p_k[:, x, :], keys[:, x, :], keep["ident"][:, :])
            ins.then_inc(sem["kt"], 1)
            pe.wait_ge(sem["kt_ok"], 1)

            def product(b, j, first=False):
                pe.wait_ge(sem["lo_ok"], b + 1)
                for m in range(2):
                    if not first:
                        pe.wait_ge(sem["q_ok"], 2 * b + m - 3)
                    ms = slice(m * P, (m + 1) * P)
                    for c in range(KD):
                        ins = three(nc, acc[2 * j + m][:, :], (hi[j][:, c, ms], lo[j][:, c, ms]),
                                    (keep["h_hi"][:, c, :], keep["h_lo"][:, c, :]), c == 0, c == KD - 1)
                    ins.then_inc(sem["mm"], 1)

            def score(b, first=False):
                for m in range(2):
                    pe.wait_ge(sem["q_ok"], 2 * b + m + 1)
                    if not first:
                        pe.wait_ge(sem["s_ok"], 2 * b + m - 1)
                    for i in range(TT):
                        ins = nc.tensor.matmul(p_s[m][:, i, :], q[m][:, i * P:(i + 1) * P], keys_t[:, m, :], start=True, stop=True)
                    ins.then_inc(sem["sc"], 1)

            product(0, 0, True)
            product(1, 1, True)
            score(0, True)
            with pe.Fori(1, PH // 2) as i:
                product(2 * i, 0)
                score(2 * i - 1)
                product(2 * i + 1, 1)
                score(2 * i)
            score(PH - 1)


PLAIN = 64
PICK = 48
SOFT_AT = 52
SLOTS_AT = 56
CH = 32
CHUNKS = S // CH
GTOK = 8
UNROLL = 8


def phase_experts(nc, a, keep, scores, acts, gates):
    with ExitStack() as stack:
        k = Kit(nc, stack, "u", Y_AT)
        match = [k.sb(f"match{j}", [P, P, 2 * GTOK], BF16) for j in range(2)]
        hot = [k.sb(f"hot{j}", [P, P, 3, GTOK], BF16) for j in range(2)]
        assert k.at <= Y_AT + 32 * KB
        k.at = Y_AT + 32 * KB
        raw = [k.sb(f"raw{j}", [P, 8, BW]) for j in range(2)]
        ut = [k.sb(f"ut{j}", [P, KD, P]) for j in range(2)]
        hi = [k.sb(f"hi{j}", [P, KD, P], F32R) for j in range(2)]
        lo = [k.sb(f"lo{j}", [P, KD, P], F32R) for j in range(2)]
        ao = [k.sb(f"ao{j}", [P, 2, S]) for j in range(2)]
        assert k.at <= X2_AT
        k.at = X2_AT + 16 * KB
        gs_at = k.at
        gs = [k.sb(f"gs{j}", [P, P, CH]) for j in range(2)]
        after = k.at
        k.at = gs_at
        sc, sc2, eq, cand = (k.sb(n, [P, 16 * P]) for n in ("sc", "sc2", "eq", "cand"))
        assert k.at <= after
        k.at = after
        top = k.sb("top", [P, 16, TOPK])
        topi = k.sb("topi", [P, 16, TOPK], U32)
        topf = k.sb("topf", [P, 16, TOPK])
        best = k.sb("best", [P, PH, TOPK])
        pos = k.sb("pos", [P, PH * TOPK], U32)
        ab = k.sb("ab", [P, 2, PH * TOPK], U32)
        abf = k.sb("abf", [P, 2, PH * TOPK])
        carrier = k.sb("carrier", [P, 1])
        sel = k.sb("sel", [P, 3, TT, P])
        z = k.sb("z", [P, TT * PH])
        keys = k.sb("keys", [P, S // GTOK, 2, GTOK], BF16)
        parts = k.sb("parts", [P, S // GTOK, 3, GTOK], BF16)
        rest = [k.sb(f"rest{j}", [P, S]) for j in range(2)]
        iota16 = k.sb("iota16", [P, TOPK])
        iota = k.sb("iota", [P, P, 2 * GTOK], BF16)
        p_s = [k.ps(f"s{j}", [P, S]) for j in range(4)]
        p_g = [k.ps(f"g{j}", [P, 4, P]) for j in range(4)]
        names = ("iota_ok u_in0 u_in1 ut_ok hi_ok lo_ok mm act_ok a_out0 a_out1 step exp_ok sel_ok slot_t slot_ok hot_ok g_mm g_ok "
                 "g_out0 g_out1").split()
        sem = {n: k.sem(n) for n in names}
        dve_c = k.count("dve_chain")
        block = stack.enter_context(nc.Block())
        u = a["u_experts"][0].rearrange("(b m r) (q c) -> b q r m c", m=8, r=32, q=4)
        au = acts.rearrange("(b x) p t -> b p x t", x=2)
        TILES = NE // P
        TURNS = (TILES - PLAIN) // UNROLL
        STEPS = 1 + 5 * 2 * PH + 2 + 5 * PH + 2 + 2 + 2 * 3 + 17

        @block.sync
        def _(sp):
            def load(n, j, wait=True):
                if wait:
                    sp.wait_ge(sem["ut_ok"], 2 * n - 2)
                for q in range(4):
                    sp.dma_start(raw[j][32 * q:32 * q + 32, :, :], u[n, q] if isinstance(n, int) else
                                 u[bass.ds(n, 1), q].rearrange("o r m c -> (o r) m c")).then_inc(sem[f"u_in{j}"], 16)

            def store(n, j):
                sp.wait_ge(sem["act_ok"], 2 * n + 2)
                sp.dma_start(au[n], ao[j][:, :, :]).then_inc(sem[f"a_out{j}"], 16)

            def gates_out(c, j):
                sp.wait_ge(sem["g_ok"], (c + 1) * (CH // 4))
                sp.dma_start(gates[c], gs[j][:, :, :]).then_inc(sem[f"g_out{j}"], 16)

            load(0, 0, False)
            load(1, 1, False)
            with sp.Fori(0, PLAIN // 4) as i:
                for j in range(2):
                    load(2 * i + j + 2, j)
                    store(2 * i + j, j)

            def turn(i, last=False):
                for x in range(UNROLL // 2):
                    n = PLAIN // 2 + i * (UNROLL // 2) + x
                    if not (last and x >= UNROLL // 2 - 2):
                        load(n + 2, x % 2)
                    store(n, x % 2)
                    if x % 2:
                        gates_out(2 * i + x // 2, x // 2)

            with sp.Fori(0, TURNS - 1) as i:
                turn(i)
            turn(TURNS - 1, True)
            for j in range(2):
                sp.wait_ge(sem[f"a_out{j}"], 16 * TILES // 4)
                sp.wait_ge(sem[f"g_out{j}"], 16 * TURNS)

        @block.gpsimd
        def _(pool):
            nc.gpsimd.iota(iota16[:, :], pattern=[[1, TOPK]], base=0, channel_multiplier=0,
                           allow_small_or_imprecise_dtypes=True).then_inc(sem["iota_ok"], 1)
            nc.gpsimd.iota(iota[:, :, :], pattern=[[1, P], [0, 2 * GTOK]], base=0, channel_multiplier=0,
                           allow_small_or_imprecise_dtypes=True).then_inc(sem["iota_ok"], 1)

            def split_lo(t, j, wait=True):
                pool.wait_ge(sem["hi_ok"], t + 1)
                if wait:
                    pool.wait_ge(sem["mm"], t - 1)
                nc.gpsimd.tensor_tensor(lo[j][:, :, :], ut[j][:, :, :], hi[j][:, :, :].bitcast(F32), ALU.subtract).then_inc(sem["lo_ok"], 1)

            split_lo(0, 0, False)
            split_lo(1, 1, False)
            with pool.Fori(1, TILES // 2) as i:
                for j in range(2):
                    split_lo(2 * i + j, j)

        @block.scalar
        def _(act):
            def split_hi(t, j, wait=True):
                act.wait_ge(sem["ut_ok"], t + 1)
                if wait:
                    act.wait_ge(sem["mm"], t - 1)
                nc.scalar.activation(hi[j][:, :, :], ut[j][:, :, :], ACT.Copy).then_inc(sem["hi_ok"], 1)

            def gelu(t, j, first=False):
                act.wait_ge(sem["mm"], t + 1)
                if not first and j % 2 == 0:
                    act.wait_ge(sem[f"a_out{j // 2}"], (t - j) * 4)
                nc.scalar.activation(ao[j // 2][:, j % 2, :], p_s[j][:, :], ACT.Gelu).then_inc(sem["act_ok"], 1)

            def plain(i, first=False):
                for j in range(4):
                    t = 4 * i + j
                    split_hi(t + 1, (j + 1) % 2, not (first and j == 0))
                    gelu(t, j, first)

            split_hi(0, 0, False)
            plain(0, True)
            with act.Fori(1, SOFT_AT // 4) as i:
                plain(i)
            act.wait_ge(sem["step"], TT * STEPS)
            nc.scalar.activation(sel[:, 2, :, :], sel[:, 2, :, :], ACT.Exp).then_inc(sem["exp_ok"], 1)
            with act.Fori(SOFT_AT // 4, PLAIN // 4) as i:
                plain(i)

            def turn(i, first=False, last=False):
                for x in range(UNROLL):
                    t = PLAIN + i * UNROLL + x
                    if not (last and x == UNROLL - 1):
                        split_hi(t + 1, (x + 1) % 2)
                    act.wait_ge(sem["mm"], t + 1)
                    j = x % 4
                    if x % 2 == 0:
                        act.wait_ge(sem[f"a_out{j // 2}"], (t - j) * 4)
                    nc.scalar.activation(ao[j // 2][:, j % 2, :], p_s[j][:, :], ACT.Gelu).then_inc(sem["act_ok"], 1)
                    chunk = x // 4
                    if x % 4 == 0 and not first:
                        act.wait_ge(sem[f"g_out{chunk}"], 16 * i)
                    for y in range(2):
                        n = 2 * x + y
                        act.wait_ge(sem["g_mm"], 2 * UNROLL * i + n + 1)
                        at = (n % 8) * 4
                        nc.scalar.activation(gs[chunk][:, :, at:at + 4].rearrange("p i t -> p t i"), p_g[n % 4][:, :, :], ACT.Copy).then_inc(sem["g_ok"], 1)

            turn(0, True)
            with act.Fori(1, TURNS - 1) as i:
                turn(i)
            turn(TURNS - 1, False, True)

        @block.vector
        def _(dve):
            slots = [P, PH, TOPK, TOPK]

            def transposes(t, j, wait=True):
                if j % 2 == 0:
                    dve.wait_ge(sem[f"u_in{j // 2}"], (t - j) * 16 + 64)
                if wait:
                    dve.wait_ge(sem["lo_ok"], t - 1)
                half = raw[j // 2][:, 4 * (j % 2):4 * (j % 2) + 4, :]
                nc.vector.transpose(ut[j % 2][:, :, :].rearrange("p m (b e) -> p b m e", b=4),
                                    half.rearrange("p b (m r) -> p b m r", m=KD)).then_inc(sem["ut_ok"], 1)

            steps = Count(sem["step"])
            beside = [0]

            def step(i, ins):
                steps.inc(ins)
                if steps.n * (PICK // TT) // STEPS > beside[0]:
                    j = beside[0] + 2
                    transposes(i * (PICK // TT) + j, j % 4)
                    beside[0] += 1

            def fence(i):
                dve.wait_ge(steps.sem, i * STEPS + steps.n)
                step(i, nc.vector.memset(carrier[:, :], 0.0))

            def largest(i, n, w, src, tmp, vals, index):
                for x in range(n):
                    step(i, nc.vector.max(vals[:, x, 0:8], src[:, x * w:(x + 1) * w]))
                fence(i)
                for x in range(n):
                    step(i, nc.vector.max_index(index[:, x, 0:8], vals[:, x, 0:8], src[:, x * w:(x + 1) * w]))
                    step(i, nc.vector.match_replace(tmp[:, x * w:(x + 1) * w], vals[:, x, 0:8], src[:, x * w:(x + 1) * w], -FLT_MAX))
                fence(i)
                for x in range(n):
                    step(i, nc.vector.max(vals[:, x, 8:16], tmp[:, x * w:(x + 1) * w]))
                fence(i)
                for x in range(n):
                    step(i, nc.vector.max_index(index[:, x, 8:16], vals[:, x, 8:16], tmp[:, x * w:(x + 1) * w]))
                fence(i)

            transposes(0, 0, False)
            transposes(1, 1, False)
            dve.wait_ge(sem["iota_ok"], 2)
            with dve.Fori(0, TT) as i:
                step(i, nc.vector.tensor_copy(sc[:, :].rearrange("p (o h n) -> p o h n", o=1, h=16), scores[:, bass.ds(i, 1), :, :]))
                fence(i)
                largest(i, 2 * PH, P, sc, sc2, top, topi)
                step(i, nc.vector.tensor_copy(topf[:, :, :], topi[:, :, :]))
                half = top[:, :, :].rearrange("p (h s) k -> p s h k", s=2)
                first = half[:, 0].rearrange("p h (k o) -> p h k o", o=1).broadcast_to(slots)
                second = half[:, 1].rearrange("p h (o k) -> p h o k", o=1).broadcast_to(slots)
                step(i, nc.vector.tensor_tensor(cand[:, :].rearrange("p (h a b) -> p h a b", h=PH, a=TOPK), first, second, ALU.add))
                fence(i)
                largest(i, PH, TOPK * TOPK, cand, sc2, best, pos[:, :].rearrange("p (h k) -> p h k", h=PH))
                step(i, nc.vector.tensor_scalar(ab[:, 0, :], pos[:, :], 4, None, ALU.logical_shift_right))
                step(i, nc.vector.tensor_scalar(ab[:, 1, :], pos[:, :], 15, None, ALU.bitwise_and))
                fence(i)
                step(i, nc.vector.tensor_copy(abf[:, :, :], ab[:, :, :]))
                step(i, nc.vector.tensor_tensor(sel[:, 2, bass.ds(i, 1), :].rearrange("p o (h k) -> p (o h) k", h=PH), best[:, :, :],
                                                best[:, :, 0:1].broadcast_to([P, PH, TOPK]), ALU.subtract))
                fence(i)
                for s, e_flat in enumerate((eq, sc)):
                    e = e_flat[:, :].rearrange("p (h k a) -> p h k a", h=PH, k=TOPK)
                    rank = abf[:, s, :].rearrange("p (h k o) -> p h k o", h=PH, o=1).broadcast_to(slots)
                    upto = iota16[:, :].rearrange("p (x y a) -> p x y a", x=1, y=1).broadcast_to(slots)
                    key = topf[:, :, :].rearrange("p (h s) k -> p s h k", s=2)[:, s].rearrange("p h (o a) -> p h o a", o=1).broadcast_to(slots)
                    step(i, nc.vector.tensor_tensor(e, rank, upto, ALU.is_equal))
                    fence(i)
                    step(i, nc.vector.tensor_tensor(e, e, key, ALU.mult))
                    fence(i)
                    step(i, nc.vector.reduce_sum(sel[:, s, bass.ds(i, 1), :].rearrange("p o (n q) -> p (o n) q", q=1),
                                                 e_flat[:, :].rearrange("p (n a) -> p n a", a=TOPK), AX.X))
                fence(i)
                assert steps.n == STEPS and beside[0] == PICK // TT

            for t in range(PICK + 2, SOFT_AT + 2):
                transposes(t, t % 4)
            dve.wait_ge(sem["exp_ok"], 1)
            ev = sel[:, 2, :, :].rearrange("p i (h k) -> p (i h) k", k=TOPK)
            chained(dve, dve_c, nc.vector.reduce_sum(z[:, :], ev, AX.X))
            chained(dve, dve_c, nc.vector.reciprocal(z[:, :], z[:, :]))
            nc.vector.tensor_tensor(ev, ev, z[:, :].rearrange("p (x o) -> p x o", o=1).broadcast_to([P, TT * PH, TOPK]),
                                    ALU.mult).then_inc(sem["sel_ok"], 1)
            for t in range(SOFT_AT + 2, SLOTS_AT + 2):
                transposes(t, t % 4)
            dve.wait_ge(sem["slot_t"], 3)
            by_slot = [p_g[s][:, :, :].rearrange("p i (g t) -> p (i g) t", t=GTOK) for s in range(3)]
            rests = [r[:, :].rearrange("p (g t) -> p g t", t=GTOK) for r in rest]
            for s in range(2):
                nc.vector.tensor_copy(keys[:, :, s, :], by_slot[s]).then_inc(sem["slot_ok"], 1)
            chained(dve, dve_c, nc.vector.tensor_copy(parts[:, :, 0, :], by_slot[2]))
            chained(dve, dve_c, nc.vector.tensor_tensor(rests[0], by_slot[2], parts[:, :, 0, :], ALU.subtract))
            chained(dve, dve_c, nc.vector.tensor_copy(parts[:, :, 1, :], rests[0]))
            chained(dve, dve_c, nc.vector.tensor_tensor(rests[1], rests[0], parts[:, :, 1, :], ALU.subtract))
            nc.vector.tensor_copy(parts[:, :, 2, :], rests[1]).then_inc(sem["slot_ok"], 1)
            for t in range(SLOTS_AT + 2, PLAIN + 2):
                transposes(t, t % 4)
            dve.wait_ge(sem["slot_ok"], 3)

            def turn(i, first=False, last=False):
                for x in range(UNROLL):
                    t = PLAIN + i * UNROLL + x
                    g = i * UNROLL + x
                    if not (last and x >= UNROLL - 2):
                        transposes(t + 2, (x + 2) % 4)
                    if not (first and x < 2):
                        dve.wait_ge(sem["g_mm"], 2 * g - 2)
                    m, h = match[x % 2], hot[x % 2]
                    key = keys[:, bass.ds(g, 1), :, :].rearrange("p o s t -> p o (s t)").broadcast_to([P, P, 2 * GTOK])
                    nc.vector.tensor_tensor(m[:, :, :], iota[:, :, :], key, ALU.is_equal).then_inc(sem["hot_ok"], 1)
                    dve.wait_ge(sem["hot_ok"], 2 * g + 1)
                    ones = m[:, :, 0:GTOK].rearrange("p i (o t) -> p i o t", o=1).broadcast_to([P, P, 3, GTOK])
                    w = parts[:, bass.ds(g, 1), :, :].broadcast_to([P, P, 3, GTOK])
                    nc.vector.tensor_tensor(h[:, :, :, :], ones, w, ALU.mult).then_inc(sem["hot_ok"], 1)

            turn(0, True)
            with dve.Fori(1, TURNS - 1) as i:
                turn(i)
            turn(TURNS - 1, False, True)

        @block.tensor
        def _(pe):
            ident = keep["ident"][:, :]

            def product(t, j, wait=True):
                pe.wait_ge(sem["lo_ok"], t + 1)
                if wait:
                    pe.wait_ge(sem["act_ok"], t - 3)
                for c in range(KD):
                    ins = three(nc, p_s[j][:, :], (hi[j % 2][:, c, :], lo[j % 2][:, c, :]),
                                (keep["h_hi"][:, c, :], keep["h_lo"][:, c, :]), c == 0, c == KD - 1)
                ins.then_inc(sem["mm"], 1)

            def plain(i, first=False):
                for j in range(4):
                    product(4 * i + j, j, not first)

            plain(0, True)
            with pe.Fori(1, SLOTS_AT // 4) as i:
                plain(i)
            pe.wait_ge(sem["sel_ok"], 1)
            for s in range(3):
                for i in range(TT):
                    ins = nc.tensor.transpose(p_g[s][:, i, :], sel[:, s, i, :], ident)
                ins.then_inc(sem["slot_t"], 1)
            with pe.Fori(SLOTS_AT // 4, PLAIN // 4) as i:
                plain(i)

            def turn(i, first=False):
                for x in range(UNROLL):
                    product(PLAIN + i * UNROLL + x, x % 4)
                    g = i * UNROLL + x
                    pe.wait_ge(sem["hot_ok"], 2 * g + 2)
                    m, h = match[x % 2], hot[x % 2]
                    for y in range(2):
                        n = 2 * x + y
                        if not (first and n < 4):
                            pe.wait_ge(sem["g_ok"], 2 * UNROLL * i + n - 3)
                        for b in range(4):
                            t = 4 * y + b
                            for part in range(3):
                                ins = nc.tensor.matmul(p_g[n % 4][:, b, :], m[:, :, GTOK + t], h[:, :, part, t], start=part == 0, stop=part == 2)
                        ins.then_inc(sem["g_mm"], 1)

            turn(0, True)
            with pe.Fori(1, TURNS) as i:
                turn(i)


GT = 4


def phase_combine(nc, a, keep, acts, gates, x2, out):
    with ExitStack() as stack:
        k = Kit(nc, stack, "v", LOW)
        v = k.sb("v", [P, GT, D])
        v_hi = [k.sb(f"v_hi{j}", [P, GT, D], F32R) for j in range(2)]
        v_lo = [k.sb(f"v_lo{j}", [P, GT, D], F32R) for j in range(2)]
        at = [k.sb(f"at{j}", [P, GT, S]) for j in range(2)]
        assert k.at <= X2_AT
        k.at = X2_AT + 16 * KB
        gt = [k.sb(f"gt{j}", [P, CHUNKS, GT * CH]) for j in range(2)]
        w_hi = [k.sb(f"w_hi{j}", [P, GT, S], F32R) for j in range(2)]
        w_lo = [k.sb(f"w_lo{j}", [P, GT, S], F32R) for j in range(2)]
        acc = k.sb("acc", [P, TT, D])
        gate2 = k.sb("gate2", [P, D])
        g_fin = k.sb("g_fin", [P, D])
        ssq, fin, root = (k.sb(n, [P, TT]) for n in ("ssq", "fin", "root"))
        diag = at[0][:, 0:2, :].rearrange("p a (b n) -> p (a b) n", n=P)
        p_o = [k.ps(f"o{j}", [P, S]) for j in range(8)]
        names = ("v_in a_in0 a_in1 g_in0 g_in1 gf_in diag_ok bc bc_ok zeroed vhi_ok vlo_ok w_ok whi_ok wlo_ok mm add_ok "
                 "ssq_ok root_ok y_ok out_ok").split()
        sem = {n: k.sem(n) for n in names}
        dve_c = k.count("dve_chain")
        block = stack.enter_context(nc.Block())
        vv = a["v_experts"][0].rearrange("(g x p) d -> g p x d", x=GT, p=P)
        av = acts.rearrange("(g x) p t -> g p x t", x=GT)
        gv = gates.rearrange("c j (g x) t -> g j c (x t)", x=GT)
        NG = NE // P // GT

        @block.sync
        def _(sp):
            def load(g, j, first=False):
                if not first:
                    sp.wait_ge(sem["vlo_ok"], g)
                sp.dma_start(v[:, :, :], vv[g]).then_inc(sem["v_in"], 16)
                if not first:
                    sp.wait_ge(sem["wlo_ok"], g - 1)
                sp.dma_start(at[j][:, :, :], av[g]).then_inc(sem[f"a_in{j}"], 16)
                sp.dma_start(gt[j][:, :, :], gv[g]).then_inc(sem[f"g_in{j}"], 16)

            sp.wait_ge(sem["bc"], 1)
            load(0, 0, True)
            sp.dma_start(g_fin[:, :], a["g_final"].rearrange("(o d) -> o d", o=1).to_broadcast([P, D])).then_inc(sem["gf_in"], 16)
            sp.wait_ge(sem["vlo_ok"], 1)
            sp.dma_start(v[:, :, :], vv[1]).then_inc(sem["v_in"], 16)
            sp.dma_start(at[1][:, :, :], av[1]).then_inc(sem["a_in1"], 16)
            sp.dma_start(gt[1][:, :, :], gv[1]).then_inc(sem["g_in1"], 16)
            with sp.Fori(1, NG // 2) as i:
                for j in range(2):
                    load(2 * i + j, j)
            ov = out[0].rearrange("(i p) d -> p i d", p=P)
            for i in range(TT):
                sp.wait_ge(sem["y_ok"], i + 1)
                sp.dma_start(ov[:, i, :], acc[:, i, :]).then_inc(sem["out_ok"], 16)
            sp.wait_ge(sem["out_ok"], 16 * TT)

        @block.gpsimd
        def _(pool):
            for c in range(KD):
                nc.gpsimd.tensor_scalar(diag[:, c, :], keep["ident"][:, :], keep["mod"][:, 40 + c:41 + c], None, ALU.mult).then_inc(sem["diag_ok"], 1)
            nc.gpsimd.memset(acc[:, :, :], 0.0).then_inc(sem["zeroed"], 1)

            def weigh(i, j):
                pool.wait_ge(sem[f"a_in{j}"], 16 * i + 16)
                pool.wait_ge(sem[f"g_in{j}"], 16 * i + 16)
                x = at[j][:, :, :].rearrange("p x (c t) -> p x c t", t=CH)
                nc.gpsimd.tensor_tensor(x, x, gt[j][:, :, :].rearrange("p c (x t) -> p x c t", t=CH), ALU.mult).then_inc(sem["w_ok"], 1)

            with pool.Fori(0, NG // 2) as i:
                for j in range(2):
                    weigh(i, j)

        @block.scalar
        def _(act):
            act.wait_ge(sem["bc"], 1)
            for j in range(2):
                nc.scalar.activation(gate2[:, j * S:(j + 1) * S], p_o[j][:, :], ACT.Copy).then_inc(sem["bc_ok"], 1)

            def split(g, j, first=False):
                act.wait_ge(sem["v_in"], 16 * g + 16)
                if not first:
                    act.wait_ge(sem["mm"], 8 * g - 8)
                nc.scalar.activation(v_hi[j][:, :, :], v[:, :, :], ACT.Copy).then_inc(sem["vhi_ok"], 1)
                act.wait_ge(sem["w_ok"], g + 1)
                nc.scalar.activation(w_hi[j][:, :, :], at[j][:, :, :], ACT.Copy).then_inc(sem["whi_ok"], 1)

            split(0, 0, True)
            split(1, 1, True)
            with act.Fori(1, NG // 2) as i:
                for j in range(2):
                    split(2 * i + j, j)
            act.wait_ge(sem["ssq_ok"], 2)
            nc.scalar.activation(root[:, :], root[:, :], ACT.Sqrt, bias=keep["eps"][:, :], scale=DOWN / D).then_inc(sem["root_ok"], 1)

        @block.vector
        def _(dve):
            def split(g, j):
                dve.wait_ge(sem["vhi_ok"], g + 1)
                nc.vector.tensor_tensor(v_lo[j][:, :, :], v[:, :, :], v_hi[j][:, :, :].bitcast(F32), ALU.subtract).then_inc(sem["vlo_ok"], 1)
                dve.wait_ge(sem["whi_ok"], g + 1)
                nc.vector.tensor_tensor(w_lo[j][:, :, :], at[j][:, :, :], w_hi[j][:, :, :].bitcast(F32), ALU.subtract).then_inc(sem["wlo_ok"], 1)

            def add(g, banks, first=False):
                for n in banks:
                    dve.wait_ge(sem["mm"], 8 * g + n + 1)
                    if not first:
                        dve.wait_ge(sem["add_ok"], 8 * g + n - 7)
                    o = acc[:, n // 2, n % 2 * S:(n % 2 + 1) * S]
                    nc.vector.tensor_tensor(o, o, p_o[n][:, :], ALU.add).then_inc(sem["add_ok"], 1)

            split(0, 0)
            dve.wait_ge(sem["zeroed"], 1)
            split(1, 1)
            add(0, range(8), True)
            split(2, 0)
            add(1, range(8))
            with dve.Fori(1, NG // 2 - 1) as i:
                split(2 * i + 1, 1)
                add(2 * i, range(8))
                split(2 * i + 2, 0)
                add(2 * i + 1, range(8))
            split(NG - 1, 1)
            add(NG - 2, range(8))
            add(NG - 1, range(8))
            dve.wait_ge(sem["add_ok"], 8 * NG)
            dve.wait_ge(sem["bc_ok"], 2)
            sq = at[0][:, 0:2, :].rearrange("p a b -> p (a b)")
            for i in range(TT):
                chained(dve, dve_c, nc.vector.tensor_tensor(acc[:, i, :], acc[:, i, :], gate2[:, :], ALU.mult))
                chained(dve, dve_c, nc.vector.tensor_tensor(acc[:, i, :], acc[:, i, :], x2[:, i, :], ALU.add))
                chained(dve, dve_c, nc.vector.tensor_tensor_reduce(
                    out=sq, in0=acc[:, i, :], in1=acc[:, i, :], scale=1.0, scalar=0.0,
                    op0=ALU.mult, op1=ALU.add, accum_out=ssq[:, i:i + 1]))
            rstd_dve_in(nc, sem["ssq_ok"], ssq[:, :], fin[:, :], root[:, :])
            dve.wait_ge(sem["root_ok"], 1)
            rstd_dve_out(nc, dve, dve_c, root[:, :], fin[:, :])
            dve.wait_ge(sem["gf_in"], 16)
            for i in range(TT):
                nc.vector.scalar_tensor_tensor(acc[:, i, :], acc[:, i, :], root[:, i:i + 1], g_fin[:, :], ALU.mult, ALU.mult).then_inc(sem["y_ok"], 1)

        @block.tensor
        def _(pe):
            pe.wait_ge(sem["diag_ok"], KD)
            for c in range(KD):
                for x in range(2):
                    half = model_order(p_o[x][:, :], 2)
                    ins = nc.tensor.matmul(half[:, :, c], keep["ones"][:, :], diag[:, c, 2 * x * 32:(2 * x + 2) * 32], start=True, stop=True)
            ins.then_inc(sem["bc"], 1)
            pe.wait_ge(sem["bc_ok"], 2)

            def group(g, j, first=False):
                pe.wait_ge(sem["vlo_ok"], g + 1)
                pe.wait_ge(sem["wlo_ok"], g + 1)
                for n in range(8):
                    if not first:
                        pe.wait_ge(sem["add_ok"], 8 * g + n - 7)
                    ts, cs = slice(n // 2 * P, (n // 2 + 1) * P), slice(n % 2 * S, (n % 2 + 1) * S)
                    for x in range(GT):
                        ins = three(nc, p_o[n][:, :], (w_hi[j][:, x, ts], w_lo[j][:, x, ts]), (v_hi[j][:, x, cs], v_lo[j][:, x, cs]), x == 0, x == GT - 1)
                    ins.then_inc(sem["mm"], 1)

            group(0, 0, True)
            group(1, 1)
            with pe.Fori(1, NG // 2) as i:
                for j in range(2):
                    group(2 * i + j, j)


def program(nc, a, out, stop=99):
    with ExitStack() as top:
        k = Kit(nc, top, "keep", KEEP_AT)
        keep = {n: k.sb(n, shape) for n, shape in (
            ("ident", [P, P]), ("ones", [P, P]), ("invn", [P, 16]), ("eps", [P, 1]), ("cols", [P, V_ROWS]), ("mod", [P, 48]),
            ("scale1", [P, KD]), ("scale2", [P, KD]), ("csil", [P, KD]), ("neglam", [P, 1]), ("sinks", [P, 8]))}
        assert k.at <= LOW
        kh = Kit(nc, top, "h", H_AT)
        keep["h_hi"], keep["h_lo"] = (kh.sb(n, [P, KD, S], F32R) for n in ("hi", "lo"))
        phase_condition(nc, a, keep)
        if stop <= 1:
            return
        ky = Kit(nc, top, "y", Y_AT)
        y_hi, y_lo = (ky.sb(n, [P, NBR * CB, S], F32R) for n in ("hi", "lo"))
        xt = Kit(nc, top, "mixin", XT_AT).sb("xt", [P, 2 * MIX_BLOCKS, S])
        phase_project(nc, a, keep, xt, y_hi)
        if stop <= 2:
            return
        phase_mix(nc, a, keep, xt, *(y[:, :, :].rearrange("p (g c) t -> p g c t", c=CB) for y in (y_hi, y_lo)))
        if stop <= 3:
            return
        merged = Kit(nc, top, "y", MERGED_AT).sb("merged", [P, KD, S])
        phase_gate(nc, a, keep, y_hi, y_lo, merged)
        if stop <= 4:
            return
        x2 = Kit(nc, top, "x2", X2_AT).sb("x2", [P, TT, D])
        phase_out(nc, a, keep, merged, y_hi[:, 0:KD, :], y_hi[:, KD:, :], y_lo, x2)
        if stop <= 5:
            return
        scores = Kit(nc, top, "peer", Y_AT).sb("scores", [P, TT, 2 * PH, NK])
        phase_query(nc, a, keep, scores)
        if stop <= 6:
            return
        acts = nc.dram_tensor("expert_acts", [NE // P, P, S], F32, kind="Internal").ap()
        gates = nc.dram_tensor("expert_gates", [CHUNKS, P, P, CH], F32, kind="Internal").ap()
        phase_experts(nc, a, keep, scores, acts, gates)
        if stop <= 7:
            return
        phase_combine(nc, a, keep, acts, gates, x2, out)


_INS = ["x", "c", "w_ada", "b_ada", "g_norm1", "w_in", "lam_q1", "lam_k1", "lam_q2", "lam_k2", "g_subln", "conv_w", "w_pool",
        "pool_scale", "sinks", "w_branch", "w_o", "g_norm2", "w_q", "sub_keys", "u_experts", "v_experts", "g_final"]


def kernel(**inputs):
    import numpy as _np
    import concourse.bacc as _bacc
    from concourse import mybir as _mybir
    from concourse.bass_utils import run_bass_kernel_spmd as _run

    nc = _bacc.Bacc("TRN2", target_bir_lowering=False, num_devices=1)
    arrays, args = {}, {}
    for name in _INS:
        arr = _np.ascontiguousarray(inputs[name])
        arrays[f"in_{name}_dram"] = arr
        args[name] = nc.dram_tensor(f"in_{name}_dram", arr.shape, _mybir.dt.from_np(arr.dtype), kind="ExternalInput").ap()
    out = nc.dram_tensor("out_0_dram", (1, S, D), F32, kind="ExternalOutput").ap()
    program(nc, args, out)
    r = _run(nc, [arrays], core_ids=[0])
    return r.results[0]["out_0_dram"]
```

```python
from contextlib import ExitStack

import concourse.bass as bass
from concourse import mybir

P = 128
F32 = mybir.dt.float32
F32R = mybir.dt.float32r
BF16 = mybir.dt.bfloat16
U32 = mybir.dt.uint32
ALU = mybir.AluOpType
ACT = mybir.ActivationFunctionType
AX = mybir.AxisListType

EPS = 1e-6
NEG = -1e30
FLT_MAX = 3.4028234663852886e38
DOWN = 2.0 ** -60
UP = 2.0 ** -30
O_BOUND = 2.0 ** 66
SQ_DOWN = 2.0 ** -16
LAM_INIT = 0.2

D = 1024
S = 512
TT = S // P
KD = D // P
BW = 256
HALF = D // 2
CB = HALF // P
NBR = 4
HD = 64
HA = 4
IN_COLS = 8448
MIX_BLOCKS = 17
GATE_BLOCKS = 16
ADA_BLOCKS = 6 * D // BW
PH = 8
NK = 128
TOPK = 16
NE = NK * NK

V_C, V_ADA, V_G1, V_G2, V_CONV, V_POOL, V_SUB = 0, 8, 56, 64, 72, 84, 88
V_ROWS = 89
M_AQ, M_AK, M_AV, M_BB, M_BC, M_BX, M_CZ, M_DQ, M_DK, M_DV = 0, 4, 8, 12, 16, 20, 24, 28, 32, 33


class Count:

    def __init__(self, sem):
        self.sem = sem
        self.n = 0

    def inc(self, ins, by=1):
        ins.then_inc(self.sem, by)
        self.n += by
        return self.n


KB = 1024
KEEP_AT = 16512
LOW = KEEP_AT + 2 * KB
H_AT, Y_AT, XT_AT, X2_AT, MERGED_AT = LOW, LOW + 32 * KB, LOW + 96 * KB, LOW + 112 * KB, LOW + 128 * KB


class Kit:

    def __init__(self, nc, stack, tag, at):
        self.nc, self.stack, self.tag, self.at = nc, stack, tag, at

    def sb(self, name, shape, dt=F32):
        size = 2 if dt == BF16 else 4
        for n in shape[1:]:
            size *= n
        t = self.nc.alloc_sbuf_tensor_at(f"{self.tag}_{name}", shape, dt, offset=self.at)
        self.at += -(-size // 32) * 32
        return t

    def ps(self, name, shape, dt=F32):
        return self.stack.enter_context(self.nc.psum_tensor(f"{self.tag}_{name}", shape, dt))

    def sem(self, name):
        return self.stack.enter_context(self.nc.semaphore(f"{self.tag}_{name}"))

    def count(self, name):
        return Count(self.sem(name))


def rows_mm(nc, banks, ones, diag, ready):
    for j in range(2):
        ins = nc.tensor.matmul(banks[j][:, :], ones[:, :], diag[:, 4 * j:4 * j + 4, :].rearrange("p k n -> p (k n)"), start=True, stop=True)
    ins.then_inc(ready, 1)


def rows_out(nc, row, banks, ready):
    for j in range(2):
        nc.scalar.activation(row.rearrange("p (q m r) -> p m q r", q=4, m=KD)[:, 4 * j:4 * j + 4],
                             banks[j][:, :].rearrange("p (m q r) -> p m q r", m=4, q=4), ACT.Copy).then_inc(ready, 1)


def three(nc, out, w, x, first, last):
    nc.tensor.matmul(out, w[0], x[0], start=first, stop=False)
    nc.tensor.matmul(out, w[0], x[1], start=False, stop=False)
    return nc.tensor.matmul(out, w[1], x[0], start=False, stop=last)


def chained(eng, sig, ins):
    eng.wait_ge(sig.sem, sig.inc(ins))


def rstd_dve_in(nc, done, ssq, fin, out, most=FLT_MAX):
    nc.vector.tensor_scalar(fin, ssq, most, None, ALU.is_le).then_inc(done, 1)
    nc.vector.tensor_scalar(out, ssq, most, None, ALU.min).then_inc(done, 1)


def rstd_dve_out(nc, dve, sig, root, fin, ready=None):
    chained(dve, sig, nc.vector.reciprocal(root, root))
    last = nc.vector.scalar_tensor_tensor(root, root, UP, fin, ALU.mult, ALU.mult)
    if ready is None:
        chained(dve, sig, last)
    else:
        last.then_inc(ready, 1)


def model_order(x, q=4):
    return x.rearrange("p (q m r) -> p q m r", q=q, m=KD)


def h2_order(x):
    return x.rearrange("p (m q r) -> p q m r", q=4, m=KD)


def modulate(nc, out, coef, x, bank, ready, engine):
    scale, shift = coef
    for c in range(4 * bank, 4 * bank + 4):
        if engine == "act":
            ins = nc.scalar.activation(out[:, c, :], x[:, c, :], ACT.Identity, bias=shift[:, c:c + 1], scale=scale[:, c:c + 1])
        else:
            ins = nc.vector.tensor_scalar(out[:, c, :], x[:, c, :], scale[:, c:c + 1], shift[:, c:c + 1], ALU.mult, ALU.add)
        ins.then_inc(ready, 1)


def weight_parts(space):
    return space[:, :, :].rearrange("p (x a) b -> p x (a b)", x=4).rearrange("p x (k n) -> p x k n", k=KD)


def phase_condition(nc, a, keep, raw, w_in, space, w_hi_ok, w_lo_ok):
    with ExitStack() as stack:
        k = Kit(nc, stack, "cond", Y_AT)
        ring = [k.sb(f"ada{j}", [P, KD, S]) for j in range(4)]
        rows = k.sb("rows", [P, P])
        lamv = k.sb("lamv", [P, 4, HD])
        lamp = k.sb("lamp", [P, 2, HD])
        lams = k.sb("lams", [P, 4])
        x = k.sb("x", [P, TT, D])
        xn = k.sb("xn", [P, TT, D])
        sq = k.sb("sq", [P, D])
        ssq, fin, root = (k.sb(n, [P, TT]) for n in ("ssq", "fin", "root"))
        acc = k.sb("acc", [P, 2, D])
        hf = k.sb("hf", [P, KD, S])
        p_cols = k.ps("cols", [P, 512])
        p_mod = k.ps("mod", [P, 512])
        p_x = [k.ps(f"x{j}", [P, KD, P]) for j in range(2)]

        rows_in, lam_in, x_in = k.sem("rows_in"), k.sem("lam_in"), k.sem("x_in")
        ada_in = [k.sem(f"ada_in{j}") for j in range(4)]
        ada_last, blk_ok = k.sem("ada_last"), k.sem("blk_ok")
        const, cols_t, cols_ok, sil_ok, mod_mm = (k.sem(n) for n in ("const", "cols_t", "cols_ok", "sil_ok", "mod_mm"))
        lam_e, ssq_ok, root_ok, xn_ok, x_t, h_ok, hi_ok = (
            k.sem(n) for n in ("lam_e", "ssq_ok", "root_ok", "xn_ok", "x_t", "h_ok", "hi_ok"))
        coef_ok, lam_s, hv_ok, fac_ok = (k.sem(n) for n in ("coef_ok", "lam_s", "hv_ok", "fac_ok"))
        dve_c, pool_c, acc_c = k.count("dve_chain"), k.count("pool_chain"), k.count("acc_chain")
        ada = a["w_ada"][0].rearrange("(k p) n -> p k n", p=P)
        coef = (keep["scale1"], keep["mod"])
        w = a["w_in"][0].rearrange("(k p) n -> p k n", p=P)
        assert k.at <= XT_AT + 68 * KB
        w_parts = weight_parts(space)
        block = stack.enter_context(nc.Block())
        vectors = []
        r = 0
        for name, src in (("c", a["c"]), ("b_ada", a["b_ada"]), ("g_norm1", a["g_norm1"]), ("g_norm2", a["g_norm2"]),
                          ("conv_w", a["conv_w"].rearrange("l j n -> l (j n)")), ("pool_scale", a["pool_scale"]),
                          ("g_subln", a["g_subln"])):
            n = src.shape[1] // P
            plain = 2 * KD if name == "b_ada" else 0 if name == "g_norm2" else n
            if plain:
                vectors.append((rows[r:r + plain, :], src[0, 0:plain * P].rearrange("(m p) -> m p", p=P)))
            for m in range(plain, n, KD):
                vectors.append((rows[r + m:r + m + KD, :].rearrange("m (q r) -> m q r", q=4),
                                src[0, m * P:(m + KD) * P].rearrange("(q m r) -> m q r", q=4, m=KD)))
            r += n

        @block.sync
        def _(sp):
            sp.dma_start(x[:, :, :], a["x"][0].rearrange("(i p) d -> p i d", p=P)).then_inc(x_in, 16)
            sp.wait_ge(const, 5)
            for dst, src in vectors:
                sp.dma_start(dst, src).then_inc(rows_in, 16)
            for j in range(4):
                for half in range(2):
                    ks = slice(4 * half, 4 * half + 4)
                    sp.dma_start(ring[j][:, ks, :], ada[:, ks, j * S:(j + 1) * S]).then_inc(ada_last if j == 3 and half else ada_in[j], 16)
            for n, name in enumerate(("lam_q1", "lam_k1", "lam_q2", "lam_k2")):
                sp.dma_start(lamv[:, n, :], a[name].to_broadcast([P, HD])).then_inc(lam_in, 16)
            sp.dma_start(keep["sinks"][:, :], a["sinks"].to_broadcast([P, 8])).then_inc(lam_in, 16)
            for b in range(4):
                sp.dma_start(raw[b][:, :, :], w[:, :, b * BW:(b + 1) * BW]).then_inc(w_in[b], 16)
            sp.wait_ge(lam_in, 80)

        @block.gpsimd
        def _(pool):
            nc.gpsimd.memset(rows[:, :], 0.0).then_inc(const, 1)
            nc.gpsimd.memset(keep["eps"][:, :], EPS * DOWN).then_inc(const, 1)
            nc.gpsimd.memset(keep["ones"][:, :], 1.0).then_inc(const, 1)
            nc.gpsimd.memset(keep["inv_count"][:, :], 0.0).then_inc(const, 1)
            chained(pool, pool_c, nc.gpsimd.memset(keep["ident"][:, :], 0.0))
            nc.gpsimd.affine_select(out=keep["ident"][:, :], in_=keep["ident"][:, :], compare_op=ALU.not_equal, fill=1.0,
                                    base=0, pattern=[[-1, P]], channel_multiplier=1).then_inc(const, 1)

        @block.scalar
        def _(act):
            act.wait_ge(ssq_ok, 2)
            act.wait_ge(const, 5)
            nc.scalar.activation(root[:, :], root[:, :], ACT.Sqrt, bias=keep["eps"][:, :], scale=DOWN / D).then_inc(root_ok, 1)
            act.wait_ge(cols_ok, 1)
            nc.scalar.activation(keep["csil"][:, :], keep["cols"][:, V_C:V_C + KD], ACT.Silu).then_inc(sil_ok, 1)
            act.wait_ge(fac_ok, 1)
            for i in range(TT):
                nc.scalar.activation(xn[:, i, :], x[:, i, :], ACT.Copy, scale=root[:, i:i + 1]).then_inc(xn_ok, 1)
            act.wait_ge(lam_s, 2)
            nc.scalar.activation(lams[:, 2:4], lams[:, 0:2], ACT.Exp).then_inc(lam_e, 1)
            act.wait_ge(w_in[0], 16)
            act.wait_ge(acc_c.sem, KD)
            nc.scalar.activation(w_parts[:, 0], raw[0][:, :, :], ACT.Copy).then_inc(w_hi_ok, 1)
            act.wait_ge(coef_ok, 2)
            for i in range(TT):
                act.wait_ge(x_t, i + 1)
                ts = slice(i * P, (i + 1) * P)
                modulate(nc, hf[:, :, ts], coef, p_x[i % 2], 0, h_ok, "act")
                act.wait_ge(h_ok, 4 * i + 4)
                act.wait_ge(hv_ok, 4 * i + 4)
                nc.scalar.activation(keep["h_hi"][:, :, ts], hf[:, :, ts], ACT.Copy).then_inc(hi_ok, 1)

        @block.vector
        def _(dve):
            dve.wait_ge(x_in, 16)
            for i in range(TT):
                chained(dve, dve_c, nc.vector.tensor_tensor_reduce(
                    out=sq[:, :], in0=x[:, i, :], in1=x[:, i, :], scale=1.0, scalar=0.0,
                    op0=ALU.mult, op1=ALU.add, accum_out=ssq[:, i:i + 1]))
            rstd_dve_in(nc, ssq_ok, ssq[:, :], fin[:, :], root[:, :])
            dve.wait_ge(cols_t, 1)
            nc.vector.tensor_copy(keep["cols"][:, :], p_cols[:, 0:V_ROWS]).then_inc(cols_ok, 1)
            dve.wait_ge(root_ok, 1)
            rstd_dve_out(nc, dve, dve_c, root[:, :], fin[:, :], fac_ok)
            dve.wait_ge(sil_ok, 1)
            for b in (0, 2, 3):
                dve.wait_ge(ada_in[b], 32 if b < 3 else 16)
                o = acc[:, b // 2, b % 2 * S:(b % 2 + 1) * S]
                chained(dve, acc_c, nc.vector.tensor_scalar(o, ring[b][:, 0, :], keep["csil"][:, 0:1], None, ALU.mult))
                for c in range(1, KD):
                    if b == 3 and c == 4:
                        dve.wait_ge(ada_last, 16)
                    chained(dve, acc_c, nc.vector.scalar_tensor_tensor(o, ring[b][:, c, :], keep["csil"][:, c:c + 1], o, ALU.mult, ALU.add))
            dve.wait_ge(lam_in, 80)
            for n in range(2):
                nc.vector.tensor_tensor_reduce(
                    out=lamp[:, n, :], in0=lamv[:, 2 * n, :], in1=lamv[:, 2 * n + 1, :], scale=1.0, scalar=0.0,
                    op0=ALU.mult, op1=ALU.add, accum_out=lams[:, n:n + 1]).then_inc(lam_s, 1)
            dve.wait_ge(mod_mm, 1)
            nc.vector.tensor_tensor(keep["mod"][:, 0:2 * KD], p_mod[:, 0:2 * KD], keep["cols"][:, V_ADA:V_ADA + 2 * KD], ALU.add).then_inc(coef_ok, 1)
            dve.wait_ge(coef_ok, 1)
            nc.vector.scalar_tensor_tensor(keep["scale1"][:, :], keep["mod"][:, KD:2 * KD], 1.0, keep["cols"][:, V_G1:V_G1 + KD], ALU.add, ALU.mult).then_inc(coef_ok, 1)
            dve.wait_ge(coef_ok, 2)

            def low(i):
                dve.wait_ge(hi_ok, i + 1)
                ts = slice(i * P, (i + 1) * P)
                nc.vector.tensor_tensor(keep["h_lo"][:, :, ts], hf[:, :, ts], keep["h_hi"][:, :, ts].bitcast(F32), ALU.subtract)

            for i in range(TT):
                dve.wait_ge(x_t, i + 1)
                modulate(nc, hf[:, :, i * P:(i + 1) * P], coef, p_x[i % 2], 1, hv_ok, "dve")
                if i == 0:
                    dve.wait_ge(w_hi_ok, 1)
                    dve.wait_ge(blk_ok, 1)
                    nc.vector.tensor_tensor(w_parts[:, 2], raw[0][:, :, :], w_parts[:, 0].bitcast(F32), ALU.subtract).then_inc(w_lo_ok, 1)
                else:
                    low(i - 1)
            low(TT - 1)
            dve.wait_ge(lam_e, 1)
            chained(dve, dve_c, nc.vector.tensor_tensor(keep["neglam"][:, :], lams[:, 3:4], lams[:, 2:3], ALU.subtract))
            nc.vector.tensor_scalar(keep["neglam"][:, :], keep["neglam"][:, :], -LAM_INIT, None, ALU.add)

        @block.tensor
        def _(pe):
            pe.wait_ge(rows_in, len(vectors) * 16)
            pe.wait_ge(const, 5)
            nc.tensor.transpose(p_cols[:, 0:P], rows[:, :], keep["ident"][:, :]).then_inc(cols_t, 1)

            def transposes(i):
                pe.wait_ge(xn_ok, i + 1)
                for c in range(KD):
                    ins = nc.tensor.transpose(p_x[i % 2][:, c, :], xn[:, i, c * P:(c + 1) * P], keep["ident"][:, :])
                ins.then_inc(x_t, 1)

            transposes(0)
            transposes(1)
            for b in range(4):
                if b == 1:
                    pe.wait_ge(ada_in[1], 32)
                    for c in range(4):
                        for x in range(KD):
                            ins = nc.tensor.matmul(p_mod[:, 4 + c:5 + c], ring[1][:, x, c * P:(c + 1) * P], keep["csil"][:, x:x + 1], start=x == 0, stop=x == KD - 1)
                    ins.then_inc(blk_ok, 1)
                    continue
                pe.wait_ge(acc_c.sem, KD * max(b, 1))
                for c in range(4 * b, 4 * b + 4):
                    ins = nc.tensor.matmul(p_mod[:, c:c + 1], acc[:, c // KD, c % KD * P:(c % KD + 1) * P], keep["ones"][:, 0:1], start=True, stop=True)
            ins.then_inc(mod_mm, 1)
            for i in range(2, TT):
                pe.wait_ge(h_ok, 4 * i - 4)
                pe.wait_ge(hv_ok, 4 * i - 4)
                transposes(i)


def phase_project(nc, a, keep, xt, space, raw, w_in, hi_ok, lo_ok):
    with ExitStack() as stack:
        k = Kit(nc, stack, "proj", XT_AT + 100 * KB)
        parts = weight_parts(space)
        hi, lo = [parts[:, j] for j in (0, 1)], [parts[:, j] for j in (2, 3)]
        acc = [k.ps(f"acc{j}", [P, S]) for j in range(4)]
        share, ordered = k.sb("share", [P, D]), k.sb("ordered", [P, D])
        ka = Kit(nc, stack, "proj", Y_AT + 32 * KB)
        ring = [ka.sb(f"ada{j}", [P, KD, S]) for j in range(2)]
        p_mod = k.ps("mod", [P, 4 * KD])
        ada_in = [k.sem(f"ada_in{j}") for j in range(2)]
        share_ok, order_ok, mod_mm, mod_ok = (k.sem(n) for n in ("share_ok", "order_ok", "mod_mm", "mod_ok"))
        ada = a["w_ada"][0].rearrange("(k p) n -> p k n", p=P)
        mm, out_ok = k.sem("mm"), k.sem("out_ok")
        w = a["w_in"][0].rearrange("(k p) n -> p k n", p=P)
        NB = MIX_BLOCKS
        block = stack.enter_context(nc.Block())

        def cols(b):
            return w[:, :, bass.ds(b * BW, BW)]

        @block.sync
        def _(sp):
            for j in range(2):
                sp.dma_start(ring[j][:, :, :], ada[:, :, 2 * D + j * S:2 * D + (j + 1) * S]).then_inc(ada_in[j], 16)

            def load(b, j):
                sp.wait_ge(lo_ok, b - 3)
                sp.dma_start(raw[j][:, :, :], cols(b)).then_inc(w_in[j], 16)

            with sp.Fori(1, NB // 4) as i:
                for j in range(4):
                    load(4 * i + j, j)
                    if j >= 2:
                        sp.wait_ge(share_ok, 16 * i + 8 * (j - 1) - 16)
                        sp.dma_start(ring[j - 2][:, :, :], ada[:, :, bass.ds((4 + 2 * i + j - 2) * S, S)]).then_inc(ada_in[j - 2], 16)
            load(NB - 1, 0)

        def split_hi(act, b, j, turn, first=False):
            act.wait_ge(w_in[j], 16 * turn + 16)
            if not first:
                act.wait_ge(mm, 2 * b - 2)
            nc.scalar.activation(hi[j % 2][:, :, :], raw[j][:, :, :], ACT.Copy).then_inc(hi_ok, 1)

        @block.scalar
        def _(act):
            def store(b, j):
                for m in range(2):
                    act.wait_ge(mm, 2 * b + m + 1)
                    nc.scalar.activation(xt[:, bass.ds(2 * b + m, 1), :], acc[2 * (j % 2) + m][:, :], ACT.Copy).then_inc(out_ok, 1)

            split_hi(act, 1, 1, 0, True)
            store(0, 0)
            for b in range(1, 4):
                split_hi(act, b + 1, (b + 1) % 4, (b + 1) // 4)
                store(b, b)
            with act.Fori(1, NB // 4) as i:
                for j in range(4):
                    split_hi(act, 4 * i + j + 1, (j + 1) % 4, i + (j + 1) // 4)
                    store(4 * i + j, j)
            store(NB - 1, 0)

        @block.vector
        def _(dve):
            def split_lo(b, j):
                dve.wait_ge(hi_ok, b + 1)
                nc.vector.tensor_tensor(lo[j % 2][:, :, :], raw[j][:, :, :], hi[j % 2][:, :, :].bitcast(F32),
                                        ALU.subtract).then_inc(lo_ok, 1)

            def shares(i, steps):
                for n in steps:
                    x, c = n // KD, n % KD
                    o = share[:, x * S:(x + 1) * S]
                    if c == 0:
                        dve.wait_ge(ada_in[x], 16 * i + 16)
                        nc.vector.tensor_scalar(o, ring[x][:, 0, :], keep["csil"][:, 0:1], None, ALU.mult).then_inc(share_ok, 1)
                    else:
                        dve.wait_ge(share_ok, 16 * i + n)
                        nc.vector.scalar_tensor_tensor(o, ring[x][:, c, :], keep["csil"][:, c:c + 1], o, ALU.mult, ALU.add).then_inc(share_ok, 1)

            def turn(i, first=False):
                if not first:
                    split_lo(4 * i, 0)
                split_lo(4 * i + 1, 1)
                if not first:
                    dve.wait_ge(order_ok, i)
                shares(i, range(0, 5))
                split_lo(4 * i + 2, 2)
                shares(i, range(5, 11))
                split_lo(4 * i + 3, 3)
                shares(i, range(11, 16))
                dve.wait_ge(share_ok, 16 * i + 16)
                if not first:
                    dve.wait_ge(mod_mm, i)
                nc.vector.tensor_copy(h2_order(ordered[:, :]), model_order(share[:, :])).then_inc(order_ok, 1)

            turn(0, True)
            with dve.Fori(1, NB // 4) as i:
                turn(i)
            split_lo(NB - 1, 0)
            dve.wait_ge(mod_mm, 4)
            nc.vector.tensor_tensor(keep["mod"][:, 2 * KD:], p_mod[:, :], keep["cols"][:, V_ADA + 2 * KD:V_ADA + 6 * KD], ALU.add).then_inc(mod_ok, 1)
            dve.wait_ge(mod_ok, 1)
            nc.vector.scalar_tensor_tensor(keep["scale2"][:, :], keep["mod"][:, 4 * KD:5 * KD], 1.0, keep["cols"][:, V_G2:V_G2 + KD],
                                           ALU.add, ALU.mult).then_inc(mod_ok, 1)

        @block.tensor
        def _(pe):
            def product(b, j, first=False):
                pe.wait_ge(lo_ok, b + 1)
                for m in range(2):
                    if not first:
                        pe.wait_ge(out_ok, 2 * b + m - 3)
                    ms = slice(m * P, (m + 1) * P)
                    for c in range(KD):
                        ins = three(nc, acc[2 * (j % 2) + m][:, :], (hi[j % 2][:, c, ms], lo[j % 2][:, c, ms]),
                                    (keep["h_hi"][:, c, :], keep["h_lo"][:, c, :]), c == 0, c == KD - 1)
                    ins.then_inc(mm, 1)

            def section(i):
                pe.wait_ge(order_ok, i + 1)
                for m in range(KD):
                    ins = nc.tensor.matmul(p_mod[:, bass.ds(KD * i + m, 1)], ordered[:, m * P:(m + 1) * P], keep["ones"][:, 0:1], start=True, stop=True)
                ins.then_inc(mod_mm, 1)

            for b in range(4):
                product(b, b, b < 2)
            section(0)
            with pe.Fori(1, NB // 4) as i:
                for j in range(4):
                    product(4 * i + j, j)
                section(i)
            product(NB - 1, 0)
            pe.wait_ge(out_ok, 2 * NB)


def phase_mix(nc, a, keep, xt, y_hi, y_lo, tanhs):
    units = [u for i in range(TT) for u in [("A", i, h) for h in range(HA)] + [("B", i, g) for g in range(2)]]
    NU = len(units)
    with ExitStack() as stack:
        k = Kit(nc, stack, "mix", XT_AT + 68 * KB)
        vn = k.sb("vn", [P, TT, HA, P])
        dvn = k.sb("dvn", [P, TT, P])
        kd = k.sb("kd", [P, 2, S])
        sm = k.sb("sm", [P, 2, 1024])
        pt = k.sb("pt", [P, 2, 8, P])
        causal = k.sb("causal", [P, S])
        band = k.sb("band", [P, 2 * P])
        pad = [k.sb(f"pad{j}", [P, 16 + S]) for j in range(2)]
        rcount = k.sb("rcount", [P, 16])
        wpool = k.sb("wpool", [P, 4, P])
        small = {n: k.sb(n, [P, 2, 4]) for n in ("mx", "nm", "z", "r", "sd", "es")}
        ssq, fin, root = (k.sb(n, [P, 16]) for n in ("ssq", "fin", "root"))
        subg = k.sb("subg", [P, 1])
        p_s = [k.ps(f"s{j}", [P, 1024]) for j in range(2)]
        p_t = k.ps("t", [P, 8, P])
        p_o = k.ps("o", [P, S])
        p_w = k.ps("w", [P, S])
        kg = Kit(nc, stack, "gate_w", Y_AT)
        raw = [kg.sb(f"raw{j}", [P, KD, P]) for j in range(2)]
        kg.at = Y_AT + 16 * KB
        hi = [kg.sb(f"hi{j}", [P, KD, P], F32R) for j in range(2)]
        lo = [kg.sb(f"lo{j}", [P, KD, P], F32R) for j in range(2)]
        th = [kg.sb(f"th{j}", [P, S]) for j in range(2)]
        assert kg.at <= Y_AT + 40 * KB
        wg = a["w_in"][0].rearrange("(k p) n -> p k n", p=P)[:, :, MIX_BLOCKS * BW:]
        NG = NBR * KD
        names = ("g_in0 g_in1 g_hi g_lo g_mm th_ok th_out0 th_out1 masks small_in vt vn_ok sc stats exped normed tr pt_ok pv o_ok pool_d pw y2_ok conv_ok "
                 "ssq_ok root_ok on_ok yt y0_ok pads subg_ok").split()
        sem = {n: k.sem(n) for n in names}
        dve_c, pool_c = k.count("dve_chain"), k.count("pool_chain")
        block = stack.enter_context(nc.Block())
        scale = HD ** -0.5

        def width(u):
            kind, i, _ = u
            return (i + 1) * P if kind == "A" else (P if i == 0 else 2 * P)

        def group(n):
            kind = units[n][0]
            return 2 if kind == "A" else 4

        def view(t, n):
            m = group(n)
            return t.rearrange("p (m w) -> p m w", m=m)[:, :, 0:width(units[n])]

        def blocks(n):
            w = width(units[n]) // P
            return [(m, j) for m in range(1 if units[n][0] == "A" else 4) for j in range(w)]

        @block.sync
        def _(sp):
            for g in range(2):
                for half in range(2):
                    sp.dma_start(kd[half * HD:(half + 1) * HD, g, :], xt[g * HD:(g + 1) * HD, M_DK, :]).then_inc(sem["small_in"], 16)
            sp.dma_start(wpool[:, :, :], a["w_pool"][0].rearrange("g c e -> c g e")).then_inc(sem["small_in"], 16)

            def load(n):
                sp.dma_start(raw[n % 2][:, :, :], wg[:, :, n * P:(n + 1) * P]).then_inc(sem[f"g_in{n % 2}"], 16)

            load(0)
            load(1)
            for n in range(NG):
                if n + 2 < NG:
                    sp.wait_ge(sem["g_lo"], n + 1)
                    load(n + 2)
                sp.wait_ge(sem["th_ok"], n + 1)
                sp.dma_start(tanhs[n], th[n % 2][:, :]).then_inc(sem[f"th_out{n % 2}"], 16)
            for j in range(2):
                sp.wait_ge(sem[f"th_out{j}"], 16 * NG // 2)
            sp.wait_ge(sem["small_in"], 80)

        @block.gpsimd
        def _(pool):
            nc.gpsimd.memset(causal[:, :], 0.0).then_inc(sem["pads"], 1)
            nc.gpsimd.memset(band[:, :], 0.0).then_inc(sem["pads"], 1)
            nc.gpsimd.memset(pad[0][:, 0:16], 0.0).then_inc(sem["pads"], 1)
            nc.gpsimd.memset(pad[1][:, 0:16], 0.0).then_inc(sem["pads"], 1)
            pool.wait_ge(sem["pads"], 4)
            nc.gpsimd.affine_select(out=causal[:, :], in_=causal[:, :], compare_op=ALU.is_ge, fill=NEG, base=S - P,
                                    pattern=[[-1, S]], channel_multiplier=1).then_inc(sem["masks"], 1)
            chained(pool, pool_c, nc.gpsimd.affine_select(out=band[:, :], in_=band[:, :], compare_op=ALU.is_gt, fill=NEG, base=0,
                                                         pattern=[[1, 2 * P]], channel_multiplier=-1))
            nc.gpsimd.affine_select(out=band[:, :], in_=band[:, :], compare_op=ALU.is_ge, fill=NEG, base=P,
                                    pattern=[[-1, 2 * P]], channel_multiplier=1).then_inc(sem["masks"], 1)
            chained(pool, pool_c, nc.gpsimd.iota(rcount[:, :], pattern=[[1, 16]], base=1, channel_multiplier=0,
                                                 allow_small_or_imprecise_dtypes=True))
            nc.gpsimd.tensor_copy(keep["inv_count"][:, :], rcount[:, :]).then_inc(sem["pads"], 1)

            pool.wait_ge(sem["y2_ok"], 1)
            for g in range(4):
                w = 2 << g
                src, at = xt[:, M_CZ + g, :], 0
                chained(pool, pool_c, nc.gpsimd.tensor_copy(pad[0][:, 16:], src))
                for level in range(g + 1):
                    sh = 1 << level
                    chained(pool, pool_c, nc.gpsimd.tensor_tensor(pad[1 - at][:, 16:], pad[at][:, 16:], pad[at][:, 16 - sh:16 + S - sh], ALU.add))
                    at = 1 - at
                t = pad[at]
                nc.gpsimd.tensor_scalar(t[:, 16 + w:], t[:, 16 + w:], 1.0 / w, None, ALU.mult).then_inc(pool_c.sem, 1)
                nc.gpsimd.tensor_tensor(t[:, 16:16 + w], t[:, 16:16 + w], keep["inv_count"][:, 0:w], ALU.mult).then_inc(pool_c.sem, 1)
                pool_c.n += 2
                pool.wait_ge(pool_c.sem, pool_c.n)
                nc.gpsimd.tensor_tensor(src, t[:, 16:], src, ALU.subtract).then_inc(sem["pool_d"], 1)
                pool.wait_ge(sem["pool_d"], g + 1)

            z = xt[:, M_BX:M_BX + 4, :]
            chained(pool, pool_c, nc.gpsimd.tensor_tensor(z, z, xt[:, M_BC:M_BC + 4, :], ALU.mult))
            for c in range(CB):
                y, zc = xt[:, M_BC + c, :], xt[:, M_BX + c, :]
                taps = [keep["cols"][:, V_CONV + 4 * j + c:V_CONV + 4 * j + c + 1] for j in range(3)]
                chained(pool, pool_c, nc.gpsimd.tensor_scalar(y, zc, taps[2], None, ALU.mult))
                for back, tap in ((1, taps[1]), (2, taps[0])):
                    n = S - back
                    tmp = pad[back - 1][:, 16:16 + n]
                    chained(pool, pool_c, nc.gpsimd.tensor_scalar(tmp, zc[:, 0:n], tap, None, ALU.mult))
                    chained(pool, pool_c, nc.gpsimd.tensor_tensor(y[:, back:], y[:, back:], tmp, ALU.add))
                chained(pool, pool_c, nc.gpsimd.tensor_tensor(y, y, xt[:, M_BB + c, :], ALU.mult))
                chained(pool, pool_c, nc.gpsimd.tensor_copy(y_hi[:, 1, c, :], y))
                nc.gpsimd.tensor_tensor(y_lo[:, 1, c, :], y, y_hi[:, 1, c, :].bitcast(F32), ALU.subtract).then_inc(sem["conv_ok"], 1)
            pool.wait_ge(sem["conv_ok"], 4)

        def gate_bank(n):
            return p_w[:, :] if n < NU else p_t[:, 4 * (n % 2):4 * (n % 2) + 4, :].rearrange("p k n -> p (k n)")

        @block.scalar
        def _(act):
            act.wait_ge(sem["vt"], 1)
            nc.scalar.activation(vn[:, 0:2, :, :].rearrange("p i h e -> p (i h e)"), p_s[0][:, :], ACT.Copy).then_inc(sem["vn_ok"], 1)
            act.wait_ge(sem["vt"], 2)
            nc.scalar.activation(vn[:, 2:4, :, :].rearrange("p i h e -> p (i h e)"), p_s[1][:, :], ACT.Copy).then_inc(sem["vn_ok"], 1)
            act.wait_ge(sem["vt"], 3)
            nc.scalar.activation(dvn[:, :, :], p_t[:, 0:4, :], ACT.Copy).then_inc(sem["vn_ok"], 1)

            def exps(n):
                u, b = units[n], n % 2
                act.wait_ge(sem["stats"], n + 1)
                for m in range(group(n)):
                    t = view(sm[:, b, :], n)[:, m, :]
                    ins = nc.scalar.activation(t, t, ACT.Exp, bias=small["nm"][:, b, m:m + 1], accum_out=small["z"][:, b, m:m + 1])
                if u[0] == "B":
                    ins = nc.scalar.activation(small["es"][:, b, :], small["sd"][:, b, :], ACT.Exp)
                ins.then_inc(sem["exped"], 1)

            def split_hi(n):
                act.wait_ge(sem[f"g_in{n % 2}"], 16 * (n // 2) + 16)
                if n >= 2:
                    act.wait_ge(sem["g_mm"], n - 1)
                nc.scalar.activation(hi[n % 2][:, :, :], raw[n % 2][:, :, :], ACT.Copy).then_inc(sem["g_hi"], 1)

            def tanh(n):
                act.wait_ge(sem["g_mm"], n + 1)
                if n >= 2:
                    act.wait_ge(sem[f"th_out{n % 2}"], 16 * (n // 2))
                nc.scalar.activation(th[n % 2][:, :], gate_bank(n), ACT.Tanh, scale=0.5).then_inc(sem["th_ok"], 1)

            split_hi(0)
            exps(0)
            for n, (kind, i, h) in enumerate(units):
                if n + 1 < NU:
                    exps(n + 1)
                act.wait_ge(sem["tr"], n + 1)
                if n >= 2:
                    act.wait_ge(sem["pv"], n - 1)
                nb = len(blocks(n))
                nc.scalar.activation(pt[:, n % 2, 0:nb, :], p_t[:, 0:nb, :], ACT.Copy).then_inc(sem["pt_ok"], 1)
                split_hi(n + 1)
                tanh(n)
                act.wait_ge(sem["pv"], n + 1)
                if kind == "A":
                    nc.scalar.activation(xt[:, M_AV + i, h * P:(h + 1) * P], p_o[:, 0:P], ACT.Copy).then_inc(sem["o_ok"], 1)
                else:
                    nc.scalar.activation(xt[:, M_DQ + 2 * h:M_DQ + 2 * h + 2, i * P:(i + 1) * P],
                                         p_o[:, 0:2 * P].rearrange("p (m q) -> p m q", m=2), ACT.Copy).then_inc(sem["o_ok"], 1)
            for g in range(4):
                split_hi(NU + 1 + g)
                tanh(NU + g)
                act.wait_ge(sem["pw"], g + 1)
                nc.scalar.activation(xt[:, M_CZ + g, :], p_w[:, :], ACT.Copy, scale=keep["cols"][:, V_POOL + g:V_POOL + g + 1]).then_inc(sem["y2_ok"], 1)
            split_hi(NU + 5)
            tanh(NU + 4)
            act.wait_ge(sem["ssq_ok"], 2)
            nc.scalar.activation(root[:, :], root[:, :], ACT.Sqrt, bias=keep["eps"][:, :], scale=DOWN / SQ_DOWN / P).then_inc(sem["root_ok"], 1)
            act.wait_ge(sem["subg_ok"], 1)

            def head_out(h):
                act.wait_ge(sem["yt"], h + 1)
                nc.scalar.activation(xt[:, M_AQ + h, :], p_s[h % 2][:, 0:S], ACT.Copy, scale=subg[:, :]).then_inc(sem["y0_ok"], 1)

            split_hi(NU + 6)
            tanh(NU + 5)
            head_out(0)
            split_hi(NU + 7)
            head_out(1)
            tanh(NU + 6)
            head_out(2)
            tanh(NU + 7)
            head_out(3)

        @block.vector
        def _(dve):
            nc.vector.tensor_scalar(subg[:, :], keep["cols"][:, V_SUB:V_SUB + 1], 1.0 - LAM_INIT, None, ALU.mult).then_inc(sem["subg_ok"], 1)
            dve.wait_ge(sem["pads"], 5)
            nc.vector.reciprocal(keep["inv_count"][:, :], keep["inv_count"][:, :]).then_inc(sem["y2_ok"], 1)
            dve.wait_ge(sem["masks"], 2)

            def scores_in(n):
                (kind, i, h), b = units[n], n % 2
                m, w = group(n), width(units[n])
                t = view(sm[:, b, :], n)
                mask = causal[:, S - w:] if kind == "A" else band[:, 2 * P - w:]
                dve.wait_ge(sem["sc"], n + 1)
                if n >= 2:
                    dve.wait_ge(sem["tr"], n - 1)
                dve_c.inc(nc.vector.scalar_tensor_tensor(t, view(p_s[b][:, :], n), scale, mask.rearrange("p (o w) -> p o w", o=1).broadcast_to([P, m, w]),
                                                         ALU.mult, ALU.add))
                dve.wait_ge(dve_c.sem, dve_c.n)
                mx, nm = small["mx"][:, b, 0:m], small["nm"][:, b, 0:m]
                chained(dve, dve_c, nc.vector.reduce_max(mx, t, AX.X))
                if kind == "B":
                    sink = keep["sinks"][:, 4 * h:4 * h + 4].rearrange("p (pair odd) -> p odd pair", odd=2)
                    mx2, sd2 = (small[x][:, b, :].rearrange("p (odd pair) -> p odd pair", odd=2) for x in ("mx", "sd"))
                    chained(dve, dve_c, nc.vector.tensor_tensor(mx2, mx2, sink, ALU.max))
                    chained(dve, dve_c, nc.vector.tensor_tensor(sd2, sink, mx2, ALU.subtract))
                nc.vector.tensor_scalar(nm, mx, -1.0, None, ALU.mult).then_inc(sem["stats"], 1)

            def normalise(n):
                (kind, i, h), b = units[n], n % 2
                t = view(sm[:, b, :], n)
                z, r = small["z"][:, b, :], small["r"][:, b, :]
                dve.wait_ge(sem["exped"], n + 1)
                if kind == "A":
                    chained(dve, dve_c, nc.vector.reciprocal(r[:, 0:2], z[:, 0:2]))
                    chained(dve, dve_c, nc.vector.tensor_tensor(r[:, 1:2], r[:, 1:2], keep["neglam"][:, :], ALU.mult))
                    chained(dve, dve_c, nc.vector.tensor_scalar(t[:, 0, :], t[:, 0, :], r[:, 0:1], None, ALU.mult))
                    nc.vector.scalar_tensor_tensor(t[:, 0, :], t[:, 1, :], r[:, 1:2], t[:, 0, :], ALU.mult, ALU.add).then_inc(sem["normed"], 1)
                else:
                    chained(dve, dve_c, nc.vector.tensor_tensor(z, z, small["es"][:, b, :], ALU.add))
                    chained(dve, dve_c, nc.vector.reciprocal(r, z))
                    nc.vector.tensor_tensor(t, t, r.rearrange("p (m o) -> p m o", o=1).broadcast_to([P, 4, width(units[n])]),
                                            ALU.mult).then_inc(sem["normed"], 1)

            def split_lo(n):
                dve.wait_ge(sem["g_hi"], n + 1)
                nc.vector.tensor_tensor(lo[n % 2][:, :, :], raw[n % 2][:, :, :], hi[n % 2][:, :, :].bitcast(F32), ALU.subtract).then_inc(sem["g_lo"], 1)

            scores_in(0)
            split_lo(0)
            for n in range(NU):
                if n + 1 < NU:
                    scores_in(n + 1)
                normalise(n)
                split_lo(n + 1)
            dve.wait_ge(sem["o_ok"], NU)
            dve.wait_ge(sem["tr"], NU)
            o = xt[:, M_AV:M_AV + 4, :].rearrange("p i (h e) -> p (i h) e", e=P)
            sq = sm[:, :, :].rearrange("p b (x e) -> p (b x) e", e=P)
            chained(dve, dve_c, nc.vector.tensor_scalar(sq, o, O_BOUND, -O_BOUND, ALU.min, ALU.max))
            split_lo(NU + 1)
            chained(dve, dve_c, nc.vector.scalar_tensor_tensor(sq, sq, SQ_DOWN, sq, ALU.mult, ALU.mult))
            chained(dve, dve_c, nc.vector.reduce_sum(ssq[:, :], sq, AX.X))
            split_lo(NU + 2)
            rstd_dve_in(nc, sem["ssq_ok"], ssq[:, :], fin[:, :], root[:, :], FLT_MAX * SQ_DOWN)
            for n in range(NU + 3, NU + 6):
                split_lo(n)
            dve.wait_ge(sem["root_ok"], 1)
            rstd_dve_out(nc, dve, dve_c, root[:, :], fin[:, :])
            nc.vector.tensor_tensor(o, o, root[:, :].rearrange("p (x o) -> p x o", o=1).broadcast_to([P, 16, P]),
                                    ALU.mult).then_inc(sem["on_ok"], 1)
            split_lo(NU + 6)
            split_lo(NU + 7)

        @block.tensor
        def _(pe):
            ident = keep["ident"][:, :]
            for half in range(2):
                for j in range(8):
                    i, h = 2 * half + j // 4, j % 4
                    ins = nc.tensor.transpose(p_s[half][:, j * P:(j + 1) * P], xt[:, M_AV + h, i * P:(i + 1) * P], ident)
                ins.then_inc(sem["vt"], 1)
            for i in range(TT):
                ins = nc.tensor.transpose(p_t[:, i, :], xt[:, M_DV, i * P:(i + 1) * P], ident)
            ins.then_inc(sem["vt"], 1)
            pe.wait_ge(sem["small_in"], 80)

            def scores(n):
                kind, i, h = units[n]
                if n < 2:
                    pe.wait_ge(sem["vn_ok"], n + 1)
                else:
                    pe.wait_ge(sem["stats"], n - 1)
                out = view(p_s[n % 2][:, :], n)
                qs = slice(i * P, (i + 1) * P)
                for m in range(group(n)):
                    if kind == "A":
                        rows = slice(m * HD, (m + 1) * HD)
                        q, kk = xt[rows, M_AQ + h, qs], xt[rows, M_AK + h, 0:(i + 1) * P]
                    else:
                        rows = slice(m // 2 * HD, (m // 2 + 1) * HD)
                        q, kk = xt[rows, M_DQ + 2 * h + m % 2, qs], kd[rows, h, max(0, (i - 1) * P):(i + 1) * P]
                    ins = nc.tensor.matmul(out[:, m, :], q, kk, start=True, stop=True)
                ins.then_inc(sem["sc"], 1)

            def gate_product(n):
                pe.wait_ge(sem["g_lo"], n + 1)
                if n:
                    pe.wait_ge(sem["th_ok"], n if n < NU else n - 1)
                for c in range(KD):
                    ins = three(nc, gate_bank(n), (hi[n % 2][:, c, :], lo[n % 2][:, c, :]),
                                (keep["h_hi"][:, c, :], keep["h_lo"][:, c, :]), c == 0, c == KD - 1)
                ins.then_inc(sem["g_mm"], 1)

            scores(0)
            scores(1)
            for n, (kind, i, h) in enumerate(units):
                pe.wait_ge(sem["normed"], n + 1)
                if n == 0:
                    pe.wait_ge(sem["vn_ok"], 3)
                else:
                    pe.wait_ge(sem["pt_ok"], n)
                for x, (m, j) in enumerate(blocks(n)):
                    ins = nc.tensor.transpose(p_t[:, x, :], view(sm[:, n % 2, :], n)[:, m, j * P:(j + 1) * P], ident)
                ins.then_inc(sem["tr"], 1)
                if n + 2 < NU:
                    scores(n + 2)
                gate_product(n)
                pe.wait_ge(sem["pt_ok"], n + 1)
                if n >= 1:
                    pe.wait_ge(sem["o_ok"], n)
                w = width(units[n]) // P
                for x, (m, j) in enumerate(blocks(n)):
                    if kind == "A":
                        ins = nc.tensor.matmul(p_o[:, 0:P], pt[:, n % 2, x, :], vn[:, j, h, :], start=j == 0, stop=j == w - 1)
                    else:
                        at = m // 2 * HD
                        ins = nc.tensor.matmul(p_o[at:at + HD, m % 2 * P:(m % 2 + 1) * P], dvn[:, i + 1 - w + j, h * HD:(h + 1) * HD],
                                               pt[:, n % 2, x, :], start=j == 0, stop=j == w - 1)
                ins.then_inc(sem["pv"], 1)
            pe.wait_ge(sem["pt_ok"], NU)
            for g in range(4):
                gate_product(NU + g)
                pe.wait_ge(sem["pool_d"], g + 1)
                if g:
                    pe.wait_ge(sem["y2_ok"], g + 1)
                else:
                    pe.wait_ge(sem["th_ok"], NU)
                nc.tensor.matmul(p_w[:, :], wpool[:, g, :], xt[:, M_CZ + g, :], start=True, stop=True).then_inc(sem["pw"], 1)
            gate_product(NU + 4)
            gate_product(NU + 5)
            pe.wait_ge(sem["on_ok"], 1)
            for h in range(HA):
                if h >= 2:
                    gate_product(NU + 4 + h)
                    pe.wait_ge(sem["y0_ok"], h - 1)
                for i in range(TT):
                    ins = nc.tensor.transpose(p_s[h % 2][:, i * P:(i + 1) * P], xt[:, M_AV + i, h * P:(h + 1) * P], ident)
                ins.then_inc(sem["yt"], 1)


def phase_gate(nc, a, keep, xt, y_hi, y_lo, tanhs, m_hi, m_lo, gate1, gate2_row, w_o, wo_in, x2, x_in):
    with ExitStack() as stack:
        merged = Kit(nc, stack, "gate", MERGED_AT).sb("merged", [P, KD, S])
        k = Kit(nc, stack, "gate", MERGED_AT + 36 * KB)
        diag = k.sb("diag", [P, KD, P])
        raw = [k.sb(f"raw{j}", [P, CB, BW]) for j in range(2)]
        hi = [k.sb(f"hi{j}", [P, CB, BW], F32R) for j in range(2)]
        lo = [k.sb(f"lo{j}", [P, CB, BW], F32R) for j in range(2)]
        th = [k.sb(f"th{j}", [P, 2, S]) for j in range(2)]
        part = [k.sb(f"part{j}", [P, S]) for j in range(2)]
        gate2 = diag[:, :, :].rearrange("p k n -> p (k n)")
        p_b = [k.ps(f"b{j}", [P, S]) for j in range(4)]
        p_r = [k.ps(f"r{j}", [P, S]) for j in range(2)]
        names = "b_in0 b_in1 t_in0 t_in1 y_hi_ok y_lo_ok hi_ok lo_ok mm part_ok add_ok m_hi_ok diag_ok bc bc_ok row_out".split()
        sem = {n: k.sem(n) for n in names}
        wb = a["w_branch"][0].rearrange("g (k p) n -> p (g k) n", p=P)
        wo = a["w_o"][0].rearrange("(k p) n -> p k n", p=P)
        block = stack.enter_context(nc.Block())

        def branch(r):
            return 0 if isinstance(r, int) and r == NBR - 1 else r + 1

        @block.sync
        def _(sp):
            def load(r, d, wait=True):
                s, g, j = 4 * r + d, branch(r), d % 2
                if wait:
                    sp.wait_ge(sem["lo_ok"], s - 1)
                sp.dma_start(raw[j][:, :, :], wb[:, bass.ds(4 * g, CB), d * BW:(d + 1) * BW]).then_inc(sem[f"b_in{j}"], 16)
                if wait:
                    sp.wait_ge(sem["part_ok"], 2 * s - 2)
                sp.dma_start(th[j][:, :, :], tanhs[bass.ds(KD * g + 2 * d, 2)].rearrange("m p t -> p m t")).then_inc(sem[f"t_in{j}"], 16)

            for d in range(4):
                load(0, d, d >= 2)
            with sp.Fori(1, NBR - 1) as r:
                for d in range(4):
                    load(r, d)
                    at = bass.ds((4 * r + d - 4) * P, P)
                    sp.dma_start(w_o[:, :, at], wo[:, :, at]).then_inc(wo_in, 16)
            for d in range(4):
                load(NBR - 1, d)
                sp.dma_start(x2[:, d, :], a["x"][0, d * P:(d + 1) * P, :]).then_inc(x_in, 16)
            sp.wait_ge(sem["bc_ok"], 4)
            sp.dma_start(gate2_row, gate2[0:1, :]).then_inc(sem["row_out"], 16)
            sp.wait_ge(sem["row_out"], 16)

        @block.scalar
        def _(act):
            def split(r, d, wait=True):
                s, j = 4 * r + d, d % 2
                act.wait_ge(sem[f"b_in{j}"], (2 * r + d // 2) * 16 + 16)
                if wait:
                    act.wait_ge(sem["mm"], 2 * s - 2)
                nc.scalar.activation(hi[j][:, :, :], raw[j][:, :, :], ACT.Copy).then_inc(sem["hi_ok"], 1)

            def y_part(g, m):
                nc.scalar.activation(y_hi[:, CB * g:CB * g + CB, :], xt[:, m:m + CB, :], ACT.Copy).then_inc(sem["y_hi_ok"], 1)

            def diagonals(at):
                for c in range(KD):
                    nc.scalar.activation(diag[:, c, :], keep["ident"][:, :], ACT.Copy, scale=keep["mod"][:, at + c:at + c + 1]).then_inc(sem["diag_ok"], 1)

            split(0, 0, False)
            split(0, 1, False)
            y_part(2, M_CZ)
            split(0, 2)
            y_part(3, M_DQ)
            split(0, 3)
            y_part(0, M_AQ)
            diagonals(2 * KD)
            with act.Fori(1, NBR - 1) as r:
                for d in range(4):
                    split(r, d)
            act.wait_ge(sem["bc"], 1)
            rows_out(nc, gate1[:, :], p_r, sem["bc_ok"])
            diagonals(5 * KD)
            split(NBR - 1, 0)
            for d in range(4):
                if d < 3:
                    split(NBR - 1, d + 1)
                if d == 2:
                    act.wait_ge(sem["bc"], 2)
                    rows_out(nc, gate2, p_r, sem["bc_ok"])
                act.wait_ge(sem["add_ok"], 2 * (4 * (NBR - 2) + d) + 2)
                nc.scalar.activation(m_hi[:, 2 * d:2 * d + 2, :], merged[:, 2 * d:2 * d + 2, :], ACT.Copy, scale=0.5).then_inc(sem["m_hi_ok"], 1)

        @block.vector
        def _(dve):
            def split(r, d):
                dve.wait_ge(sem["hi_ok"], 4 * r + d + 1)
                nc.vector.tensor_tensor(lo[d % 2][:, :, :], raw[d % 2][:, :, :], hi[d % 2][:, :, :].bitcast(F32), ALU.subtract).then_inc(sem["lo_ok"], 1)

            def y_part(n, g, m):
                dve.wait_ge(sem["y_hi_ok"], n + 1)
                ys = slice(CB * g, CB * g + CB)
                nc.vector.tensor_tensor(y_lo[:, ys, :], xt[:, m:m + CB, :], y_hi[:, ys, :].bitcast(F32), ALU.subtract).then_inc(sem["y_lo_ok"], 1)

            def weigh(r, d, first=False):
                s = 4 * r + d
                dve.wait_ge(sem[f"t_in{d % 2}"], (2 * r + d // 2) * 16 + 16)
                for m in range(2):
                    dve.wait_ge(sem["mm"], 2 * s + m + 1)
                    if not first and not (isinstance(r, int) and r == 1 and d == 0):
                        dve.wait_ge(sem["add_ok"], 2 * (s - 4) + m - 1)
                    o = merged[:, 2 * d + m, :] if first else part[m][:, :]
                    nc.vector.scalar_tensor_tensor(o, th[d % 2][:, m, :], 1.0, p_b[2 * (d % 2) + m][:, :], ALU.add, ALU.mult).then_inc(sem["part_ok"], 1)

            def low(d):
                dve.wait_ge(sem["m_hi_ok"], d + 1)
                cs = slice(2 * d, 2 * d + 2)
                nc.vector.scalar_tensor_tensor(m_lo[:, cs, :], merged[:, cs, :], 0.5, m_hi[:, cs, :].bitcast(F32), ALU.mult, ALU.subtract)

            def turn(r, first=False):
                for d in range(4):
                    split(r, d + 1) if d < 3 else split(r + 1, 0)
                    if first and d < 3:
                        y_part(d, (2, 3, 0)[d], (M_CZ, M_DQ, M_AQ)[d])
                    weigh(r, d, first)

            split(0, 0)
            turn(0, True)
            turn(1)
            with dve.Fori(2, NBR - 1) as r:
                turn(r)
            for d in range(4):
                if d < 3:
                    split(NBR - 1, d + 1)
                weigh(NBR - 1, d)
                if d:
                    low(d - 1)
            low(3)

        @block.gpsimd
        def _(pool):
            def add(r, d):
                for m in range(2):
                    pool.wait_ge(sem["part_ok"], 2 * (4 * r + d) + m + 1)
                    c = 2 * d + m
                    nc.gpsimd.tensor_tensor(merged[:, c, :], merged[:, c, :], part[m][:, :], ALU.add).then_inc(sem["add_ok"], 1)

            with pool.Fori(1, NBR) as r:
                for d in range(4):
                    add(r, d)

        @block.tensor
        def _(pe):
            def product(r, d, first=False):
                s, g, j = 4 * r + d, branch(r), d % 2
                pe.wait_ge(sem["lo_ok"], s + 1)
                for m in range(2):
                    if not first:
                        pe.wait_ge(sem["part_ok"], 2 * s + m - 3)
                    ms = slice(m * P, (m + 1) * P)
                    for c in range(CB):
                        ins = three(nc, p_b[2 * j + m][:, :], (hi[j][:, c, ms], lo[j][:, c, ms]),
                                    (y_hi[:, bass.ds(4 * g + c, 1), :], y_lo[:, bass.ds(4 * g + c, 1), :]), c == 0, c == CB - 1)
                    ins.then_inc(sem["mm"], 1)

            for d in range(4):
                product(0, d, d < 2)
            pe.wait_ge(sem["y_lo_ok"], 3)
            pe.wait_ge(sem["diag_ok"], KD)
            rows_mm(nc, p_r, keep["ones"], diag, sem["bc"])
            with pe.Fori(1, NBR - 1) as r:
                for d in range(4):
                    product(r, d)
            for d in range(4):
                product(NBR - 1, d)
                if d == 0:
                    pe.wait_ge(sem["diag_ok"], 2 * KD)
                    pe.wait_ge(sem["bc_ok"], 2)
                    rows_mm(nc, p_r, keep["ones"], diag, sem["bc"])


def phase_out(nc, keep, m_hi, m_lo, gate1, raw, w_in, x2, x_in, ahead):
    with ExitStack() as stack:
        kw = Kit(nc, stack, "out", Y_AT)
        hi, lo = kw.sb("hi", [P, KD, D], F32R), kw.sb("lo", [P, KD, D], F32R)
        hf = Kit(nc, stack, "out", MERGED_AT).sb("hf", [P, KD, S])
        k = Kit(nc, stack, "out", MERGED_AT + 36 * KB)
        mixed = [k.sb(f"mixed{j}", [P, BW]) for j in range(2)]
        xn = k.sb("xn", [P, 2, D])
        sq = k.sb("sq", [P, D])
        ssq, fin, root = (k.sb(n, [P, TT]) for n in ("ssq", "fin", "root"))
        assert k.at <= X2_AT + 76 * KB
        acc = [k.ps(f"acc{j}", [P, S]) for j in range(4)]
        p_x = [k.ps(f"x{j}", [P, KD, P]) for j in range(2)]
        coef = (keep["scale2"], keep["mod"][:, 3 * KD:4 * KD])
        names = "hv_ok hi_ok lo_ok mm x2_ok ssq_ok root_ok xn_ok x_t h_ok h_hi_ok".split()
        sem = {n: k.sem(n) for n in names}
        dve_c = k.count("dve_chain")
        NB = D // BW
        block = stack.enter_context(nc.Block())

        pieces = [(slice(0, KD // 2), slice(0, BW)), (slice(KD // 2, KD), slice(0, BW))]
        pieces += [(slice(0, KD), slice(b * BW, (b + 1) * BW)) for b in range(1, NB)]

        @block.sync
        def _(sp):
            ahead(sp)

        @block.scalar
        def _(act):
            act.wait_ge(w_in, 16 * D // P)
            for cs, bs in pieces:
                nc.scalar.activation(hi[:, cs, bs], raw[:, cs, bs], ACT.Copy).then_inc(sem["hi_ok"], 1)
            for i in range(TT):
                r = root[:, i:i + 1]
                act.wait_ge(sem["ssq_ok"], 2 * i + 2)
                nc.scalar.activation(r, r, ACT.Sqrt, bias=keep["eps"][:, :], scale=DOWN / D).then_inc(sem["root_ok"], 1)
                act.wait_ge(sem["x_t"], i + 1)
                ts = slice(i * P, (i + 1) * P)
                modulate(nc, hf[:, :, ts], coef, p_x[i % 2], 0, sem["h_ok"], "act")
                act.wait_ge(sem["h_ok"], 4 * i + 4)
                act.wait_ge(sem["hv_ok"], 4 * i + 4)
                nc.scalar.activation(keep["h_hi"][:, :, ts], hf[:, :, ts], ACT.Copy).then_inc(sem["h_hi_ok"], 1)

        @block.vector
        def _(dve):
            for n, (cs, bs) in enumerate(pieces):
                dve.wait_ge(sem["hi_ok"], n + 1)
                nc.vector.tensor_tensor(lo[:, cs, bs], raw[:, cs, bs], hi[:, cs, bs].bitcast(F32), ALU.subtract).then_inc(sem["lo_ok"], 1)
            dve.wait_ge(x_in, 16 * TT)

            def low(i):
                dve.wait_ge(sem["h_hi_ok"], i + 1)
                ts = slice(i * P, (i + 1) * P)
                nc.vector.tensor_tensor(keep["h_lo"][:, :, ts], hf[:, :, ts], keep["h_hi"][:, :, ts].bitcast(F32), ALU.subtract)

            def add(i):
                for b in range(NB):
                    n = NB * i + b
                    bs = slice(b * BW, (b + 1) * BW)
                    dve.wait_ge(sem["mm"], n + 1)
                    chained(dve, dve_c, nc.vector.tensor_tensor(mixed[b % 2][:, :], acc[b][:, 0:BW], gate1[:, bs], ALU.mult))
                    nc.vector.tensor_tensor(x2[:, i, bs], x2[:, i, bs], mixed[b % 2][:, :], ALU.add).then_inc(sem["x2_ok"], 1)
                dve.wait_ge(sem["x2_ok"], NB * (i + 1))
                chained(dve, dve_c, nc.vector.tensor_tensor_reduce(
                    out=sq[:, :], in0=x2[:, i, :], in1=x2[:, i, :], scale=1.0, scalar=0.0,
                    op0=ALU.mult, op1=ALU.add, accum_out=ssq[:, i:i + 1]))
                rstd_dve_in(nc, sem["ssq_ok"], ssq[:, i:i + 1], fin[:, i:i + 1], root[:, i:i + 1])

            def norm(i):
                dve.wait_ge(sem["root_ok"], i + 1)
                rstd_dve_out(nc, dve, dve_c, root[:, i:i + 1], fin[:, i:i + 1])
                if i >= 2:
                    dve.wait_ge(sem["x_t"], i - 1)
                nc.vector.tensor_scalar(h2_order(xn[:, i % 2, :]), model_order(x2[:, i, :]), root[:, i:i + 1], None, ALU.mult).then_inc(sem["xn_ok"], 1)

            def shift(i):
                dve.wait_ge(sem["x_t"], i + 1)
                modulate(nc, hf[:, :, i * P:(i + 1) * P], coef, p_x[i % 2], 1, sem["hv_ok"], "dve")

            for i in range(TT):
                add(i)
                norm(i)
                if i:
                    low(i - 1)
                shift(i)
            low(TT - 1)

        @block.tensor
        def _(pe):
            def transposes(i):
                pe.wait_ge(sem["xn_ok"], i + 1)
                if i >= 2:
                    pe.wait_ge(sem["h_ok"], 4 * i - 4)
                    pe.wait_ge(sem["hv_ok"], 4 * i - 4)
                for c in range(KD):
                    ins = nc.tensor.transpose(p_x[i % 2][:, c, :], xn[:, i % 2, c * P:(c + 1) * P], keep["ident"][:, :])
                ins.then_inc(sem["x_t"], 1)

            for i in range(TT):
                ts = slice(i * P, (i + 1) * P)
                for b in range(NB):
                    if i:
                        pe.wait_ge(sem["x2_ok"], NB * (i - 1) + b + 1)
                    bs = slice(b * BW, (b + 1) * BW)
                    for c in range(KD):
                        if i == 0 and (b, c) == (0, 0):
                            pe.wait_ge(sem["lo_ok"], 1)
                        elif i == 0 and c == (0 if b else KD // 2):
                            pe.wait_ge(sem["lo_ok"], b + 2)
                        ins = three(nc, acc[b][:, 0:BW], (m_hi[:, c, ts], m_lo[:, c, ts]), (hi[:, c, bs], lo[:, c, bs]), c == 0, c == KD - 1)
                    ins.then_inc(sem["mm"], 1)
                    if i and b == 2:
                        transposes(i - 1)
            transposes(TT - 1)


def load_queries(sp, a, raw, w_in, b):
    w = a["w_q"][0].rearrange("(q m r) n -> q r m n", q=4, m=KD)
    for x in range(4):
        sp.dma_start(raw[32 * x:32 * x + 32, :, :], w[x, :, :, bass.ds(b * BW, BW)]).then_inc(w_in, 16)


def load_experts(sp, a, raw, u_in, n):
    u = a["u_experts"][0].rearrange("(b m r) (q c) -> b q r m c", m=8, r=32, q=4)
    for q in range(4):
        sp.dma_start(raw[32 * q:32 * q + 32, :, :], u[bass.ds(n, 1), q].rearrange("o r m c -> (o r) m c")).then_inc(u_in, 16)


def expert_groups(a, acts):
    return a["v_experts"][0].rearrange("(g x p) d -> g p x d", x=GT, p=P), acts.rearrange("(g x) p t -> g p x t", x=GT)


def phase_query(nc, a, keep, scores, raw, w_in, ahead):
    with ExitStack() as stack:
        k = Kit(nc, stack, "query", X2_AT + 16 * KB)
        hi = [k.sb(f"hi{j}", [P, KD, BW], F32R) for j in range(2)]
        lo = [k.sb(f"lo{j}", [P, KD, BW], F32R) for j in range(2)]
        q = [k.sb(f"q{j}", [P, S]) for j in range(2)]
        keys = k.sb("keys", [P, 2, P])
        keys_t = k.sb("keys_t", [P, 2, P])
        acc = [k.ps(f"acc{j}", [P, S]) for j in range(4)]
        p_s = [k.ps(f"s{j}", [P, TT, P]) for j in range(2)]
        p_k = k.ps("k", [P, 2, P])
        names = "keys_in kt kt_ok hi_ok lo_ok mm q_ok sc s_ok".split()
        sem = {n: k.sem(n) for n in names}
        block = stack.enter_context(nc.Block())

        halves = (slice(0, KD // 2), slice(KD // 2, KD))
        @block.sync
        def _(sp):
            sp.dma_start(keys[:, :, :], a["sub_keys"][0].rearrange("s n d -> n s d")).then_inc(sem["keys_in"], 16)

            ahead(sp)
            with sp.Fori(1, PH // 2) as i:
                for j in range(2):
                    sp.wait_ge(sem["lo_ok"], 2 * i + j)
                    load_queries(sp, a, raw[j], w_in[j], 2 * i + j)

        @block.scalar
        def _(act):
            def split(b, j, turn, first=False):
                act.wait_ge(w_in[j], 64 * turn + 64)
                if not first:
                    act.wait_ge(sem["mm"], 2 * b - 2)
                nc.scalar.activation(hi[j][:, :, :], raw[j][:, :, :], ACT.Copy).then_inc(sem["hi_ok"], 1)

            def queries(b, j, first=False):
                for m in range(2):
                    act.wait_ge(sem["mm"], 2 * b + m + 1)
                    if not first:
                        act.wait_ge(sem["sc"], 2 * b + m - 1)
                    nc.scalar.activation(q[m][:, :], acc[2 * j + m][:, :], ACT.Copy).then_inc(sem["q_ok"], 1)

            act.wait_ge(w_in[0], 64)
            for ks in halves:
                nc.scalar.activation(hi[0][:, ks, :], raw[0][:, ks, :], ACT.Copy).then_inc(sem["hi_ok"], 1)
            split(1, 1, 0, True)
            act.wait_ge(sem["kt"], 1)
            nc.scalar.activation(keys_t[:, :, :], p_k[:, :, :], ACT.Copy).then_inc(sem["kt_ok"], 1)
            queries(0, 0, True)
            split(2, 0, 1)
            queries(1, 1)
            with act.Fori(1, PH // 2 - 1) as i:
                for j in range(2):
                    split(2 * i + j + 1, 1 - j, i + j)
                    queries(2 * i + j, j)
            split(PH - 1, 1, PH // 2 - 1)
            queries(PH - 2, 0)
            queries(PH - 1, 1)

        @block.vector
        def _(dve):
            def split(b, j):
                dve.wait_ge(sem["hi_ok"], b + 2)
                nc.vector.tensor_tensor(lo[j][:, :, :], raw[j][:, :, :], hi[j][:, :, :].bitcast(F32), ALU.subtract).then_inc(sem["lo_ok"], 1)

            def out(b):
                for m in range(2):
                    dve.wait_ge(sem["sc"], 2 * b + m + 1)
                    nc.vector.tensor_copy(scores[:, :, bass.ds(2 * b + m, 1), :], p_s[m][:, :, :]).then_inc(sem["s_ok"], 1)

            for n, ks in enumerate(halves):
                dve.wait_ge(sem["hi_ok"], n + 1)
                nc.vector.tensor_tensor(lo[0][:, ks, :], raw[0][:, ks, :], hi[0][:, ks, :].bitcast(F32), ALU.subtract).then_inc(sem["lo_ok"], 1)
            split(1, 1)
            with dve.Fori(1, PH // 2) as i:
                for j in range(2):
                    split(2 * i + j, j)
                    out(2 * i + j - 2)
            out(PH - 2)
            out(PH - 1)

        @block.tensor
        def _(pe):
            def product(b, j, first=False):
                if isinstance(b, int) and b == 0:
                    pe.wait_ge(sem["lo_ok"], 1)
                else:
                    pe.wait_ge(sem["lo_ok"], b + 2)
                for m in range(2):
                    if not first:
                        pe.wait_ge(sem["q_ok"], 2 * b + m - 3)
                    ms = slice(m * P, (m + 1) * P)
                    for c in range(KD):
                        if first and j == 0 and (m, c) == (0, KD // 2):
                            pe.wait_ge(sem["lo_ok"], 2)
                        ins = three(nc, acc[2 * j + m][:, :], (hi[j][:, c, ms], lo[j][:, c, ms]),
                                    (keep["h_hi"][:, c, :], keep["h_lo"][:, c, :]), c == 0, c == KD - 1)
                    ins.then_inc(sem["mm"], 1)

            def score(b, first=False):
                for m in range(2):
                    pe.wait_ge(sem["q_ok"], 2 * b + m + 1)
                    if not first:
                        pe.wait_ge(sem["s_ok"], 2 * b + m - 1)
                    for i in range(TT):
                        ins = nc.tensor.matmul(p_s[m][:, i, :], q[m][:, i * P:(i + 1) * P], keys_t[:, m, :], start=True, stop=True)
                    ins.then_inc(sem["sc"], 1)

            product(0, 0, True)
            pe.wait_ge(sem["keys_in"], 16)
            for x in range(2):
                ins = nc.tensor.transpose(p_k[:, x, :], keys[:, x, :], keep["ident"][:, :])
            ins.then_inc(sem["kt"], 1)
            product(1, 1, True)
            pe.wait_ge(sem["kt_ok"], 1)
            score(0, True)
            with pe.Fori(1, PH // 2) as i:
                product(2 * i, 0)
                score(2 * i - 1)
                product(2 * i + 1, 1)
                score(2 * i)
            score(PH - 1)


PLAIN = 64
PICK = 56
SOFT_AT = 60
CH = 32
CHUNKS = S // CH
GTOK = 8
GT = 4
AT0_AT, V_AT = Y_AT + 24 * KB, X2_AT + 76 * KB
UNROLL = 8


def phase_experts(nc, a, keep, scores, acts, gates, raw, u_in, v, at0, v_in, w_in0):
    with ExitStack() as stack:
        k = Kit(nc, stack, "u", Y_AT)
        match = [k.sb(f"match{j}", [P, P, 2 * GTOK], BF16) for j in range(2)]
        hot = [k.sb(f"hot{j}", [P, P, 3, GTOK], BF16) for j in range(2)]
        assert k.at <= AT0_AT
        k.at = Y_AT + 48 * KB
        ut = [k.sb(f"ut{j}", [P, KD, P]) for j in range(2)]
        hi = [k.sb(f"hi{j}", [P, KD, P], F32R) for j in range(2)]
        lo = [k.sb(f"lo{j}", [P, KD, P], F32R) for j in range(2)]
        ao = [k.sb(f"ao{j}", [P, 2, S]) for j in range(2)]
        assert k.at <= X2_AT
        k.at = X2_AT + 16 * KB
        gs_at = k.at
        gs = [k.sb(f"gs{j}", [P, P, CH]) for j in range(2)]
        after = k.at
        k.at = gs_at
        sc, sc2, eq, cand = (k.sb(n, [P, 16 * P]) for n in ("sc", "sc2", "eq", "cand"))
        assert k.at <= after
        k.at = after
        top = k.sb("top", [P, 16, TOPK])
        topi = k.sb("topi", [P, 16, TOPK], U32)
        topf = k.sb("topf", [P, 16, TOPK])
        best = k.sb("best", [P, PH, TOPK])
        pos = k.sb("pos", [P, PH * TOPK], U32)
        ab = k.sb("ab", [P, 2, PH * TOPK], U32)
        abf = k.sb("abf", [P, 2, PH * TOPK])
        carrier = k.sb("carrier", [P, 1])
        sel = k.sb("sel", [P, 3, TT, P])
        z = k.sb("z", [P, TT * PH])
        keys = k.sb("keys", [P, S // GTOK, 2, GTOK], BF16)
        parts = k.sb("parts", [P, S // GTOK, 3, GTOK], BF16)
        rest = [k.sb(f"rest{j}", [P, S]) for j in range(2)]
        iota16 = k.sb("iota16", [P, TOPK])
        iota = k.sb("iota", [P, P, 2 * GTOK], BF16)
        assert k.at <= V_AT
        p_s = [k.ps(f"s{j}", [P, S]) for j in range(4)]
        p_g = [k.ps(f"g{j}", [P, 4, P]) for j in range(4)]
        names = ("iota_ok ut_ok hi_ok lo_ok mm act_ok a_out0 a_out1 step exp_ok sel_ok slot_t slot_ok hot_ok g_mm g_ok "
                 "g_out0 g_out1").split()
        sem = {n: k.sem(n) for n in names}
        dve_c = k.count("dve_chain")
        block = stack.enter_context(nc.Block())
        au = acts.rearrange("(b x) p t -> b p x t", x=2)
        TILES = NE // P
        TURNS = (TILES - PLAIN) // UNROLL
        STEPS = 1 + 5 * 2 * PH + 2 + 5 * PH + 2 + 2 + 2 * 3 + 17

        @block.sync
        def _(sp):
            def load(n, j):
                sp.wait_ge(sem["ut_ok"], 2 * n - 2)
                load_experts(sp, a, raw[j], u_in[j], n)

            def store(n, j):
                sp.wait_ge(sem["act_ok"], 2 * n + 2)
                sp.dma_start(au[n], ao[j][:, :, :]).then_inc(sem[f"a_out{j}"], 16)

            def gates_out(c, j):
                sp.wait_ge(sem["g_ok"], (c + 1) * (CH // 4))
                sp.dma_start(gates[c], gs[j][:, :, :]).then_inc(sem[f"g_out{j}"], 16)

            with sp.Fori(0, PLAIN // 4) as i:
                for j in range(2):
                    load(2 * i + j + 2, j)
                    store(2 * i + j, j)

            def turn(i, last=False):
                for x in range(UNROLL // 2):
                    n = PLAIN // 2 + i * (UNROLL // 2) + x
                    if not (last and x >= UNROLL // 2 - 2):
                        load(n + 2, x % 2)
                    if last and x == UNROLL // 2 - 2:
                        vv, av = expert_groups(a, acts)
                        sp.dma_start(v[:, :, :], vv[0]).then_inc(v_in, 16)
                        sp.dma_start(at0[:, :, :], av[0]).then_inc(w_in0, 16)
                    if x % 2:
                        gates_out(2 * i + x // 2, x // 2)
                    store(n, x % 2)

            with sp.Fori(0, TURNS - 1) as i:
                turn(i)
            turn(TURNS - 1, True)
            for j in range(2):
                sp.wait_ge(sem[f"a_out{j}"], 16 * TILES // 4)
                sp.wait_ge(sem[f"g_out{j}"], 16 * TURNS)

        @block.gpsimd
        def _(pool):
            nc.gpsimd.iota(iota16[:, :], pattern=[[1, TOPK]], base=0, channel_multiplier=0,
                           allow_small_or_imprecise_dtypes=True).then_inc(sem["iota_ok"], 1)
            nc.gpsimd.iota(iota[:, :, :], pattern=[[1, P], [0, 2 * GTOK]], base=0, channel_multiplier=0,
                           allow_small_or_imprecise_dtypes=True).then_inc(sem["iota_ok"], 1)

            def split_lo(t, j, wait=True):
                pool.wait_ge(sem["hi_ok"], t + 1)
                if wait:
                    pool.wait_ge(sem["mm"], t - 1)
                nc.gpsimd.tensor_tensor(lo[j][:, :, :], ut[j][:, :, :], hi[j][:, :, :].bitcast(F32), ALU.subtract).then_inc(sem["lo_ok"], 1)

            pool.wait_ge(sem["lo_ok"], 1)
            split_lo(1, 1, False)
            with pool.Fori(1, TILES // 2) as i:
                for j in range(2):
                    split_lo(2 * i + j, j)

        @block.scalar
        def _(act):
            def split_hi(t, j, wait=True):
                act.wait_ge(sem["ut_ok"], t + 1)
                if wait:
                    act.wait_ge(sem["mm"], t - 1)
                nc.scalar.activation(hi[j][:, :, :], ut[j][:, :, :], ACT.Copy).then_inc(sem["hi_ok"], 1)

            def gelu(t, j, first=False):
                act.wait_ge(sem["mm"], t + 1)
                if not first and j % 2 == 0:
                    act.wait_ge(sem[f"a_out{j // 2}"], (t - j) * 4)
                nc.scalar.activation(ao[j // 2][:, j % 2, :], p_s[j][:, :], ACT.Gelu).then_inc(sem["act_ok"], 1)

            def plain(i, first=False):
                for j in range(4):
                    t = 4 * i + j
                    split_hi(t + 1, (j + 1) % 2, not (first and j == 0))
                    gelu(t, j, first)

            split_hi(0, 0, False)
            plain(0, True)
            with act.Fori(1, SOFT_AT // 4) as i:
                plain(i)
            act.wait_ge(sem["step"], TT * STEPS)
            nc.scalar.activation(sel[:, 2, :, :], sel[:, 2, :, :], ACT.Exp).then_inc(sem["exp_ok"], 1)
            with act.Fori(SOFT_AT // 4, PLAIN // 4) as i:
                plain(i)

            def turn(i, first=False, last=False):
                for x in range(UNROLL):
                    t = PLAIN + i * UNROLL + x
                    if not (last and x == UNROLL - 1):
                        split_hi(t + 1, (x + 1) % 2)
                    chunk = x // 4
                    if x % 4 == 0 and not first:
                        act.wait_ge(sem[f"g_out{chunk}"], 16 * i)
                    for y in range(2):
                        n = 2 * x + y
                        act.wait_ge(sem["g_mm"], 2 * UNROLL * i + n + 1)
                        at = (n % 8) * 4
                        nc.scalar.activation(gs[chunk][:, :, at:at + 4].rearrange("p i t -> p t i"), p_g[n % 4][:, :, :], ACT.Copy).then_inc(sem["g_ok"], 1)
                    gelu(t, x % 4)

            turn(0, True)
            with act.Fori(1, TURNS - 1) as i:
                turn(i)
            turn(TURNS - 1, False, True)

        @block.vector
        def _(dve):
            slots = [P, PH, TOPK, TOPK]

            def transposes(t, j, wait=True):
                if j % 2 == 0:
                    dve.wait_ge(u_in[j // 2], (t - j) * 16 + 64)
                if wait:
                    dve.wait_ge(sem["lo_ok"], t - 1)
                half = raw[j // 2][:, 4 * (j % 2):4 * (j % 2) + 4, :]
                nc.vector.transpose(ut[j % 2][:, :, :].rearrange("p m (b e) -> p b m e", b=4),
                                    half.rearrange("p b (m r) -> p b m r", m=KD)).then_inc(sem["ut_ok"], 1)

            steps = Count(sem["step"])
            beside = [0]
            both = 2 * PICK // TT

            def step(pair, ins):
                steps.inc(ins)
                if steps.n * both // (2 * STEPS) > beside[0]:
                    j = beside[0] + 2
                    transposes(pair * both + j, j % 4)
                    beside[0] += 1

            def fence(pair):
                dve.wait_ge(steps.sem, pair * 2 * STEPS + steps.n)
                step(pair, nc.vector.memset(carrier[:, :], 0.0))

            def largest(pair, n, w, src, tmp, vals, index):
                for x in range(n):
                    step(pair, nc.vector.max(vals[:, x, 0:8], src[:, x * w:(x + 1) * w]))
                fence(pair)
                for x in range(n):
                    step(pair, nc.vector.max_index(index[:, x, 0:8], vals[:, x, 0:8], src[:, x * w:(x + 1) * w]))
                    step(pair, nc.vector.match_replace(tmp[:, x * w:(x + 1) * w], vals[:, x, 0:8], src[:, x * w:(x + 1) * w], -FLT_MAX))
                fence(pair)
                for x in range(n):
                    step(pair, nc.vector.max(vals[:, x, 8:16], tmp[:, x * w:(x + 1) * w]))
                fence(pair)
                for x in range(n):
                    step(pair, nc.vector.max_index(index[:, x, 8:16], vals[:, x, 8:16], tmp[:, x * w:(x + 1) * w]))
                fence(pair)

            transposes(0, 0, False)
            dve.wait_ge(sem["hi_ok"], 1)
            nc.vector.tensor_tensor(lo[0][:, :, :], ut[0][:, :, :], hi[0][:, :, :].bitcast(F32), ALU.subtract).then_inc(sem["lo_ok"], 1)
            transposes(1, 1, False)
            dve.wait_ge(sem["iota_ok"], 2)
            def retrieve(pair, half_tile):
                i = 2 * pair + half_tile
                step(pair, nc.vector.tensor_copy(sc[:, :].rearrange("p (o h n) -> p o h n", o=1, h=16), scores[:, bass.ds(i, 1), :, :]))
                fence(pair)
                largest(pair, 2 * PH, P, sc, sc2, top, topi)
                step(pair, nc.vector.tensor_copy(topf[:, :, :], topi[:, :, :]))
                half = top[:, :, :].rearrange("p (h s) k -> p s h k", s=2)
                first = half[:, 0].rearrange("p h (k o) -> p h k o", o=1).broadcast_to(slots)
                second = half[:, 1].rearrange("p h (o k) -> p h o k", o=1).broadcast_to(slots)
                step(pair, nc.vector.tensor_tensor(cand[:, :].rearrange("p (h a b) -> p h a b", h=PH, a=TOPK), first, second, ALU.add))
                fence(pair)
                largest(pair, PH, TOPK * TOPK, cand, sc2, best, pos[:, :].rearrange("p (h k) -> p h k", h=PH))
                step(pair, nc.vector.tensor_scalar(ab[:, 0, :], pos[:, :], 4, None, ALU.logical_shift_right))
                step(pair, nc.vector.tensor_scalar(ab[:, 1, :], pos[:, :], 15, None, ALU.bitwise_and))
                fence(pair)
                step(pair, nc.vector.tensor_copy(abf[:, :, :], ab[:, :, :]))
                step(pair, nc.vector.tensor_tensor(sel[:, 2, bass.ds(i, 1), :].rearrange("p o (h k) -> p (o h) k", h=PH), best[:, :, :],
                                                best[:, :, 0:1].broadcast_to([P, PH, TOPK]), ALU.subtract))
                fence(pair)
                for s, e_flat in enumerate((eq, sc)):
                    e = e_flat[:, :].rearrange("p (h k a) -> p h k a", h=PH, k=TOPK)
                    rank = abf[:, s, :].rearrange("p (h k o) -> p h k o", h=PH, o=1).broadcast_to(slots)
                    upto = iota16[:, :].rearrange("p (x y a) -> p x y a", x=1, y=1).broadcast_to(slots)
                    key = topf[:, :, :].rearrange("p (h s) k -> p s h k", s=2)[:, s].rearrange("p h (o a) -> p h o a", o=1).broadcast_to(slots)
                    step(pair, nc.vector.tensor_tensor(e, rank, upto, ALU.is_equal))
                    fence(pair)
                    step(pair, nc.vector.tensor_tensor(e, e, key, ALU.mult))
                    fence(pair)
                    step(pair, nc.vector.reduce_sum(sel[:, s, bass.ds(i, 1), :].rearrange("p o (n q) -> p (o n) q", q=1),
                                                 e_flat[:, :].rearrange("p (n a) -> p n a", a=TOPK), AX.X))
                fence(pair)

            with dve.Fori(0, TT // 2) as pair:
                retrieve(pair, 0)
                retrieve(pair, 1)
                assert steps.n == 2 * STEPS and beside[0] == both

            for t in range(PICK + 2, SOFT_AT + 2):
                transposes(t, t % 4)
            dve.wait_ge(sem["exp_ok"], 1)
            ev = sel[:, 2, :, :].rearrange("p i (h k) -> p (i h) k", k=TOPK)
            chained(dve, dve_c, nc.vector.reduce_sum(z[:, :], ev, AX.X))
            chained(dve, dve_c, nc.vector.reciprocal(z[:, :], z[:, :]))
            nc.vector.tensor_tensor(ev, ev, z[:, :].rearrange("p (x o) -> p x o", o=1).broadcast_to([P, TT * PH, TOPK]),
                                    ALU.mult).then_inc(sem["sel_ok"], 1)
            for t in range(SOFT_AT + 2, PLAIN):
                transposes(t, t % 4)
            dve.wait_ge(sem["slot_t"], 3)
            by_slot = [p_g[s][:, :, :].rearrange("p i (g t) -> p (i g) t", t=GTOK) for s in range(3)]
            rests = [r[:, :].rearrange("p (g t) -> p g t", t=GTOK) for r in rest]
            for s in range(2):
                nc.vector.tensor_copy(keys[:, :, s, :], by_slot[s]).then_inc(sem["slot_ok"], 1)
            chained(dve, dve_c, nc.vector.tensor_copy(parts[:, :, 0, :], by_slot[2]))
            chained(dve, dve_c, nc.vector.tensor_tensor(rests[0], by_slot[2], parts[:, :, 0, :], ALU.subtract))
            chained(dve, dve_c, nc.vector.tensor_copy(parts[:, :, 1, :], rests[0]))
            chained(dve, dve_c, nc.vector.tensor_tensor(rests[1], rests[0], parts[:, :, 1, :], ALU.subtract))
            nc.vector.tensor_copy(parts[:, :, 2, :], rests[1]).then_inc(sem["slot_ok"], 1)
            for t in range(PLAIN, PLAIN + 2):
                transposes(t, t % 4)
            dve.wait_ge(sem["slot_ok"], 3)

            def turn(i, first=False, last=False):
                for x in range(UNROLL):
                    t = PLAIN + i * UNROLL + x
                    g = i * UNROLL + x
                    if not (first and x < 2):
                        dve.wait_ge(sem["g_mm"], 2 * g - 2)
                    m, h = match[x % 2], hot[x % 2]
                    key = keys[:, bass.ds(g, 1), :, :].rearrange("p o s t -> p o (s t)").broadcast_to([P, P, 2 * GTOK])
                    nc.vector.tensor_tensor(m[:, :, :], iota[:, :, :], key, ALU.is_equal).then_inc(sem["hot_ok"], 1)
                    dve.wait_ge(sem["hot_ok"], 2 * g + 1)
                    ones = m[:, :, 0:GTOK].rearrange("p i (o t) -> p i o t", o=1).broadcast_to([P, P, 3, GTOK])
                    w = parts[:, bass.ds(g, 1), :, :].broadcast_to([P, P, 3, GTOK])
                    nc.vector.tensor_tensor(h[:, :, :, :], ones, w, ALU.mult).then_inc(sem["hot_ok"], 1)
                    if not (last and x >= UNROLL - 2):
                        transposes(t + 2, (x + 2) % 4)

            turn(0, True)
            with dve.Fori(1, TURNS - 1) as i:
                turn(i)
            turn(TURNS - 1, False, True)

        @block.tensor
        def _(pe):
            ident = keep["ident"][:, :]

            def product(t, j, wait=True):
                pe.wait_ge(sem["lo_ok"], t + 1)
                if wait:
                    pe.wait_ge(sem["act_ok"], t - 3)
                for c in range(KD):
                    ins = three(nc, p_s[j][:, :], (hi[j % 2][:, c, :], lo[j % 2][:, c, :]),
                                (keep["h_hi"][:, c, :], keep["h_lo"][:, c, :]), c == 0, c == KD - 1)
                ins.then_inc(sem["mm"], 1)

            def plain(i, first=False):
                for j in range(4):
                    product(4 * i + j, j, not first)

            plain(0, True)
            with pe.Fori(1, PLAIN // 4 - 1) as i:
                plain(i)
            product(PLAIN - 4, 0)
            product(PLAIN - 3, 1)
            pe.wait_ge(sem["sel_ok"], 1)
            for s in range(3):
                for i in range(TT):
                    ins = nc.tensor.transpose(p_g[s][:, i, :], sel[:, s, i, :], ident)
                ins.then_inc(sem["slot_t"], 1)
            product(PLAIN - 2, 2)
            product(PLAIN - 1, 3)

            def turn(i, first=False):
                for x in range(UNROLL):
                    g = i * UNROLL + x
                    pe.wait_ge(sem["hot_ok"], 2 * g + 2)
                    m, h = match[x % 2], hot[x % 2]
                    for y in range(2):
                        n = 2 * x + y
                        if not (first and n < 4):
                            pe.wait_ge(sem["g_ok"], 2 * UNROLL * i + n - 3)
                        for b in range(4):
                            t = 4 * y + b
                            for part in range(3):
                                ins = nc.tensor.matmul(p_g[n % 4][:, b, :], m[:, :, GTOK + t], h[:, :, part, t], start=part == 0, stop=part == 2)
                        ins.then_inc(sem["g_mm"], 1)
                    product(PLAIN + i * UNROLL + x, x % 4)

            turn(0, True)
            with pe.Fori(1, TURNS) as i:
                turn(i)




def phase_combine(nc, a, keep, acts, gates, gate2_row, x2, out, v, at0, v_in, w_in0):
    with ExitStack() as stack:
        k = Kit(nc, stack, "v", LOW)
        v_hi = [k.sb(f"v_hi{j}", [P, GT, D], F32R) for j in range(2)]
        v_lo = [k.sb("v_lo0", [P, GT, D], F32R)]
        at = [at0, k.sb("at1", [P, GT, S])]
        assert k.at <= AT0_AT
        k.at = AT0_AT + 8 * KB
        v_lo.append(k.sb("v_lo1", [P, GT, D], F32R))
        gt = [k.sb(f"gt{j}", [P, CHUNKS, GT * CH]) for j in range(2)]
        acc = k.sb("acc", [P, TT, D])
        assert k.at <= X2_AT
        k.at = X2_AT + 16 * KB
        w_hi = [k.sb(f"w_hi{j}", [P, GT, S], F32R) for j in range(2)]
        w_lo = [k.sb(f"w_lo{j}", [P, GT, S], F32R) for j in range(2)]
        gate2 = k.sb("gate2", [P, D])
        g_fin = k.sb("g_fin", [P, D])
        ssq, fin, root = (k.sb(n, [P, TT]) for n in ("ssq", "fin", "root"))
        sq = k.sb("sq", [P, D])
        assert k.at <= V_AT
        p_o = [k.ps(f"o{j}", [P, S]) for j in range(8)]
        names = ("w_in1 w0_ok hi0_ok gf_in vhi_ok vlo_ok w_ok whi_ok wlo_ok mm add_ok "
                 "ssq_ok root_ok y_ok out_ok").split()
        sem = {n: k.sem(n) for n in names}
        dve_c = k.count("dve_chain")
        sem |= {"v_in": v_in, "w_in0": w_in0}
        block = stack.enter_context(nc.Block())
        vv, av = expert_groups(a, acts)
        gv = gates.rearrange("c j (g x) t -> g j c (x t)", x=GT)
        NG = NE // P // GT

        @block.sync
        def _(sp):
            def load(g, j):
                sp.wait_ge(sem["vlo_ok"], g)
                sp.dma_start(v[:, :, :], vv[g]).then_inc(sem["v_in"], 16)
                sp.wait_ge(sem["wlo_ok"], g - 1)
                sp.dma_start(at[j][:, :, :], av[g]).then_inc(sem[f"w_in{j}"], 16)
                sp.dma_start(gt[j][:, :, :], gv[g]).then_inc(sem[f"w_in{j}"], 16)

            sp.dma_start(gt[0][:, :, :], gv[0]).then_inc(sem["w_in0"], 16)
            sp.wait_ge(sem["vlo_ok"], 1)
            sp.dma_start(v[:, :, :], vv[1]).then_inc(sem["v_in"], 16)
            sp.dma_start(at[1][:, :, :], av[1]).then_inc(sem["w_in1"], 16)
            sp.dma_start(gt[1][:, :, :], gv[1]).then_inc(sem["w_in1"], 16)
            sp.dma_start(g_fin[:, :], a["g_final"].rearrange("(o d) -> o d", o=1).to_broadcast([P, D])).then_inc(sem["gf_in"], 16)
            sp.dma_start(gate2[:, :], gate2_row.to_broadcast([P, D])).then_inc(sem["gf_in"], 16)
            with sp.Fori(1, NG // 2) as i:
                for j in range(2):
                    load(2 * i + j, j)
            ov = out[0].rearrange("(i p) d -> p i d", p=P)
            for i in range(TT):
                sp.wait_ge(sem["y_ok"], i + 1)
                sp.dma_start(ov[:, i, :], acc[:, i, :]).then_inc(sem["out_ok"], 16)
            sp.wait_ge(sem["out_ok"], 16 * TT)

        def weigh(eng, ops, i, j):
            eng.wait_ge(sem[f"w_in{j}"], 32 * i + 32)
            x = at[j][:, :, :].rearrange("p x (c t) -> p x c t", t=CH)
            ops.tensor_tensor(x, x, gt[j][:, :, :].rearrange("p c (x t) -> p x c t", t=CH), ALU.mult).then_inc(sem["w_ok"], 1)

        @block.gpsimd
        def _(pool):
            weigh(pool, nc.gpsimd, 0, 1)
            with pool.Fori(1, NG // 2) as i:
                for j in range(2):
                    weigh(pool, nc.gpsimd, i, j)

        @block.scalar
        def _(act):
            act.wait_ge(sem["v_in"], 16)
            for x in range(GT):
                nc.scalar.activation(v_hi[0][:, x, :], v[:, x, :], ACT.Copy).then_inc(sem["hi0_ok"] if x < GT - 1 else sem["vhi_ok"], 1)

            def split(g, j, first=False):
                act.wait_ge(sem["v_in"], 16 * g + 16)
                if not first:
                    act.wait_ge(sem["mm"], 8 * g - 8)
                nc.scalar.activation(v_hi[j][:, :, :], v[:, :, :], ACT.Copy).then_inc(sem["vhi_ok"], 1)
                act.wait_ge(sem["w_ok"], g)
                nc.scalar.activation(w_hi[j][:, :, :], at[j][:, :, :], ACT.Copy).then_inc(sem["whi_ok"], 1)

            for x in range(GT):
                act.wait_ge(sem["w0_ok"], x + 1)
                nc.scalar.activation(w_hi[0][:, x, :], at[0][:, x, :], ACT.Copy).then_inc(sem["hi0_ok"] if x < GT - 1 else sem["whi_ok"], 1)
            split(1, 1, True)
            with act.Fori(1, NG // 2) as i:
                for j in range(2):
                    split(2 * i + j, j)
            for i in range(TT):
                act.wait_ge(sem["ssq_ok"], 2 * i + 2)
                r = root[:, i:i + 1]
                nc.scalar.activation(r, r, ACT.Sqrt, bias=keep["eps"][:, :], scale=DOWN / D).then_inc(sem["root_ok"], 1)

        @block.vector
        def _(dve):
            def split(g, j):
                dve.wait_ge(sem["vhi_ok"], g + 1)
                nc.vector.tensor_tensor(v_lo[j][:, :, :], v[:, :, :], v_hi[j][:, :, :].bitcast(F32), ALU.subtract).then_inc(sem["vlo_ok"], 1)
                dve.wait_ge(sem["whi_ok"], g + 1)
                nc.vector.tensor_tensor(w_lo[j][:, :, :], at[j][:, :, :], w_hi[j][:, :, :].bitcast(F32), ALU.subtract).then_inc(sem["wlo_ok"], 1)

            def add(g, banks, first=False):
                for n in banks:
                    dve.wait_ge(sem["mm"], 8 * g + n + 1)
                    o = acc[:, n // 2, n % 2 * S:(n % 2 + 1) * S]
                    if first:
                        nc.vector.tensor_copy(o, p_o[n][:, :]).then_inc(sem["add_ok"], 1)
                    else:
                        dve.wait_ge(sem["add_ok"], 8 * g + n - 7)
                        nc.vector.tensor_tensor(o, o, p_o[n][:, :], ALU.add).then_inc(sem["add_ok"], 1)

            for x in range(GT):
                if x < GT - 1:
                    dve.wait_ge(sem["hi0_ok"], x + 1)
                else:
                    dve.wait_ge(sem["vhi_ok"], 1)
                ins = nc.vector.tensor_tensor(v_lo[0][:, x, :], v[:, x, :], v_hi[0][:, x, :].bitcast(F32), ALU.subtract)
            ins.then_inc(sem["vlo_ok"], 1)
            dve.wait_ge(sem["w_in0"], 32)
            for x in range(GT + 1):
                if x < GT:
                    o = at[0][:, x, :].rearrange("p (c t) -> p c t", t=CH)
                    nc.vector.tensor_tensor(o, o, gt[0][:, :, x * CH:(x + 1) * CH], ALU.mult).then_inc(sem["w0_ok"], 1)
                if x:
                    if x < GT:
                        dve.wait_ge(sem["hi0_ok"], GT - 1 + x)
                    else:
                        dve.wait_ge(sem["whi_ok"], 1)
                    ins = nc.vector.tensor_tensor(w_lo[0][:, x - 1, :], at[0][:, x - 1, :], w_hi[0][:, x - 1, :].bitcast(F32), ALU.subtract)
            ins.then_inc(sem["wlo_ok"], 1)
            split(1, 1)
            add(0, range(8), True)
            split(2, 0)
            add(1, range(8))
            with dve.Fori(1, NG // 2 - 1) as i:
                split(2 * i + 1, 1)
                add(2 * i, range(8))
                split(2 * i + 2, 0)
                add(2 * i + 1, range(8))
            split(NG - 1, 1)
            add(NG - 2, range(8))
            dve.wait_ge(sem["wlo_ok"], NG)
            dve.wait_ge(sem["gf_in"], 32)

            def finish(i):
                dve.wait_ge(sem["root_ok"], i + 1)
                rstd_dve_out(nc, dve, dve_c, root[:, i:i + 1], fin[:, i:i + 1])
                nc.vector.scalar_tensor_tensor(acc[:, i, :], acc[:, i, :], root[:, i:i + 1], g_fin[:, :], ALU.mult, ALU.mult).then_inc(sem["y_ok"], 1)

            for i in range(TT):
                add(NG - 1, (2 * i, 2 * i + 1))
                dve.wait_ge(sem["add_ok"], 8 * (NG - 1) + 2 * i + 2)
                chained(dve, dve_c, nc.vector.tensor_tensor(acc[:, i, :], acc[:, i, :], gate2[:, :], ALU.mult))
                chained(dve, dve_c, nc.vector.tensor_tensor(acc[:, i, :], acc[:, i, :], x2[:, i, :], ALU.add))
                chained(dve, dve_c, nc.vector.tensor_tensor_reduce(
                    out=sq[:, :], in0=acc[:, i, :], in1=acc[:, i, :], scale=1.0, scalar=0.0,
                    op0=ALU.mult, op1=ALU.add, accum_out=ssq[:, i:i + 1]))
                rstd_dve_in(nc, sem["ssq_ok"], ssq[:, i:i + 1], fin[:, i:i + 1], root[:, i:i + 1])
                if i:
                    finish(i - 1)
            finish(TT - 1)

        @block.tensor
        def _(pe):
            def group(g, j, first=False):
                pe.wait_ge(sem["vlo_ok"], g + 1)
                pe.wait_ge(sem["wlo_ok"], g + 1)
                for n in range(8):
                    if not first:
                        pe.wait_ge(sem["add_ok"], 8 * g + n - 7)
                    ts, cs = slice(n // 2 * P, (n // 2 + 1) * P), slice(n % 2 * S, (n % 2 + 1) * S)
                    for x in range(GT):
                        ins = three(nc, p_o[n][:, :], (w_hi[j][:, x, ts], w_lo[j][:, x, ts]), (v_hi[j][:, x, cs], v_lo[j][:, x, cs]), x == 0, x == GT - 1)
                    ins.then_inc(sem["mm"], 1)

            group(0, 0, True)
            group(1, 1)
            with pe.Fori(1, NG // 2) as i:
                for j in range(2):
                    group(2 * i + j, j)


def program(nc, a, out, stop=99):
    with ExitStack() as top:
        k = Kit(nc, top, "keep", KEEP_AT)
        keep = {n: k.sb(n, shape) for n, shape in (
            ("ident", [P, P]), ("ones", [P, P]), ("inv_count", [P, 16]), ("eps", [P, 1]), ("cols", [P, V_ROWS]), ("mod", [P, 48]),
            ("scale1", [P, KD]), ("scale2", [P, KD]), ("csil", [P, KD]), ("neglam", [P, 1]), ("sinks", [P, 8]))}
        assert k.at <= LOW
        kh = Kit(nc, top, "h", H_AT)
        keep["h_hi"], keep["h_lo"] = (kh.sb(n, [P, KD, S], F32R) for n in ("hi", "lo"))
        kw = Kit(nc, top, "w_in", XT_AT + 68 * KB)
        w_raw, w_in = [kw.sb(f"raw{j}", [P, KD, BW]) for j in range(4)], [kw.sem(f"in{j}") for j in range(4)]
        w_hi_ok, w_lo_ok = kw.sem("hi_ok"), kw.sem("lo_ok")
        ky = Kit(nc, top, "y", Y_AT)
        y_hi, y_lo = (ky.sb(n, [P, NBR * CB, S], F32R) for n in ("hi", "lo"))
        phase_condition(nc, a, keep, w_raw, w_in, y_hi, w_hi_ok, w_lo_ok)
        if stop <= 1:
            return
        xt = Kit(nc, top, "mixin", XT_AT).sb("xt", [P, 2 * MIX_BLOCKS, S])
        phase_project(nc, a, keep, xt, y_hi, w_raw, w_in, w_hi_ok, w_lo_ok)
        if stop <= 2:
            return
        tanhs = nc.dram_tensor("gate_tanhs", [NBR * KD, P, S], F32, kind="Internal").ap()
        phase_mix(nc, a, keep, xt, *(y[:, :, :].rearrange("p (g c) t -> p g c t", c=CB) for y in (y_hi, y_lo)), tanhs)
        if stop <= 3:
            return
        x2 = Kit(nc, top, "x2", X2_AT).sb("x2", [P, TT, D])
        m_hi = Kit(nc, top, "merged", XT_AT).sb("hi", [P, KD, S], F32R)
        m_lo = Kit(nc, top, "merged", MERGED_AT + 16 * KB).sb("lo", [P, KD, S], F32R)
        w_o = Kit(nc, top, "w_o", H_AT).sb("raw", [P, KD, D])
        kg = Kit(nc, top, "gate1", MERGED_AT + 32 * KB)
        gate1 = kg.sb("row", [P, D])
        gate2_row = nc.dram_tensor("gate2_row", [1, D], F32, kind="Internal").ap()
        wo_in, x_in = kg.sem("wo_in"), kg.sem("x_in")
        phase_gate(nc, a, keep, xt, y_hi, y_lo, tanhs, m_hi, m_lo, gate1, gate2_row, w_o, wo_in, x2, x_in)
        if stop <= 4:
            return
        kq = Kit(nc, top, "w_q", X2_AT + 76 * KB)
        q_raw, q_in = [kq.sb(f"raw{j}", [P, KD, BW]) for j in range(2)], [kq.sem(f"in{j}") for j in range(2)]

        def first_queries(sp):
            for j in range(2):
                load_queries(sp, a, q_raw[j], q_in[j], j)

        phase_out(nc, keep, m_hi, m_lo, gate1, w_o, wo_in, x2, x_in, first_queries)
        if stop <= 5:
            return
        scores = Kit(nc, top, "peer", Y_AT).sb("scores", [P, TT, 2 * PH, NK])
        ku = Kit(nc, top, "u", Y_AT + 32 * KB)
        u_raw, u_in = [ku.sb(f"raw{j}", [P, 8, BW]) for j in range(2)], [ku.sem(f"in{j}") for j in range(2)]

        def first_experts(sp):
            for j in range(2):
                load_experts(sp, a, u_raw[j], u_in[j], j)

        phase_query(nc, a, keep, scores, q_raw, q_in, first_experts)
        if stop <= 6:
            return
        acts = nc.dram_tensor("expert_acts", [NE // P, P, S], F32, kind="Internal").ap()
        gates = nc.dram_tensor("expert_gates", [CHUNKS, P, P, CH], F32, kind="Internal").ap()
        v0 = Kit(nc, top, "v", V_AT)
        v_ahead = (v0.sb("raw", [P, GT, D]), Kit(nc, top, "at0", AT0_AT).sb("raw", [P, GT, S]), v0.sem("in"), v0.sem("w_in0"))
        phase_experts(nc, a, keep, scores, acts, gates, u_raw, u_in, *v_ahead)
        if stop <= 7:
            return
        phase_combine(nc, a, keep, acts, gates, gate2_row, x2, out, *v_ahead)


_INS = ["x", "c", "w_ada", "b_ada", "g_norm1", "w_in", "lam_q1", "lam_k1", "lam_q2", "lam_k2", "g_subln", "conv_w", "w_pool",
        "pool_scale", "sinks", "w_branch", "w_o", "g_norm2", "w_q", "sub_keys", "u_experts", "v_experts", "g_final"]


def kernel(**inputs):
    import numpy as _np
    import concourse.bacc as _bacc
    from concourse import mybir as _mybir
    from concourse.bass_utils import run_bass_kernel_spmd as _run

    nc = _bacc.Bacc("TRN2", target_bir_lowering=False, num_devices=1)
    arrays, args = {}, {}
    for name in _INS:
        arr = _np.ascontiguousarray(inputs[name])
        arrays[f"in_{name}_dram"] = arr
        args[name] = nc.dram_tensor(f"in_{name}_dram", arr.shape, _mybir.dt.from_np(arr.dtype), kind="ExternalInput").ap()
    out = nc.dram_tensor("out_0_dram", (1, S, D), F32, kind="ExternalOutput").ap()
    program(nc, args, out)
    r = _run(nc, [arrays], core_ids=[0])
    return r.results[0]["out_0_dram"]
```
